# Optimizing a Trainium2 kernel written in Bass

```python
import math
import jax, jax.numpy as jnp
from jax import lax
import numpy as np

D_MODEL = 1024
BATCH = 1
SEQ = 512
DEPTH = 2
DEC_BATCH = 8
DEC_SEQ = 8
PAST_LEN = 4096
PAGE_SIZE = 128

EXPAND = 2
D_MIX = EXPAND * D_MODEL
D_SSD = D_MIX // 2
D_RET = D_MIX // 4
D_POOL = D_MIX // 4
SSD_HEAD_DIM = 64
SSD_HEADS = D_SSD // SSD_HEAD_DIM
SSD_GROUPS = 2
SSD_HPG = SSD_HEADS // SSD_GROUPS
SSD_STATE = 128
CONV_WIDTH = 4
CONV_DIM = D_SSD + 2 * SSD_GROUPS * SSD_STATE
SSD_CHUNK = 128
RET_HEADS = 8
RET_HEAD_DIM = D_RET // RET_HEADS
RET_CHUNK = 128
ROPE_BASE = 10000.0
POOL_WINDOWS = (2, 4, 8, 16)
POOL_GROUPS = len(POOL_WINDOWS)
POOL_GROUP_DIM = D_POOL // POOL_GROUPS
POOL_BUF = max(POOL_WINDOWS) - 1
EPS = 1e-6
IN_SIZES = (D_SSD, CONV_DIM, SSD_HEADS, D_RET, D_RET, D_RET, D_RET, D_POOL, D_POOL)
D_IN_PROJ = sum(IN_SIZES)

kernel_name = "hymba_style_ssd_retention_pool_decoder_step"

def rmsnorm(x, w):
    xf = x.astype(jnp.float32)
    y = xf * lax.rsqrt(jnp.mean(xf * xf, axis=-1, keepdims=True) + EPS)
    return (y * w.astype(jnp.float32)).astype(x.dtype)

def split_cols(a, sizes):
    idx = np.cumsum(np.array(sizes))[:-1].tolist()
    return jnp.split(a, idx, axis=-1)

def to_chunks(a, c):
    b, l = a.shape[:2]
    return jnp.moveaxis(a.reshape(b, l // c, c, *a.shape[2:]), 1, 0)

def from_chunks(a):
    a = jnp.moveaxis(a, 0, 1)
    return a.reshape(a.shape[0], -1, *a.shape[3:])

def causal_conv(xbc, buf, w, b):
    ext = jnp.concatenate([buf.astype(xbc.dtype), xbc], axis=1)
    l = xbc.shape[1]
    y = ext[:, 0:l] * w[0]
    for t in range(1, CONV_WIDTH):
        y = y + ext[:, t:t + l] * w[t]
    return jax.nn.silu(y + b), ext[:, -(CONV_WIDTH - 1):]

def ssd_chunked(x, dt, a, bm, cm, h0):
    l = x.shape[1]
    c = math.gcd(l, SSD_CHUNK)
    causal = jnp.tril(jnp.ones((c, c), dtype=bool))[None, :, :, None, None]

    def step(h, inp):
        xc, dtc, bc, cc = inp
        cum = jnp.cumsum(dtc * a, axis=1)
        seg = cum[:, :, None] - cum[:, None, :]
        decay = jnp.exp(jnp.where(causal, seg, -jnp.inf))
        xdt = xc * dtc[..., None]
        scores = jnp.einsum('btgn,bsgn->btsg', cc, bc)
        y = jnp.einsum('btsg,btsgh,bsghp->btghp', scores, decay, xdt)
        y = y + jnp.einsum('btgn,bghpn->btghp', cc, h) * jnp.exp(cum)[..., None]
        last = cum[:, -1]
        w_end = jnp.exp(last[:, None] - cum)
        h_new = h * jnp.exp(last)[..., None, None] + jnp.einsum('bsgn,bsgh,bsghp->bghpn', bc, w_end, xdt)
        return h_new, y

    h_t, ys = lax.scan(step, h0, (to_chunks(x, c), to_chunks(dt, c), to_chunks(bm, c), to_chunks(cm, c)))
    return from_chunks(ys), h_t

def rotary(x, pos):
    half = x.shape[-1] // 2
    inv = ROPE_BASE ** (-jnp.arange(half, dtype=jnp.float32) / half)
    ang = pos.astype(jnp.float32)[:, None] * inv[None, :]
    cos = jnp.cos(ang)[None, :, None, :]
    sin = jnp.sin(ang)[None, :, None, :]
    x1, x2 = x[..., :half], x[..., half:]
    return jnp.concatenate([x1 * cos - x2 * sin, x1 * sin + x2 * cos], axis=-1)

def retention_chunked(q, k, v, s0):
    l = q.shape[1]
    c = math.gcd(l, RET_CHUNK)
    lg = jnp.log1p(-jnp.exp2(-5.0 - jnp.arange(RET_HEADS, dtype=jnp.float32)))
    idx = jnp.arange(c, dtype=jnp.float32)
    rel = idx[:, None] - idx[None, :]
    dmask = jnp.where(rel[None] >= 0, jnp.exp(jnp.maximum(rel, 0.0)[None] * lg[:, None, None]), 0.0)
    inner_decay = jnp.exp((idx + 1.0)[:, None] * lg[None, :])
    end_decay = jnp.exp((c - 1.0 - idx)[:, None] * lg[None, :])
    chunk_decay = jnp.exp(c * lg)

    def step(s, inp):
        qc, kc, vc = inp
        scores = jnp.einsum('bthd,bshd->bhts', qc, kc) * dmask[None]
        y = jnp.einsum('bhts,bshe->bthe', scores, vc)
        y = y + jnp.einsum('bthd,bhde->bthe', qc, s) * inner_decay[None, :, :, None]
        s_new = s * chunk_decay[None, :, None, None] + jnp.einsum('bshd,sh,bshe->bhde', kc, end_decay, vc)
        return s_new, y

    s_t, ys = lax.scan(step, s0, (to_chunks(q, c), to_chunks(k, c), to_chunks(v, c)))
    return from_chunks(ys), s_t

def multiscale_pool(u, buf, start_pos, pool_w, pool_scale):
    bsz, l, _ = u.shape
    ext = jnp.concatenate([buf.astype(jnp.float32), u.astype(jnp.float32)], axis=1)
    cs = jnp.concatenate([jnp.zeros((bsz, 1, D_POOL), jnp.float32), jnp.cumsum(ext, axis=1)], axis=1)
    pos = start_pos + jnp.arange(l)
    outs = []
    for g, w in enumerate(POOL_WINDOWS):
        sl = slice(g * POOL_GROUP_DIM, (g + 1) * POOL_GROUP_DIM)
        win = cs[:, POOL_BUF + 1:POOL_BUF + 1 + l, sl] - cs[:, POOL_BUF + 1 - w:POOL_BUF + 1 - w + l, sl]
        cnt = jnp.minimum(pos + 1, w).astype(jnp.float32)[None, :, None]
        outs.append(win / cnt - ext[:, POOL_BUF:, sl])
    pooled = jnp.concatenate(outs, axis=-1).reshape(bsz, l, POOL_GROUPS, POOL_GROUP_DIM)
    mixed = jnp.einsum('blgc,gcd->blgd', pooled, pool_w.astype(jnp.float32)).reshape(bsz, l, D_POOL)
    return mixed * pool_scale.astype(jnp.float32), ext[:, -POOL_BUF:]

def mixer_layer(x, ssm_h, conv_buf, ret_s, pool_buf, start_pos, norm_w, w_in, conv_w, conv_b,
                dt_bias, a_log, d_skip, ssd_norm_w, ret_norm_w, pool_w, pool_scale, w_out):
    f32 = jnp.float32
    bsz, l, _ = x.shape
    h = rmsnorm(x, norm_w)
    proj = jnp.einsum('bld,de->ble', h, w_in)
    z, xbc, dt_raw, q, k, v, g_ret, u, g_pool = split_cols(proj, IN_SIZES)

    xbc, conv_new = causal_conv(xbc, conv_buf, conv_w, conv_b)
    xbc = xbc.astype(f32)
    xs = xbc[..., :D_SSD].reshape(bsz, l, SSD_GROUPS, SSD_HPG, SSD_HEAD_DIM)
    bm = xbc[..., D_SSD:D_SSD + SSD_GROUPS * SSD_STATE].reshape(bsz, l, SSD_GROUPS, SSD_STATE)
    cm = xbc[..., D_SSD + SSD_GROUPS * SSD_STATE:].reshape(bsz, l, SSD_GROUPS, SSD_STATE)
    dt = jax.nn.softplus(dt_raw.astype(f32) + dt_bias.astype(f32)).reshape(bsz, l, SSD_GROUPS, SSD_HPG)
    a = -jnp.exp(a_log.astype(f32)).reshape(SSD_GROUPS, SSD_HPG)
    h0 = ssm_h.astype(f32).reshape(bsz, SSD_GROUPS, SSD_HPG, SSD_HEAD_DIM, SSD_STATE)
    y, h_new = ssd_chunked(xs, dt, a, bm, cm, h0)
    y = y + xs * d_skip.astype(f32).reshape(SSD_GROUPS, SSD_HPG, 1)
    gw = SSD_HPG * SSD_HEAD_DIM
    y = y.reshape(bsz, l, SSD_GROUPS, gw) * jax.nn.silu(z.astype(f32)).reshape(bsz, l, SSD_GROUPS, gw)
    y_ssd = rmsnorm(y, ssd_norm_w.reshape(SSD_GROUPS, gw)).reshape(bsz, l, D_SSD)

    pos = start_pos + jnp.arange(l)
    qr = rotary(q.astype(f32).reshape(bsz, l, RET_HEADS, RET_HEAD_DIM), pos)
    kr = rotary(k.astype(f32).reshape(bsz, l, RET_HEADS, RET_HEAD_DIM), pos) * (RET_HEAD_DIM ** -0.5)
    vr = v.astype(f32).reshape(bsz, l, RET_HEADS, RET_HEAD_DIM)
    o, s_new = retention_chunked(qr, kr, vr, ret_s.astype(f32))
    y_ret = rmsnorm(o, ret_norm_w.reshape(RET_HEADS, RET_HEAD_DIM)).reshape(bsz, l, D_RET) * jax.nn.silu(g_ret.astype(f32))

    pm, pool_new = multiscale_pool(u, pool_buf, start_pos, pool_w, pool_scale)
    y_pool = pm * jax.nn.silu(g_pool.astype(f32))

    mix = jnp.concatenate([y_ssd.astype(f32), y_ret.astype(f32), y_pool], axis=-1).astype(x.dtype)
    x = x + jnp.einsum('ble,ed->bld', mix, w_out)
    return (x,
            h_new.reshape(bsz, SSD_HEADS, SSD_HEAD_DIM, SSD_STATE).astype(x.dtype),
            conv_new.astype(x.dtype),
            s_new.astype(x.dtype),
            pool_new.astype(x.dtype))

def setup_inputs(seed: int = 0) -> dict:
    key = jax.random.key(seed)
    ks = jax.random.split(key, 20)
    f32 = jnp.float32
    nrm = lambda k, s: jax.random.normal(k, s, f32)
    x_prompt = nrm(ks[0], (BATCH, SEQ, D_MODEL))
    x_sample = nrm(ks[1], (DEC_BATCH, DEC_SEQ, D_MODEL))
    state_ssm = 0.1 * nrm(ks[2], (DEPTH, DEC_BATCH, SSD_HEADS, SSD_HEAD_DIM, SSD_STATE))
    state_conv = nrm(ks[3], (DEPTH, DEC_BATCH, CONV_WIDTH - 1, CONV_DIM))
    state_ret = 0.1 * nrm(ks[4], (DEPTH, DEC_BATCH, RET_HEADS, RET_HEAD_DIM, RET_HEAD_DIM))
    state_pool = nrm(ks[5], (DEPTH, DEC_BATCH, POOL_BUF, D_POOL))
    norm_w = 1.0 + 0.02 * nrm(ks[6], (DEPTH, D_MODEL))
    w_in = nrm(ks[7], (DEPTH, D_MODEL, D_IN_PROJ)) * D_MODEL ** -0.5
    conv_w = nrm(ks[8], (DEPTH, CONV_WIDTH, CONV_DIM)) * CONV_WIDTH ** -0.5
    conv_b = 0.02 * nrm(ks[9], (DEPTH, CONV_DIM))
    dt0 = jnp.exp(jax.random.uniform(ks[10], (DEPTH, SSD_HEADS), f32, math.log(1e-3), math.log(1e-1)))
    dt_bias = dt0 + jnp.log(-jnp.expm1(-dt0))
    a_log = jnp.log(jax.random.uniform(ks[11], (DEPTH, SSD_HEADS), f32, 1.0, 16.0))
    d_skip = 1.0 + 0.1 * nrm(ks[12], (DEPTH, SSD_HEADS))
    ssd_norm_w = 1.0 + 0.02 * nrm(ks[13], (DEPTH, D_SSD))
    ret_norm_w = 1.0 + 0.02 * nrm(ks[14], (DEPTH, D_RET))
    pool_w = nrm(ks[15], (DEPTH, POOL_GROUPS, POOL_GROUP_DIM, POOL_GROUP_DIM)) * POOL_GROUP_DIM ** -0.5
    pool_scale = 1.0 + 0.1 * nrm(ks[16], (DEPTH, D_POOL))
    w_out = nrm(ks[17], (DEPTH, D_MIX, D_MODEL)) * D_MIX ** -0.5
    final_norm_w = 1.0 + 0.02 * nrm(ks[18], (D_MODEL,))
    return {"x_prompt": x_prompt, "x_sample": x_sample,
            "state_ssm": state_ssm, "state_conv": state_conv, "state_ret": state_ret, "state_pool": state_pool,
            "norm_w": norm_w, "w_in": w_in, "conv_w": conv_w, "conv_b": conv_b,
            "dt_bias": dt_bias, "a_log": a_log, "d_skip": d_skip,
            "ssd_norm_w": ssd_norm_w, "ret_norm_w": ret_norm_w,
            "pool_w": pool_w, "pool_scale": pool_scale, "w_out": w_out, "final_norm_w": final_norm_w}

def reference(x_prompt, x_sample, state_ssm, state_conv, state_ret, state_pool,
              norm_w, w_in, conv_w, conv_b, dt_bias, a_log, d_skip,
              ssd_norm_w, ret_norm_w, pool_w, pool_scale, w_out, final_norm_w):
    dtp = x_prompt.dtype
    zero_ssm = jnp.zeros((BATCH, SSD_HEADS, SSD_HEAD_DIM, SSD_STATE), dtp)
    zero_conv = jnp.zeros((BATCH, CONV_WIDTH - 1, CONV_DIM), dtp)
    zero_ret = jnp.zeros((BATCH, RET_HEADS, RET_HEAD_DIM, RET_HEAD_DIM), dtp)
    zero_pool = jnp.zeros((BATCH, POOL_BUF, D_POOL), dtp)
    yp, ys = x_prompt, x_sample
    p_ssm, p_conv, p_ret, p_pool = [], [], [], []
    s_ssm, s_conv, s_ret, s_pool = [], [], [], []
    for i in range(DEPTH):
        lp = (norm_w[i], w_in[i], conv_w[i], conv_b[i], dt_bias[i], a_log[i], d_skip[i],
              ssd_norm_w[i], ret_norm_w[i], pool_w[i], pool_scale[i], w_out[i])
        yp, a1, a2, a3, a4 = mixer_layer(yp, zero_ssm, zero_conv, zero_ret, zero_pool, 0, *lp)
        ys, b1, b2, b3, b4 = mixer_layer(ys, state_ssm[i], state_conv[i], state_ret[i], state_pool[i], PAST_LEN, *lp)
        p_ssm.append(a1); p_conv.append(a2); p_ret.append(a3); p_pool.append(a4)
        s_ssm.append(b1); s_conv.append(b2); s_ret.append(b3); s_pool.append(b4)
    y_prompt = rmsnorm(yp, final_norm_w)
    y_sample = rmsnorm(ys, final_norm_w)
    return (y_prompt, y_sample,
            jnp.stack(p_ssm), jnp.stack(p_conv), jnp.stack(p_ret), jnp.stack(p_pool),
            jnp.stack(s_ssm), jnp.stack(s_conv), jnp.stack(s_ret), jnp.stack(s_pool))


_drawn_inputs = setup_inputs


def setup_inputs(seed=0):
    import zlib

    import numpy as np

    out = dict(_drawn_inputs(seed))
    spreads = {}
    factors = {'ssd_norm_w': 3.532, 'ret_norm_w': 22.563, 'final_norm_w': 8.461, 'pool_scale': 5.128}
    for name, (base, spread) in spreads.items():
        noise = np.random.default_rng([zlib.crc32(name.encode()), seed]).standard_normal(out[name].shape)
        drawn = base * np.exp(spread * noise) if base else spread * noise
        out[name] = __import__('jax').numpy.asarray(drawn.astype(out[name].dtype))
    for name, factor in factors.items():
        out[name] = (out[name] * factor).astype(out[name].dtype)
    return out
```

```python
from contextlib import ExitStack

import numpy as np

import concourse.bass as bass
from concourse import mybir

F32 = mybir.dt.float32
F32R = mybir.dt.float32r
ALU = mybir.AluOpType
ACT = mybir.ActivationFunctionType

P = 128
DEPTH = 2
D_MODEL = 1024
SEQ = 512
NB, NT = 8, 8
SMP = NB * NT
TOK = SEQ + SMP
HALF = TOK // 2
KT = D_MODEL // P
HEADS = 16
HD = 64
PAIRS = HEADS // 2
GROUPS = 2
CH = 128
TILES = SEQ // CH + 1
RH = 8
RP = RH // 2
CW = 4
CONV_CHUNKS = 12
WINDOWS = (2, 4, 8, 16)
PB = 15
PAST = 4096
EPS = 1e-6

U_DT = 0
U_CONV = 1
U_Q = U_CONV + CONV_CHUNKS
U_K = U_Q + RP
U_V = U_K + RP
U_POOL = U_V + RP
U_GPOOL = U_POOL + 4
U_Z = U_GPOOL + 4
U_GRET = U_Z + PAIRS
U_OUT = U_GRET + RP
OUT_CHUNKS = D_MODEL // P
UNITS = U_OUT + 2 * OUT_CHUNKS
CONV_ORDER = (8, 9, 10, 11, 0, 1, 2, 3, 4, 5, 6, 7)
RAW = 2

S_STK = 2
S_SSD = 14
S_SST = S_SSD + 2 * TILES
S_SSE = S_SST + NB // 2
S_RET = S_SSE
S_RST = S_RET + 2 * TILES
S_NORM = S_RST + NB // 2
assert S_NORM <= U_OUT - 2

HALO = 3 + SEQ + NB * (3 + NT)
CVO = HALO - 3
PHALO = PB + SEQ + NB * (PB + NT)

V_NW, V_CW, V_CB = 0, 8, 8 + 48
V_DS = V_CB + 12
V_SN = V_DS + 8
V_RN = V_SN + 8
V_PS = V_RN + 4
V_N = V_PS + 4


def table_places():
    at, n = {}, 0
    for name, w in (("ident", P), ("ones", P), ("blk", P), ("causal", P), ("smask", SMP), ("bmask", NB),
                    ("cos", TOK), ("sin", TOK), ("dmask", RH * CH), ("sdmask", RH * SMP),
                    ("inner", RP * CH), ("sinner", RP * NT), ("edec", RH), ("sedec", RH),
                    ("cdec", RP), ("scdec", RP), ("cnt", 4 * 16), ("fnw", KT)):
        at[name] = (n, w)
        n += w
    return at, n


TAB, TAB_N = table_places()


class Lane:

    def __init__(self, eng, chain):
        self.eng, self.chain, self.n, self.last = eng, chain, 0, None

    def go(self, ins, signal=None, n=None):
        if signal is None:
            self.n += 1
            signal, n = self.chain, self.n
        ins.then_inc(signal, 1)
        self.last = (signal, n)

    def settle(self):
        if self.last is not None:
            self.eng.wait_ge(*self.last)
            self.last = None

    def wait(self, signal, n):
        self.eng.wait_ge(signal, n)

    def close(self):
        self.settle()
        if self.n:
            self.eng.wait_ge(self.chain, self.n)
        self.n = 0


def trunk(nc: bass.Bass, a):
    with ExitStack() as ctx:
        top = [(nc.sbuf_base + 63) // 64 * 64]

        def place(name, shape, dt=F32, at=None):
            size = 4
            for d in shape[1:]:
                size *= d
            off = top[0] if at is None else at
            t = nc.alloc_sbuf_tensor_at(name, shape, dt, offset=off)
            if at is None:
                top[0] = off + (size + 31) // 32 * 32
                assert top[0] <= nc.sbuf_usable_end, (name, top[0] - nc.sbuf_usable_end)
            return t

        def sem(name):
            return ctx.enter_context(nc.semaphore(name))

        hin = place("hin", [P, 2, KT, TOK], F32R)
        w_raw = place("w_raw", [P, RAW, KT, P])
        w_hi = place("w_hi", [P, 2, KT, P], F32R)
        w_lo = place("w_lo", [P, 2, KT, P], F32R)
        work = top[0]
        mix = place("mix", [P, 2, 2, 4, TOK], F32R)
        decay = place("decay", [P, 2, HEADS, CH], at=work)
        cdec_t = place("c_decayed", [P, HEADS, CH], at=work + 4 * 4096)
        xdt = place("xdt", [P, HEADS * HD], at=work + 4 * 6144)
        xdw = place("xdt_to_end", [P, HEADS * HD], at=work + 4 * 7168)
        hT = place("ssm_state", [P, HEADS * HD], at=work + 4 * 8192)
        h0 = [place(f"h0_{i}", [P, HEADS * HD], at=work + 4 * (2048 + 1024 * i)) for i in range(4)]
        ret_work = work
        rs0 = [place(f"ret0_{i}", [P, RP, P], at=ret_work + 4 * 512 * i) for i in range(3)]
        pmat = place("ret_probs", [P, 2, RP, CH], at=ret_work + 4 * 1536)
        kw = place("k_to_end", [P, RP * P], at=ret_work + 4 * 2560)
        kwm = place("k_to_end_seq", [P, RP * P], at=ret_work + 4 * 3072)
        qd = place("q_decayed", [P, RP, CH], at=ret_work + 4 * 3584)
        rS = place("ret_state", [P, RP, P], at=ret_work + 4 * 4096)
        xbc = place("xbc", [P, CONV_CHUNKS, TOK])
        qk_at = top[0]
        qk = place("qk", [P, 2 * RP, TOK])
        x = place("x", [P, KT, TOK], at=qk_at)
        vT = place("vT", [P, RP, TOK])
        halo = place("halo", [P, 2, PHALO])
        cvt = place("conv_out", [P, 2, PHALO])
        tmp = place("tmp", [P, 2, TOK])
        ssq = place("ssq", [P, TOK])
        rstd = place("rstd", [P, TOK])
        tab = place("tab", [P, TAB_N])
        vec = place("vec", [P, V_N])
        hvec = place("head_vec", [HEADS, 2])
        pw = place("pool_w", [P, 4, P])
        cst = place("conv_state", [P, CONV_CHUNKS, NB, 3])
        cso = place("conv_state_out", [P, CONV_CHUNKS, 1 + NB, 3])
        pst = place("pool_state", [P, 4, NB, PB])
        pso = place("pool_state_out", [P, 4, 1 + NB, PB])
        stk = place("stacked", [96, TOK])
        tokv = place("token_vecs", [P, TILES, 96])
        gm = place("scores", [P, GROUPS, CH])
        btok = place("b_tok", [P, GROUPS, P])
        bseq = place("b_tok_seq", [P, 2, GROUPS, P])
        el = place("exp_last", [P, HEADS])
        els = place("exp_last_sample", [P, HEADS, NB])
        dt_raw, dt_e, dt_u, dt_l, dt_r, dt_s, dt_v, dt_w = (xbc[0:HEADS, i, :] for i in range(8))
        reset = vT[0:HEADS, 0, :]
        na = place("neg_a", [HEADS, 1])
        ecs = place("exp_cum_sample", [P, PAIRS, SMP])
        vtok = place("v_tok", [P, RP * P])
        pad = place("pad", [P, 2])
        pool_pad = place("pool_pad", [P, 2])
        eps = place("eps", [P, 1])

        acc = ctx.enter_context(nc.psum_tensor("acc", [P, 2, 2, 512], F32))
        mb = ctx.enter_context(nc.psum_tensor("misc", [P, 4, 512], F32))

        def T(name):
            o, w = TAB[name]
            return tab[:, o:o + w]

        ident, ones, blk = T("ident"), T("ones"), T("blk")

        def acc_of(u):
            if u < U_OUT:
                return acc[:, u % 2, :, 0:HALF]
            return acc[:, (u - U_OUT) % 2, :, 0:HALF]

        def halves(ap):
            return ap.rearrange("p (a n) -> p a n", a=2)

        def cols(t):
            return slice(t * CH, t * CH + (CH if t < TILES - 1 else SMP))

        def rows(t):
            return CH if t < TILES - 1 else SMP

        s_tab = sem("tables_loaded")
        s_x = sem("x_loaded")
        s_raw = [sem(f"w_loaded_{i}") for i in range(RAW)]
        s_par = sem("params_loaded")
        s_st = sem("small_states_loaded")
        w_hid = sem("w_high")
        w_split = sem("w_split")
        proj = sem("projected")
        evac = sem("acc_read")
        x_new = sem("x_updated")
        sqd = sem("squared")
        sq_add = sem("squares_added")
        nsum = sem("norm_sum")
        n_rstd = sem("norm_rstd")
        h_full = sem("h_scaled")
        h_hi = sem("h_high")
        h_lo = sem("h_split")
        dt_s1 = sem("dt_exp")
        dt_s2 = sem("dt_one_plus")
        dt_s3 = sem("dt_log")
        cum_ok = sem("cum_ready")
        wl_ok = sem("exp_to_end")
        stk_ok = sem("stacked_ready")
        stk_T = sem("stacked_turned")
        tokv_ok = sem("token_vecs_ready")
        cum_out = sem("cum_stored")
        cum_in = [sem(f"cum_spread_{i}") for i in range(2)]
        ecs_in = sem("cum_rows_spread")
        ecs_ok = sem("exp_cum_rows")
        halo_in = sem("halo_filled")
        halo_used = sem("halo_used")
        xbc_ok = sem("xbc_ready")
        rot = sem("rotated")
        sT = sem("ssd_turned")
        s_xdt = sem("ssd_xdt")
        s_bt = sem("ssd_b_tok")
        s_exp = sem("ssd_exps")
        s_row = sem("ssd_row_exps")
        s_seg = sem("ssd_segments")
        s_ec = sem("ssd_c_decayed")
        s_M = sem("ssd_weights")
        s_S = sem("ssd_state_sum")
        s_Y = sem("ssd_y_sum")
        s_y = sem("ssd_y_read")
        s_h = sem("ssd_state")
        h0_in = [sem(f"h0_loaded_{i}") for i in range(4)]
        h0_out = [sem(f"h0_stored_{i}") for i in range(4)]
        b_seq = sem("b_tok_seq_ready")
        hs_S = sem("sample_state_sum")
        hs_n = sem("sample_state")
        hs_I = sem("sample_inter")
        hs_y = sem("sample_y")
        hp_out = sem("ssm_state_stored")
        rT = sem("ret_turned")
        r_P = sem("ret_weights")
        r_v = sem("ret_v_tok")
        r_Y = sem("ret_y_sum")
        r_S = sem("ret_state_sum")
        r_y = sem("ret_y_read")
        r_s = sem("ret_state_new")
        r0_in = [sem(f"ret0_loaded_{i}") for i in range(3)]
        r0_out = [sem(f"ret0_stored_{i}") for i in range(3)]
        r_zero = sem("ret_slots_zeroed")
        r_kwm = sem("k_seq_ready")
        rs_S = sem("sample_ret_sum")
        rs_n = sem("sample_ret")
        rs_y = sem("sample_ret_y")
        rp_out = sem("ret_state_stored")
        pooled_ok = sem("pooled")
        pool_mm = sem("pool_mixed")
        g_pool = sem("pool_gate")
        g_z = sem("z_gate")
        g_z_used = sem("z_gated")
        g_ret = sem("ret_gate")
        mix_full = sem("mix_full")
        mix_hi = sem("mix_high")
        mix_lo = sem("mix_split")
        b_sq = sem("branch_squared")
        b_add = sem("branch_squares_added")
        b_sum = sem("branch_norm_sum")
        b_rstd = sem("branch_rstd")
        b_used = sem("branch_rstd_used")
        y_full = sem("ssd_out_full")
        y_hi = sem("ssd_out_high")
        y_lo = sem("ssd_out_split")
        states_out = sem("small_states_stored")
        x_out = sem("x_stored")
        x_back = sem("x_reloaded")
        ret_free = sem("ret_work_free")
        eps_ok = sem("eps_set")
        f_out = sem("y_stored")
        f_ok = sem("y_ready")
        chain_v, chain_a, chain_p = sem("vector_order"), sem("scalar_order"), sem("pool_order")
        layer_over = sem("layer_over")
        next_pe, next_act, next_dve, next_sp = (sem(f"next_layer_{e}") for e in ("pe", "act", "dve", "sp"))
        to_clear = range(s_tab.num, layer_over.num + 1)

        def next_layer(eng, begin):
            eng.sem_inc(layer_over, 1)
            eng.wait_ge(begin, 1)
            eng.sem_clear(begin)

        def clear_signals(pool):
            pool.wait_ge(layer_over, 4)
            pool.dma_reset(to_clear)
            pool.sem_clear(to_clear)
            for begin in (next_pe, next_act, next_dve, next_sp):
                pool.sem_inc(begin, 1)

        block = ctx.enter_context(nc.Block())

        @block.sync
        def _(sp):
            sp.dma_start(x[:, :, :], a["x"]).then_inc(s_x, 16)
            sp.dma_start(tab[:, :], a["tab"]).then_inc(s_tab, 16)
            next_layer(sp, next_sp)
            with sp.Fori(0, DEPTH) as l:
                for u in range(UNITS):
                    if u >= RAW:
                        sp.wait_ge(w_split, u - RAW + 1)
                    if u == RAW:
                        sp.dma_start(cst[:, :, :, :], a["cst"][l]).then_inc(s_st, 16)
                        sp.dma_start(pst[:, :, :, :], a["pst"][l]).then_inc(s_st, 16)
                    sp.dma_start(w_raw[:, u % RAW, :, :], a["w"][l, u]).then_inc(s_raw[u % RAW], 16)
                    if u == 0:
                        sp.dma_start(vec[:, :], a["vec"][l]).then_inc(s_par, 16)
                        sp.dma_start(hvec[:, :], a["hvec"][l]).then_inc(s_par, 16)
                        sp.dma_start(pw[:, :, :], a["pw"][l]).then_inc(s_par, 16)
                        sp.dma_start(reset, a["reset"]).then_inc(s_par, 16)
                next_layer(sp, next_sp)

        @block.tensor
        def _(pe):
            def project(u):
                pe.wait_ge(w_split, u + 1)
                o = u - U_OUT
                if 2 <= u < U_OUT:
                    pe.wait_ge(evac, u - 1)
                elif u in (U_OUT, U_OUT + 1):
                    pe.wait_ge(evac, U_OUT)
                elif o > 1 and o % 4 < 2:
                    pe.wait_ge(x_new, 2 * (o // 4) - 1 + o % 4)
                src = hin
                first, last = True, True
                if o >= 0:
                    first, last = o % 4 < 2, o % 4 >= 2
                    if first and o == 0:
                        pe.wait_ge(mix_lo, 8)
                out = acc_of(u)
                for half in range(2):
                    c = slice(half * HALF, (half + 1) * HALF)
                    for k in range(KT):
                        if half == 0 and u == 0:
                            pe.wait_ge(h_lo, k + 1)
                        if half == 0 and o == 2:
                            pe.wait_ge(y_lo, k + 1)
                        if o >= 0 and first:
                            hi, lo = mix[:, k // 4, 0, k % 4, c], mix[:, k // 4, 1, k % 4, c]
                        else:
                            hi, lo = src[:, 0, k, c], src[:, 1, k, c]
                        wh, wl = w_hi[:, u % 2, k, :], w_lo[:, u % 2, k, :]
                        pe.matmul(out[:, half, :], wh, hi, start=first and k == 0, stop=False)
                        pe.matmul(out[:, half, :], wh, lo, start=False, stop=False)
                        mm = pe.matmul(out[:, half, :], wl, hi, start=False, stop=last and k == KT - 1)
                mm.then_inc(proj, 1)

            def norm_sum():
                pe.wait_ge(sq_add, KT)
                for half in range(2):
                    mm = pe.matmul(mb[:, 2 + half, 0:HALF], ones, halves(ssq[:, :])[:, half, :], start=True, stop=True)
                mm.then_inc(nsum, 1)

            def ssd_turn(t):
                n = rows(t)
                if t == 0:
                    pe.wait_ge(xbc_ok, CONV_CHUNKS)
                    pe.wait_ge(tokv_ok, 1)
                else:
                    pe.wait_ge(s_h, t)
                    pe.wait_ge(s_y, t)
                for j in range(PAIRS):
                    pe.transpose(mb[0:n, j // 4, (j % 4) * P:(j % 4 + 1) * P], xbc[:, j, cols(t)], ident)
                for g in range(GROUPS):
                    pe.matmul(mb[0:n, 2, g * P:g * P + n], xbc[:, 8 + g, cols(t)], xbc[:, 10 + g, cols(t)],
                              start=True, stop=True)
                for g in range(GROUPS):
                    mm = pe.transpose(mb[0:n, 3, g * P:(g + 1) * P], xbc[:, 8 + g, cols(t)], ident)
                mm.then_inc(sT, 1)

            def ssd_y(t):
                n = rows(t)
                pe.wait_ge(s_xdt, t + 1)
                pe.wait_ge(s_bt, t + 1)
                if t < TILES - 1:
                    for g in range(GROUPS):
                        mm = pe.matmul(mb[:, g, :], btok[:, g, :], xdw[:, g * 512:(g + 1) * 512], start=True, stop=True)
                    mm.then_inc(s_S, 1)
                pe.wait_ge(s_M, t + 1)
                inter = 0 < t < TILES - 1
                if inter:
                    pe.wait_ge(s_ec, t)
                for j in range(PAIRS):
                    if t < TILES - 1:
                        dst = mb[:, 2 + j // 4, (j % 4) * P:(j % 4) * P + n]
                    else:
                        dst = mb[:, 2, j * SMP:(j + 1) * SMP]
                    for e in range(2):
                        h = 2 * j + e
                        r = slice(e * HD, (e + 1) * HD)
                        mm = pe.matmul(dst[r, :], xdt[0:n, h * HD:(h + 1) * HD], decay[0:n, t % 2, h, 0:n],
                                       start=True, stop=not inter)
                        if inter:
                            mm = pe.matmul(dst[r, :], hT[:, h * HD:(h + 1) * HD], cdec_t[:, h, :],
                                           start=False, stop=True)
                mm.then_inc(s_Y, 1)

            def ssd_sample(b):
                c = slice(SEQ + b * NT, SEQ + (b + 1) * NT)
                pe.wait_ge(h0_in[b % 4], 16 * (b // 4 + 1))
                if b == 0:
                    pe.wait_ge(s_y, TILES - 1)
                for j in range(PAIRS):
                    mm = pe.matmul(mb[:, 3, j * SMP + b * NT:j * SMP + (b + 1) * NT], h0[b % 4][:, j * P:(j + 1) * P],
                                   xbc[:, 10 + j // 4, c], start=True, stop=True)
                mm.then_inc(hs_I, 1)
                pe.wait_ge(b_seq, b + 1)
                if b == 0:
                    pe.wait_ge(s_y, TILES)
                for g in range(GROUPS):
                    i = 2 * b + g
                    if i >= 3:
                        pe.wait_ge(hs_n, i - 2)
                    pe.matmul(mb[:, i % 3, :], bseq[0:SMP, b % 2, g, :], xdw[0:SMP, g * 512:(g + 1) * 512],
                              start=True, stop=True).then_inc(hs_S, 1)

            def ret_turn(t):
                n = rows(t)
                if t == 0:
                    pe.wait_ge(rot, 2 * RP)
                    pe.wait_ge(evac, U_POOL)
                    pe.wait_ge(hs_n, 2 * NB)
                    pe.wait_ge(hs_y, 1)
                else:
                    pe.wait_ge(r_y, t)
                    pe.wait_ge(r_s, t)
                for j in range(RP):
                    for e in range(2):
                        r = slice(e * HD, (e + 1) * HD)
                        pe.matmul(mb[0:n, e, j * P:j * P + n], qk[r, RP + j, cols(t)], qk[r, j, cols(t)],
                                  start=True, stop=True)
                for j in range(RP):
                    pe.transpose(mb[0:n, 2, j * P:(j + 1) * P], qk[:, RP + j, cols(t)], ident)
                for j in range(RP):
                    mm = pe.transpose(mb[0:n, 3, j * P:(j + 1) * P], vT[:, j, cols(t)], ident)
                mm.then_inc(rT, 1)

            def ret_y(t):
                n = rows(t)
                pe.wait_ge(r_P, t + 1)
                pe.wait_ge(r_v, t + 1)
                inter = 0 < t < TILES - 1
                for j in range(RP):
                    dst = mb[:, 0, j * P:j * P + n]
                    if inter:
                        pe.matmul(dst, rS[:, j, :], qd[:, j, :], start=True, stop=False, skip_group_check=True)
                    for e in range(2):
                        r = slice(e * HD, (e + 1) * HD)
                        c = slice(j * P + e * HD, j * P + (e + 1) * HD)
                        mm = pe.matmul(dst[r, :], vtok[0:n, c], pmat[0:n, e, j, 0:n], start=not inter, stop=True,
                                       skip_group_check=inter)
                mm.then_inc(r_Y, 1)
                if t < TILES - 1:
                    for j in range(RP):
                        c = slice(j * P, (j + 1) * P)
                        mm = pe.matmul(mb[:, 1, c], kw[:, c], vtok[:, c], start=True, stop=True)
                    mm.then_inc(r_S, 1)

            def ret_sample(b):
                pe.wait_ge(r0_in[b % 3], 32 * (b // 3 + 1))
                if b == 0:
                    pe.wait_ge(r_zero, 1)
                pe.wait_ge(r_kwm, b + 1)
                for j in range(RP):
                    pe.matmul(mb[:, 3, j * SMP + b * NT:j * SMP + (b + 1) * NT], rs0[b % 3][:, j, :],
                              qd[:, j, b * NT:(b + 1) * NT], start=True, stop=True)
                if b >= 2:
                    pe.wait_ge(rs_n, b - 1)
                for j in range(RP):
                    c = slice(j * P, (j + 1) * P)
                    mm = pe.matmul(mb[:, 1 + b % 2, c], kwm[0:SMP, c], vtok[0:SMP, c], start=True, stop=True)
                mm.then_inc(rs_S, 1)

            def branch_sum(i):
                o = 2 * (i % 2)
                if i == 0:
                    pe.wait_ge(rs_y, 1)
                    pe.wait_ge(rs_n, NB)
                if i >= 2:
                    pe.wait_ge(b_rstd, i - 1)
                if i < GROUPS:
                    pe.wait_ge(b_add, 4 * (i + 1))
                    m, src = ones, ssq[:, :]
                else:
                    pe.wait_ge(b_sq, PAIRS + i - GROUPS + 1)
                    m, src = blk, tmp[:, i % 2, :]
                for half in range(2):
                    mm = pe.matmul(mb[:, o + half, 0:HALF], m, halves(src)[:, half, :], start=True, stop=True)
                mm.then_inc(b_sum, 1)

            def pool_mm_(g):
                pe.wait_ge(pooled_ok, g + 1)
                pe.wait_ge(evac, U_GPOOL + g + 1)
                dst = acc_of(U_GPOOL + g)
                for half in range(2):
                    mm = pe.matmul(dst[:, half, :], pw[:, g, :], halves(xbc[:, 8 + g, :])[:, half, :],
                                   start=True, stop=True)
                mm.then_inc(pool_mm, 1)

            pe.wait_ge(s_tab, 16)
            norm_sum()
            pe.wait_ge(nsum, 1)
            next_layer(pe, next_pe)
            with pe.Fori(0, DEPTH):
                for u in range(UNITS):
                    if U_GPOOL + 2 <= u < U_GPOOL + 6:
                        pe.wait_ge(mix_full, u - U_GPOOL - 1)
                    project(u)
                    if U_GPOOL + 1 <= u < U_GPOOL + 5:
                        pool_mm_(u - U_GPOOL - 1)
                    if u == S_STK:
                        pe.wait_ge(stk_ok, 1)
                        for t in range(TILES):
                            mm = pe.transpose(mb[0:rows(t), t // 4, (t % 4) * 96:(t % 4 + 1) * 96],
                                              stk[:, cols(t)], ident[0:96, 0:96])
                        mm.then_inc(stk_T, 1)
                    if S_SSD <= u < S_SST:
                        t = (u - S_SSD) // 2
                        (ssd_turn if (u - S_SSD) % 2 == 0 else ssd_y)(t)
                    if S_SST <= u < S_SSE:
                        ssd_sample(2 * (u - S_SST))
                        ssd_sample(2 * (u - S_SST) + 1)
                    if S_RET <= u < S_RST:
                        t = (u - S_RET) // 2
                        (ret_turn if (u - S_RET) % 2 == 0 else ret_y)(t)
                    if S_RST <= u < S_NORM:
                        ret_sample(2 * (u - S_RST))
                        ret_sample(2 * (u - S_RST) + 1)
                    if u == S_NORM:
                        for i in range(GROUPS):
                            branch_sum(i)
                    if u == S_NORM + 1:
                        for i in range(GROUPS, GROUPS + RP):
                            branch_sum(i)
                norm_sum()
                pe.wait_ge(nsum, 1)
                next_layer(pe, next_pe)

        @block.scalar
        def _(eng):
            lane = Lane(eng, chain_a)
            go, settle, wait = lane.go, lane.settle, lane.wait
            act = nc.scalar.activation

            def high(u):
                wait(s_raw[u % RAW], 16 * (u // RAW + 1))
                if u >= 2:
                    wait(proj, u - 1)
                go(act(w_hi[:, u % 2, :, :], w_raw[:, u % RAW, :, :], ACT.Copy), w_hid, u + 1)

            def square(j):
                go(act(tmp[:, j % 2, :], x[:, j, :], ACT.Square), sqd, j + 1)

            def rs(src, n):
                go(act(halves(rstd[:, :]), src, ACT.Ln, scale=1.0 / n, bias=eps[:, 0:1]))
                settle()
                return act(rstd[:, :], rstd[:, :], ACT.Exp, scale=-0.5)

            def norm_rstd():
                wait(nsum, 1)
                go(rs(mb[:, 2:4, 0:HALF], D_MODEL), n_rstd, 1)

            def read_out(u):
                wait(proj, u + 1)
                src = acc_of(u)
                if u == U_DT:
                    go(act(halves(dt_raw), src[0:HEADS], ACT.Identity, bias=hvec[:, 0:1]), evac, u + 1)
                elif u < U_Q:
                    i = u - U_CONV
                    wait(halo_in, i + 1)
                    hb = halo[:, i % 2, 0:HALO]
                    go(act(hb[:, 3:3 + HALF], src[:, 0, :], ACT.Copy))
                    go(act(hb[:, 3 + HALF:3 + SEQ], src[:, 1, 0:SEQ - HALF], ACT.Copy))
                    go(act(hb[:, 3 + SEQ:].rearrange("p (b n) -> p b n", b=NB)[:, :, 3:],
                           src[:, 1, SEQ - HALF:].rearrange("p (b n) -> p b n", b=NB), ACT.Copy), evac, u + 1)
                elif u < U_V:
                    i = u - U_Q
                    if i == 0:
                        wait(x_out, 16)
                    go(act(halves(qk[:, i, :]), src, ACT.Copy, scale=1.0 if i < RP else HD ** -0.5), evac, u + 1)
                elif u < U_POOL:
                    go(act(halves(vT[:, u - U_V, :]), src, ACT.Copy), evac, u + 1)
                elif u < U_GPOOL:
                    i = u - U_POOL
                    wait(halo_in, CONV_CHUNKS + i + 1)
                    hb = halo[:, i % 2, :]
                    go(act(hb[:, PB:PB + HALF], src[:, 0, :], ACT.Copy))
                    go(act(hb[:, PB + HALF:PB + SEQ], src[:, 1, 0:SEQ - HALF], ACT.Copy))
                    go(act(hb[:, PB + SEQ:].rearrange("p (b n) -> p b n", b=NB)[:, :, PB:],
                           src[:, 1, SEQ - HALF:].rearrange("p (b n) -> p b n", b=NB), ACT.Copy), evac, u + 1)
                elif u < U_Z:
                    i = u - U_GPOOL
                    if i >= 2:
                        wait(mix_full, i - 1)
                    go(act(halves(tmp[:, i % 2, :]), src, ACT.Silu), evac, u + 1)
                elif u < U_GRET:
                    i = u - U_Z
                    if i < 2:
                        wait(mix_full, 3 + i)
                    else:
                        wait(g_z_used, i - 1)
                    go(act(halves(tmp[:, i % 2, :]), src, ACT.Silu), evac, u + 1)
                else:
                    i = u - U_GRET
                    wait(rT, TILES)
                    go(act(halves(qk[:, RP + i, :]), src, ACT.Silu), evac, u + 1)

            def ssd_row_exps(t):
                m = decay[:, t % 2, :, :]
                wait(cum_in[t % 2], 16 * (t // 2 + 1))
                if t < TILES - 1:
                    if t > 1:
                        wait(s_Y, t)
                    go(act(cdec_t[:, :, :], m, ACT.Exp))
                    if t > 1:
                        wait(s_h, t)
                    go(act(el[:, :], m[:, :, CH - 1], ACT.Exp), s_row, t)
                else:
                    ms = m[:, :, 0:SMP].rearrange("p h (b k) -> p h b k", b=NB)
                    go(act(els[:, :, :], ms[:, :, :, NT - 1], ACT.Exp), s_row, t)
                    wait(ecs_in, 32)
                    go(act(ecs[:, :, :], ecs[:, :, :], ACT.Exp), ecs_ok, 1)

            def ssd_decay(t):
                n = rows(t)
                m = decay[0:n, t % 2, :, 0:n]
                wait(s_seg, t + 1)
                go(act(m, m, ACT.Exp), s_exp, t + 1)

            def ret_slot(t):
                n = rows(t)
                wait(rT, t + 1)
                if t > 0:
                    wait(r_S, t)
                go(act(vtok[0:n, :], mb[0:n, 3, :], ACT.Copy), r_v, t + 1)

            eng.wait_ge(s_x, 16)
            eng.wait_ge(eps_ok, 1)
            for j in range(KT):
                if j >= 2:
                    eng.wait_ge(sq_add, j - 1)
                square(j)
            norm_rstd()
            lane.close()
            next_layer(eng, next_act)
            with eng.Fori(0, DEPTH):
                high(0)
                high(1)
                for j in range(KT):
                    wait(h_full, j + 1)
                    go(act(hin[:, 0, j, :], tmp[:, j % 2, :], ACT.Copy), h_hi, j + 1)
                wait(s_par, 64)
                for u in range(UNITS):
                    if u + 2 < UNITS:
                        high(u + 2)
                    if u < U_OUT:
                        read_out(u)
                    if u == U_DT:
                        settle()
                        go(act(dt_e, dt_raw, ACT.Abs))
                        settle()
                        go(act(dt_e, dt_e, ACT.Exp, scale=-1.0), dt_s1, 1)
                        go(act(na[:, :], hvec[:, 1:2], ACT.Exp))
                        wait(dt_s2, 1)
                        settle()
                        go(act(dt_l, dt_u, ACT.Ln), dt_s3, 1)
                        wait(cum_ok, 1)
                        go(act(dt_w, dt_s, ACT.Exp), wl_ok, 1)
                    if U_CONV < u <= U_Q:
                        i = u - U_CONV - 1
                        k = CONV_ORDER[i]
                        wait(halo_used, i + 1)
                        cb = vec[:, V_CB + k:V_CB + k + 1]
                        go(act(xbc[:, k, 0:SEQ], cvt[:, i % 2, 0:SEQ], ACT.Silu, bias=cb))
                        go(act(xbc[:, k, SEQ:].rearrange("p (b n) -> p b n", b=NB),
                               cvt[:, i % 2, 3 + SEQ:HALO].rearrange(
                                   "p (b n) -> p b n", b=NB)[:, :, 0:NT], ACT.Silu, bias=cb),
                           xbc_ok, i + 1)
                    if u == U_Q:
                        ssd_decay(0)
                    if S_SSD <= u < S_SST:
                        t = (u - S_SSD) // 2
                        if (u - S_SSD) % 2 == 0:
                            wait(sT, t + 1)
                            if t > 0:
                                wait(s_S, t)
                            n = rows(t)
                            go(act(btok[0:n, :, :], mb[0:n, 3, 0:256].rearrange("p (g n) -> p g n", g=2), ACT.Copy),
                               s_bt, t + 1)
                            if t > 0:
                                ssd_decay(t)
                        elif t + 1 < TILES:
                            ssd_row_exps(t + 1)
                    if S_RET <= u < S_RST and (u - S_RET) % 2 == 0:
                        ret_slot((u - S_RET) // 2)
                    if u in (S_NORM, S_NORM + 1):
                        for i in (range(GROUPS) if u == S_NORM else range(GROUPS, GROUPS + RP)):
                            if i < GROUPS:
                                for j in range(4 * i, 4 * i + 4):
                                    if j < 2:
                                        wait(g_z_used, PAIRS)
                                    else:
                                        wait(b_add, j - 1)
                                    go(act(tmp[:, j % 2, :], xbc[:, j, :], ACT.Square), b_sq, j + 1)
                            else:
                                j = i - GROUPS
                                if j < 2:
                                    wait(b_add, PAIRS)
                                else:
                                    wait(b_sum, i - 1)
                                go(act(tmp[:, i % 2, :], qk[:, j, :], ACT.Square), b_sq, PAIRS + j + 1)
                            wait(b_sum, i + 1)
                            if i > 0:
                                wait(b_used, i)
                            o = 2 * (i % 2)
                            go(rs(mb[:, o:o + 2, 0:HALF], 512 if i < GROUPS else HD), b_rstd, i + 1)
                    if U_GPOOL + 1 <= u < U_GPOOL + 5:
                        i = u - U_GPOOL - 1
                        if i == 0:
                            wait(r_zero, 1)
                        wait(mix_full, i + 1)
                        go(act(mix[:, 1, 0, i, :], cvt[:, i % 2, 0:TOK], ACT.Copy), mix_hi, i + 1)
                    if u == U_GRET + RP - 1:
                        wait(ret_free, 1)
                        for i in range(RP):
                            wait(mix_full, 4 + i + 1)
                            go(act(mix[:, 0, 0, i, :], qk[:, i, :], ACT.Copy), mix_hi, 4 + i + 1)
                    if u == U_OUT - 1:
                        wait(proj, U_OUT)
                        for j in range(PAIRS):
                            wait(y_full, j + 1)
                            go(act(hin[:, 0, j, :], xbc[:, j, :], ACT.Copy), y_hi, j + 1)
                    o = u - U_OUT
                    if o >= 0 and o % 4 >= 2:
                        m = 2 * (o // 4) + o % 2
                        wait(x_new, m + 1)
                        if m >= 2:
                            wait(sq_add, m - 1)
                        square(m)
                norm_rstd()
                lane.close()
                next_layer(eng, next_act)

        @block.vector
        def _(eng):
            lane = Lane(eng, chain_v)
            go, settle, wait = lane.go, lane.settle, lane.wait
            V = nc.vector

            def split(u):
                wait(w_hid, u + 1)
                go(V.tensor_tensor(w_lo[:, u % 2, :, :], w_raw[:, u % RAW, :, :], w_hi[:, u % 2, :, :].bitcast(F32),
                                   ALU.subtract), w_split, u + 1)

            def add_square(j):
                wait(sqd, j + 1)
                settle()
                if j == 0:
                    go(V.tensor_copy(ssq[:, :], tmp[:, j % 2, :]), sq_add, j + 1)
                else:
                    go(V.tensor_tensor(ssq[:, :], ssq[:, :], tmp[:, j % 2, :], ALU.add), sq_add, j + 1)

            def v_(o, n=1):
                return vec[:, o:o + n]

            def dt_chain():
                wait(dt_s1, 1)
                go(V.tensor_scalar(dt_u, dt_e, 1.0, None, ALU.add), dt_s2, 1)
                settle()
                go(V.tensor_scalar(dt_r, dt_u, 1.0, None, ALU.subtract))
                settle()
                go(V.tensor_scalar(dt_v, dt_r, 0.0, None, ALU.is_equal))
                go(V.tensor_scalar(dt_s, dt_r, 1e-30, None, ALU.max))
                settle()
                go(V.tensor_tensor(dt_v, dt_v, dt_e, ALU.mult))
                go(V.reciprocal(dt_r, dt_s))
                settle()
                go(V.tensor_tensor(dt_r, dt_r, dt_e, ALU.mult))
                settle()
                wait(dt_s3, 1)
                go(V.tensor_tensor(dt_r, dt_r, dt_l, ALU.mult))
                settle()
                go(V.tensor_tensor(dt_r, dt_r, dt_v, ALU.add))
                settle()
                go(V.scalar_tensor_tensor(out=dt_r, in0=dt_raw, scalar=0.0, in1=dt_r, op0=ALU.max, op1=ALU.add))
                settle()
                go(V.tensor_scalar(dt_v, dt_r, na[:, 0:1], -1.0, ALU.mult, ALU.mult))
                go(V.tensor_copy(stk[32:32 + HEADS, :], dt_r))
                settle()
                go(V.tensor_tensor_scan(dt_u, reset, dt_v, 0.0, ALU.mult, ALU.add))
                settle()
                go(V.tensor_scalar(stk[0:HEADS, :], dt_u, -1.0, None, ALU.mult))
                for q, (o, n, w) in enumerate(((0, TILES - 1, CH), (SEQ, NB, NT))):
                    cu = dt_u[:, o:o + n * w].rearrange("p (a b) -> p a b", a=n)
                    lastc = cu[:, :, w - 1:w].to_broadcast([HEADS, n, w])
                    i = V.tensor_tensor(dt_s[:, o:o + n * w].rearrange("p (a b) -> p a b", a=n), lastc, cu,
                                        ALU.subtract)
                    if q == 0:
                        go(i)
                        settle()
                    else:
                        go(i, cum_ok, 1)
                wait(wl_ok, 1)
                settle()
                go(V.tensor_tensor(dt_w, dt_w, dt_r, ALU.mult))
                settle()
                go(V.tensor_copy(stk[64:64 + HEADS, :], dt_w), stk_ok, 1)

            def conv(i):
                k = CONV_ORDER[i]
                wait(evac, U_CONV + i + 1)
                wait(halo_in, i + 1)
                if i >= 2:
                    wait(xbc_ok, i - 1)
                h, o = halo[:, i % 2, :], cvt[:, i % 2, 0:CVO]
                w = [v_(V_CW + 4 * k + c) for c in range(CW)]
                settle()
                go(V.tensor_scalar(o, h[:, 3:3 + CVO], w[3], None, ALU.mult))
                for c in (2, 1, 0):
                    settle()
                    ins = V.scalar_tensor_tensor(out=o, in0=h[:, c:c + CVO], scalar=w[c], in1=o, op0=ALU.mult,
                                                 op1=ALU.add)
                    if c:
                        go(ins)
                    else:
                        go(ins, halo_used, i + 1)

            def rotate(i):
                wait(evac, U_Q + i + 1)
                q = qk[:, i, :]
                settle()
                go(V.stream_shuffle(cvt[:, 0, 0:TOK], q, [(p + 16) % 32 for p in range(32)]))
                settle()
                go(V.tensor_tensor(cvt[:, 1, 0:TOK], cvt[:, 0, 0:TOK], T("sin"), ALU.mult))
                go(V.tensor_tensor(q, q, T("cos"), ALU.mult))
                settle()
                go(V.tensor_tensor(q, q, cvt[:, 1, 0:TOK], ALU.add), rot, i + 1)

            def heads(ap, n=HEADS):
                return ap.rearrange("p (h d) -> p h d", h=n)

            def segments(t):
                n = rows(t)
                if t == 0:
                    wait(cum_in[0], 16)
                else:
                    wait(s_row, t)
                settle()
                for h in range(HEADS):
                    m = decay[0:n, t % 2, h, 0:n]
                    ins = V.tensor_scalar(m, m, tokv[0:n, t, h:h + 1], 0.0, ALU.add, ALU.min)
                    if h < HEADS - 1:
                        go(ins)
                    else:
                        go(ins, s_seg, t + 1)

            def ssd_1(t):
                n = rows(t)
                wait(sT, t + 1)
                src = mb[0:n, 0:2, :].rearrange("p a (h d) -> p (a h) d", d=HD)
                dt_b = tokv[0:n, t, 32:48].unsqueeze(2).to_broadcast([n, HEADS, HD])
                dw_b = tokv[0:n, t, 64:80].unsqueeze(2).to_broadcast([n, HEADS, HD])
                settle()
                go(V.tensor_tensor(heads(xdt[0:n, :]), src, dt_b, ALU.mult))
                go(V.tensor_tensor(heads(xdw[0:n, :]), src, dw_b, ALU.mult))
                mask = (T("causal") if t < TILES - 1 else T("smask")[0:SMP, :])
                go(V.tensor_tensor(gm[0:n, :, 0:n], mb[0:n, 2, 0:256].rearrange("p (g n) -> p g n", g=2)[:, :, 0:n],
                                   mask.unsqueeze(1).to_broadcast([n, GROUPS, n]), ALU.mult), s_xdt, t + 1)
                wait(s_exp, t + 1)
                if 0 < t < TILES - 1:
                    for g in range(GROUPS):
                        ins = V.tensor_tensor(cdec_t[:, 8 * g:8 * g + 8, :], cdec_t[:, 8 * g:8 * g + 8, :],
                                              xbc[:, 10 + g, cols(t)].unsqueeze(1).to_broadcast([P, 8, CH]), ALU.mult)
                        if g == 0:
                            go(ins)
                        else:
                            go(ins, s_ec, t)
                settle()
                for g in range(GROUPS):
                    m = decay[0:n, t % 2, 8 * g:8 * g + 8, 0:n]
                    ins = V.tensor_tensor(m, m, gm[0:n, g, 0:n].unsqueeze(1).to_broadcast([n, 8, n]), ALU.mult)
                    if g == 0:
                        go(ins)
                    else:
                        go(ins, s_M, t + 1)

            def ssd_2(t):
                n = rows(t)
                if t < TILES - 1:
                    wait(s_S, t + 1)
                    st = mb[:, 0:2, :].rearrange("p a n -> p (a n)")
                    if t == 0:
                        settle()
                        go(V.tensor_copy(hT[:, :], st), s_h, 1)
                    else:
                        wait(s_Y, t + 1)
                        settle()
                        go(V.tensor_tensor(heads(hT[:, :]), heads(hT[:, :]),
                                           el[:, :].unsqueeze(2).to_broadcast([P, HEADS, HD]), ALU.mult))
                        settle()
                        go(V.tensor_tensor(hT[:, :], hT[:, :], st, ALU.add), s_h, t + 1)
                    settle()
                wait(s_Y, t + 1)
                for j in range(PAIRS):
                    if t < TILES - 1:
                        src = mb[:, 2 + j // 4, (j % 4) * P:(j % 4) * P + n]
                    else:
                        src = mb[:, 2, j * SMP:(j + 1) * SMP]
                    y = xbc[:, j, cols(t)]
                    ins = V.scalar_tensor_tensor(out=y, in0=y, scalar=v_(V_DS + j), in1=src, op0=ALU.mult,
                                                 op1=ALU.add)
                    if j < PAIRS - 1:
                        go(ins)
                    else:
                        go(ins, s_y, t + 1)

            def ssd_b_seq(b):
                if b >= 2:
                    wait(hs_S, 2 * (b - 1))
                if b == 0:
                    wait(s_bt, TILES)
                settle()
                go(V.tensor_scalar(bseq[0:SMP, b % 2, :, :], btok[0:SMP, :, :], T("bmask")[0:SMP, b:b + 1], None,
                                   ALU.mult), b_seq, b + 1)

            def ssd_state(b):
                h = h0[b % 4]
                wait(hs_I, b + 1)
                if b == 0:
                    wait(s_exp, TILES)
                settle()
                go(V.tensor_tensor(heads(h[:, :]), heads(h[:, :]),
                                   els[:, :, b:b + 1].to_broadcast([P, HEADS, HD]), ALU.mult))
                settle()
                for g in range(GROUPS):
                    i = 2 * b + g
                    wait(hs_S, i + 1)
                    c = slice(g * 512, (g + 1) * 512)
                    go(V.tensor_tensor(h[:, c], h[:, c], mb[:, i % 3, :], ALU.add), hs_n, i + 1)

            def ret_1(t):
                n = rows(t)
                wait(rT, t + 1)
                if t == 0:
                    wait(hs_n, 2 * NB)
                    settle()
                    wait(r_zero, 1)
                dm = T("dmask") if t < TILES - 1 else T("sdmask")[0:SMP, :]
                ed = T("edec") if t < TILES - 1 else T("sedec")[0:SMP, :]
                settle()
                go(V.tensor_tensor(pmat[0:n, :, :, 0:n], mb[0:n, 0:2, :].rearrange("p e (j n) -> p e j n", n=P)[:, :, :, 0:n],
                                   dm.rearrange("p (e j n) -> p e j n", e=2, j=RP), ALU.mult))
                go(V.tensor_tensor(heads(kw[0:n, :], RH), heads(mb[0:n, 2, :], RH),
                                   ed.unsqueeze(2).to_broadcast([n, RH, HD]), ALU.mult))
                settle()
                if t < TILES - 1:
                    go(V.tensor_tensor(qd[:, :, :], qk[:, 0:RP, cols(t)], T("inner").rearrange("p (j n) -> p j n", j=RP),
                                       ALU.mult), r_P, t + 1)
                else:
                    for j in range(RP):
                        ins = V.tensor_tensor(qd[:, j, 0:SMP].rearrange("p (b k) -> p b k", b=NB),
                                              qk[:, j, SEQ:].rearrange("p (b k) -> p b k", b=NB),
                                              T("sinner")[:, j * NT:(j + 1) * NT].unsqueeze(1).to_broadcast([P, NB, NT]),
                                              ALU.mult)
                        if j < RP - 1:
                            go(ins)
                        else:
                            go(ins, r_P, t + 1)

            def diag(ap, e):
                r = slice(e * HD, (e + 1) * HD)
                return ap[r, :, e * HD:(e + 1) * HD]

            def ret_2(t):
                n = rows(t)
                wait(r_Y, t + 1)
                settle()
                go(V.tensor_copy(qk[:, 0:RP, cols(t)], mb[:, 0, :].rearrange("p (j n) -> p j n", n=P)[:, :, 0:n]),
                   r_y, t + 1)
                if t < TILES - 1:
                    wait(r_S, t + 1)
                    sm = mb[:, 1, :].rearrange("p (j n) -> p j n", j=RP)
                    settle()
                    if t == 0:
                        go(V.tensor_copy(diag(rS, 0), diag(sm, 0)))
                        go(V.tensor_copy(diag(rS, 1), diag(sm, 1)), r_s, 1)
                    else:
                        for e in range(2):
                            r = slice(e * HD, (e + 1) * HD)
                            go(V.tensor_tensor(diag(rS, e), diag(rS, e),
                                               T("cdec")[r, :].unsqueeze(2).to_broadcast([HD, RP, HD]), ALU.mult))
                        settle()
                        go(V.tensor_tensor(diag(rS, 0), diag(rS, 0), diag(sm, 0), ALU.add))
                        go(V.tensor_tensor(diag(rS, 1), diag(rS, 1), diag(sm, 1), ALU.add), r_s, t + 1)

            def ret_k_seq(b):
                if b > 0:
                    wait(rs_S, b)
                settle()
                go(V.tensor_scalar(kwm[0:SMP, :], kw[0:SMP, :], T("bmask")[0:SMP, b:b + 1], None, ALU.mult),
                   r_kwm, b + 1)

            def ret_state(b):
                wait(rs_S, b + 1)
                s, sm = rs0[b % 3], mb[:, 1 + b % 2, :].rearrange("p (j n) -> p j n", j=RP)
                settle()
                for e in range(2):
                    r = slice(e * HD, (e + 1) * HD)
                    go(V.tensor_tensor(diag(s, e), diag(s, e), T("scdec")[r, :].unsqueeze(2).to_broadcast([HD, RP, HD]),
                                       ALU.mult))
                settle()
                go(V.tensor_tensor(diag(s, 0), diag(s, 0), diag(sm, 0), ALU.add))
                go(V.tensor_tensor(diag(s, 1), diag(s, 1), diag(sm, 1), ALU.add), rs_n, b + 1)

            def pool(i):
                wait(evac, U_POOL + i + 1)
                wait(halo_in, CONV_CHUNKS + i + 1)
                if i == 2:
                    wait(hs_I, NB)
                cur, w = halo[:, i % 2, :], 1
                bufs = (cvt[:, 0, :], cvt[:, 1, :])
                while w < WINDOWS[i]:
                    dst = bufs[0]
                    settle()
                    go(V.tensor_tensor(dst[:, 2 * w - 1:PHALO], cur[:, 2 * w - 1:PHALO], cur[:, w - 1:PHALO - w],
                                       ALU.add))
                    cur, w, bufs = dst, 2 * w, bufs[::-1]
                settle()
                go(V.tensor_tensor(cur[:, PB:PB + 16], cur[:, PB:PB + 16], T("cnt")[:, i * 16:(i + 1) * 16], ALU.mult))
                settle()
                raw = halo[:, i % 2, :]
                go(V.scalar_tensor_tensor(out=xbc[:, 8 + i, 0:SEQ], in0=cur[:, PB:PB + SEQ], scalar=1.0 / WINDOWS[i],
                                          in1=raw[:, PB:PB + SEQ], op0=ALU.mult, op1=ALU.subtract))

                def seqs(ap):
                    return ap[:, PB + SEQ:PHALO].rearrange("p (b k) -> p b k", b=NB)[:, :, PB:]

                settle()
                go(V.scalar_tensor_tensor(out=xbc[:, 8 + i, SEQ:].rearrange("p (b k) -> p b k", b=NB), in0=seqs(cur),
                                          scalar=1.0 / WINDOWS[i], in1=seqs(raw), op0=ALU.mult, op1=ALU.subtract),
                   pooled_ok, i + 1)
                settle()
                go(V.tensor_copy(pad[:, 0:1], pad[:, 1:2]), halo_used, CONV_CHUNKS + i + 1)

            def pool_gate(i):
                wait(pool_mm, i + 1)
                settle()
                go(V.scalar_tensor_tensor(out=halves(cvt[:, i % 2, 0:TOK]), in0=acc_of(U_GPOOL + i),
                                          scalar=v_(V_PS + i), in1=halves(tmp[:, i % 2, :]), op0=ALU.mult,
                                          op1=ALU.mult), mix_full, i + 1)
                wait(mix_hi, i + 1)
                settle()
                go(V.tensor_tensor(mix[:, 1, 1, i, :], cvt[:, i % 2, 0:TOK], mix[:, 1, 0, i, :].bitcast(F32),
                                   ALU.subtract), mix_lo, i + 1)

            def ret_out(i):
                q = qk[:, i, :]
                settle()
                go(V.scalar_tensor_tensor(out=q, in0=q, scalar=v_(V_RN + i), in1=rstd[:, :], op0=ALU.mult,
                                          op1=ALU.mult), b_used, GROUPS + i + 1)
                wait(evac, U_GRET + i + 1)
                settle()
                go(V.tensor_tensor(q, q, qk[:, RP + i, :], ALU.mult), mix_full, 4 + i + 1)

            go(V.memset(pad[:, :], 0.0))
            go(V.memset(stk[:, :], 0.0))
            V.memset(eps[:, :], EPS).then_inc(eps_ok, 1)
            settle()
            eng.wait_ge(s_tab, 16)
            eng.wait_ge(s_x, 16)
            for j in range(KT):
                add_square(j)
            wait(n_rstd, 1)
            lane.close()
            next_layer(eng, next_dve)
            with eng.Fori(0, DEPTH):
                split(0)
                split(1)
                wait(s_par, 64)
                settle()
                for j in range(KT + 1):
                    if j < KT:
                        if j >= 2:
                            settle()
                        go(V.scalar_tensor_tensor(out=tmp[:, j % 2, :], in0=x[:, j, :], scalar=v_(V_NW + j),
                                                  in1=rstd[:, :], op0=ALU.mult, op1=ALU.mult), h_full, j + 1)
                    if j > 0:
                        wait(h_hi, j)
                        settle()
                        go(V.tensor_tensor(hin[:, 1, j - 1, :], tmp[:, (j - 1) % 2, :],
                                           hin[:, 0, j - 1, :].bitcast(F32), ALU.subtract), h_lo, j)
                for u in range(UNITS):
                    if u + 2 < UNITS:
                        split(u + 2)
                    if u == U_DT:
                        dt_chain()
                    if u == S_STK:
                        wait(stk_T, 1)
                        settle()
                        go(V.tensor_copy(tokv[:, 0:4, :], mb[:, 0, 0:384].rearrange("p (t n) -> p t n", t=4)))
                        go(V.tensor_copy(tokv[0:SMP, 4, :], mb[0:SMP, 1, 0:96]), tokv_ok, 1)
                    if U_CONV <= u < U_Q:
                        conv(u - U_CONV)
                    if U_Q <= u < U_V:
                        if u == U_Q:
                            wait(xbc_ok, CONV_CHUNKS)
                            segments(0)
                        rotate(u - U_Q)
                    if S_SSD <= u < S_SST:
                        t = (u - S_SSD) // 2
                        (ssd_1 if (u - S_SSD) % 2 == 0 else ssd_2)(t)
                        if (u - S_SSD) % 2 == 1 and t + 1 < TILES:
                            segments(t + 1)
                    if S_SST <= u < S_SSE:
                        for b in (2 * (u - S_SST), 2 * (u - S_SST) + 1):
                            ssd_b_seq(b)
                            ssd_state(b)
                    if u == S_SSE:
                        wait(hs_I, NB)
                        wait(ecs_ok, 1)
                        settle()
                        go(V.tensor_tensor(ecs[:, :, :], ecs[:, :, :], mb[:, 3, :].rearrange("p (j n) -> p j n", j=PAIRS),
                                           ALU.mult))
                        settle()
                        go(V.tensor_tensor(xbc[:, 0:8, SEQ:], xbc[:, 0:8, SEQ:], ecs[:, :, :], ALU.add), hs_y, 1)
                    if U_POOL <= u < U_GPOOL:
                        pool(u - U_POOL)
                    if S_RET <= u < S_RST:
                        t = (u - S_RET) // 2
                        (ret_1 if (u - S_RET) % 2 == 0 else ret_2)(t)
                    if S_RST <= u < S_NORM:
                        for b in (2 * (u - S_RST), 2 * (u - S_RST) + 1):
                            ret_k_seq(b)
                            ret_state(b)
                    if U_GPOOL + 1 <= u < U_GPOOL + 5:
                        pool_gate(u - U_GPOOL - 1)
                    if U_Z <= u < U_GRET:
                        i = u - U_Z
                        wait(evac, u + 1)
                        settle()
                        go(V.tensor_tensor(xbc[:, i, :], xbc[:, i, :], tmp[:, i % 2, :], ALU.mult), g_z_used, i + 1)
                    if u == S_NORM:
                        settle()
                        go(V.tensor_tensor(qk[:, 0:RP, SEQ:], qk[:, 0:RP, SEQ:],
                                           mb[:, 3, 0:RP * SMP].rearrange("p (j n) -> p j n", j=RP), ALU.add),
                           rs_y, 1)
                        for i in range(GROUPS):
                            for j in range(4 * i, 4 * i + 4):
                                wait(b_sq, j + 1)
                                if j == 4:
                                    wait(b_sum, 1)
                                settle()
                                if j % 4 == 0:
                                    go(V.tensor_copy(ssq[:, :], tmp[:, j % 2, :]), b_add, j + 1)
                                else:
                                    go(V.tensor_tensor(ssq[:, :], ssq[:, :], tmp[:, j % 2, :], ALU.add), b_add, j + 1)
                            wait(b_rstd, i + 1)
                            for j in range(4 * i, 4 * i + 4):
                                y = xbc[:, j, :]
                                settle()
                                go(V.scalar_tensor_tensor(out=y, in0=y, scalar=v_(V_SN + j), in1=rstd[:, :],
                                                          op0=ALU.mult, op1=ALU.mult), y_full, j + 1)
                            settle()
                            go(V.tensor_copy(pad[:, 0:1], pad[:, 1:2]), b_used, i + 1)
                    if u == S_NORM + 1:
                        for i in range(RP):
                            wait(b_rstd, GROUPS + i + 1)
                            ret_out(i)
                        for i in range(RP):
                            wait(mix_hi, 4 + i + 1)
                            settle()
                            go(V.tensor_tensor(mix[:, 0, 1, i, :], qk[:, i, :], mix[:, 0, 0, i, :].bitcast(F32),
                                               ALU.subtract), mix_lo, 4 + i + 1)
                    if u == U_OUT - 1:
                        for j in range(PAIRS):
                            wait(y_hi, j + 1)
                            settle()
                            go(V.tensor_tensor(hin[:, 1, j, :], xbc[:, j, :], hin[:, 0, j, :].bitcast(F32),
                                               ALU.subtract), y_lo, j + 1)
                    o = u - U_OUT
                    if o >= 0 and o % 4 >= 2:
                        m = 2 * (o // 4) + o % 2
                        wait(proj, u + 1)
                        if m == 0:
                            wait(x_back, 16)
                        settle()
                        go(V.tensor_tensor(halves(x[:, m, :]), halves(x[:, m, :]), acc_of(u), ALU.add),
                           x_new, m + 1)
                        add_square(m)
                wait(n_rstd, 1)
                lane.close()
                next_layer(eng, next_dve)
            for j in range(KT):
                V.scalar_tensor_tensor(out=x[:, j, :], in0=x[:, j, :], scalar=T("fnw")[:, j:j + 1], in1=rstd[:, :],
                                       op0=ALU.mult, op1=ALU.mult).then_inc(f_ok, 1)

        @block.gpsimd
        def _(eng):
            lane = Lane(eng, chain_p)
            go, settle, wait = lane.go, lane.settle, lane.wait
            G = nc.gpsimd

            def fill(i):
                conv_ = i < CONV_CHUNKS
                w, end = (3, HALO) if conv_ else (PB, PHALO)
                st = cst[:, CONV_ORDER[i], :, :] if conv_ else pst[:, i - CONV_CHUNKS, :, :]
                hb = halo[:, i % 2, 0:end]
                settle()
                go(G.memset(hb[:, 0:w], 0.0))
                settle()
                go(G.tensor_copy(hb[:, w + SEQ:].rearrange("p (b n) -> p b n", b=NB)[:, :, 0:w], st),
                   halo_in, i + 1)

            def save(i):
                conv_ = i < CONV_CHUNKS
                u = U_CONV + i if conv_ else U_POOL + i - CONV_CHUNKS
                w, end = (3, HALO) if conv_ else (PB, PHALO)
                to = cso[:, CONV_ORDER[i], :, :] if conv_ else pso[:, i - CONV_CHUNKS, :, :]
                hb = halo[:, i % 2, 0:end]
                wait(evac, u + 1)
                settle()
                go(G.tensor_copy(to[:, 0, :], hb[:, SEQ:w + SEQ]))
                go(G.tensor_copy(to[:, 1:, :], hb[:, w + SEQ:].rearrange("p (b n) -> p b n", b=NB)[:, :, NT:]))
                wait(halo_used, i + 1)

            def spread(t):
                s = cum_in[t % 2]
                if t >= 2:
                    wait(s_Y, t - 1)
                if t < TILES - 1:
                    src = a["cum"][0:HEADS * SEQ].rearrange("(t n) -> t n", t=4)[t:t + 1, :]
                    eng.dma_start(decay[:, t % 2, :, :].rearrange("p h n -> p (h n)"), src.to_broadcast([P, HEADS * CH])).then_inc(s, 16)
                else:
                    src = a["cum"][HEADS * SEQ:].rearrange("(o h n) -> o h n", o=1, h=HEADS)
                    eng.dma_start(decay[:, t % 2, :, 0:SMP], src.to_broadcast([P, HEADS, SMP])).then_inc(s, 16)

            clear_signals(eng)
            with eng.Fori(0, DEPTH) as l:
                eng.dma_start(a["x_kept"], x[:, :, :]).then_inc(x_out, 16)
                wait(s_st, 32)
                fill(0)
                fill(1)
                for u in range(U_OUT):
                    if u == U_DT + 1:
                        wait(cum_ok, 1)
                        eng.dma_start(a["cum"][0:HEADS * SEQ].rearrange("(t h n) -> h t n", t=4, h=HEADS),
                                      dt_u[:, 0:SEQ].rearrange("h (t n) -> h t n", t=4)).then_inc(cum_out, 16)
                        eng.dma_start(a["cum"][HEADS * SEQ:].rearrange("(h n) -> h n", h=HEADS),
                                      dt_u[:, SEQ:]).then_inc(cum_out, 16)
                        wait(cum_out, 32)
                        spread(0)
                        spread(1)
                        rows_ = a["cum"][HEADS * SEQ:].rearrange("(j e n) -> e j n", e=2, n=SMP)
                        for e in range(2):
                            eng.dma_start(ecs[e * HD:(e + 1) * HD, :, :], rows_[e:e + 1].to_broadcast([HD, PAIRS, SMP]))\
                               .then_inc(ecs_in, 16)
                    if U_CONV <= u < U_Q:
                        i = u - U_CONV
                        save(i)
                        fill(i + 2)
                    if U_POOL <= u < U_GPOOL:
                        i = CONV_CHUNKS + u - U_POOL
                        save(i)
                        if i + 2 < 16:
                            fill(i + 2)
                    if S_SSD <= u < S_SST and (u - S_SSD) % 2 == 1:
                        t = (u - S_SSD) // 2
                        if t + 2 < TILES:
                            spread(t + 2)
                        if t == TILES - 2:
                            wait(s_h, TILES - 1)
                            eng.dma_start(a["ssm_p"][l], hT[:, :]).then_inc(hp_out, 16)
                            wait(s_Y, TILES - 1)
                            for b in range(4):
                                eng.dma_start(h0[b][:, :], a["ssm0"][l, b]).then_inc(h0_in[b], 16)
                    if S_SST <= u < S_SSE:
                        for b in (2 * (u - S_SST), 2 * (u - S_SST) + 1):
                            wait(hs_n, 2 * b + 2)
                            eng.dma_start(a["ssm_s"][l, b], h0[b % 4][:, :]).then_inc(h0_out[b % 4], 16)
                        for b in (2 * (u - S_SST), 2 * (u - S_SST) + 1):
                            if b + 4 < NB:
                                wait(h0_out[b % 4], 16 * (b // 4 + 1))
                                eng.dma_start(h0[b % 4][:, :], a["ssm0"][l, b + 4]).then_inc(h0_in[b % 4], 16)
                    if u == S_SSE - 1:
                        wait(hs_n, 2 * NB)
                        wait(hp_out, 16)
                        for b in range(4):
                            wait(h0_out[b], 32)
                        settle()
                        for i in range(3):
                            go(G.memset(rs0[i][:, :, :], 0.0))
                        go(G.memset(rS[:, :, :], 0.0), r_zero, 1)
                        settle()
                        for b in range(3):
                            for e in range(2):
                                r = slice(e * HD, (e + 1) * HD)
                                eng.dma_start(rs0[b][r, :, e * HD:(e + 1) * HD], a["ret0"][l, b, r]).then_inc(r0_in[b], 16)
                    if u == S_RST:
                        wait(r_s, TILES - 1)
                        for e in range(2):
                            r = slice(e * HD, (e + 1) * HD)
                            eng.dma_start(a["ret_p"][l, r], rS[r, :, e * HD:(e + 1) * HD]).then_inc(rp_out, 16)
                    if S_RST <= u < S_NORM:
                        for b in (2 * (u - S_RST), 2 * (u - S_RST) + 1):
                            wait(rs_n, b + 1)
                            for e in range(2):
                                r = slice(e * HD, (e + 1) * HD)
                                eng.dma_start(a["ret_s"][l, b, r], rs0[b % 3][r, :, e * HD:(e + 1) * HD])\
                                   .then_inc(r0_out[b % 3], 16)
                            if b + 3 < NB:
                                wait(r0_out[b % 3], 32 * (b // 3 + 1))
                                for e in range(2):
                                    r = slice(e * HD, (e + 1) * HD)
                                    eng.dma_start(rs0[b % 3][r, :, e * HD:(e + 1) * HD], a["ret0"][l, b + 3, r])\
                                       .then_inc(r0_in[b % 3], 16)
                wait(rp_out, 32)
                for b in range(3):
                    wait(r0_out[b], 32 * len(range(b, NB, 3)))
                settle()
                go(G.memset(pool_pad[:, :], 0.0), ret_free, 1)
                wait(mix_lo, 8)
                wait(x_out, 16)
                eng.dma_start(x[:, :, :], a["x_kept"]).then_inc(x_back, 16)
                eng.dma_start(a["conv_o"][l], cso[:, :, :, :]).then_inc(states_out, 16)
                eng.dma_start(a["pool_o"][l], pso[:, :, :, :]).then_inc(states_out, 16)
                wait(states_out, 32)
                wait(halo_used, 16)
                lane.close()
                clear_signals(eng)
            for j in range(KT):
                eng.wait_ge(f_ok, j + 1)
                eng.dma_start(a["y"][:, j, :], x[:, j, :]).then_inc(f_out, 16)
            eng.wait_ge(f_out, 16 * KT)


def rot_order():
    return np.array([16 * (r // 32) + r % 32 if r % 32 < 16 else 32 + 16 * (r // 32) + r % 32 - 16
                     for r in range(HD)])


def tables():
    f = np.float32
    t = np.zeros((P, TAB_N), f)

    def put(name, v):
        o, w = TAB[name]
        v = np.asarray(v, f).reshape(v.shape[0], w)
        t[:v.shape[0], o:o + w] = v

    i = np.arange(P)
    put("ident", np.eye(P))
    put("ones", np.ones((P, P)))
    put("blk", (i[:, None] // HD == i[None, :] // HD) * 1.0)
    put("causal", (i[None, :] >= i[:, None]) * 1.0)
    s = np.arange(SMP)
    same = s[:, None] // NT == s[None, :] // NT
    ok = same & (s[None, :] >= s[:, None])
    put("smask", ok * 1.0)
    put("bmask", (s[:, None] // NT == np.arange(NB)[None, :]) * 1.0)
    pos = np.concatenate([np.arange(SEQ), PAST + s % NT]).astype(f)
    half = HD // 2
    inv = (10000.0 ** (-np.arange(half) / half)).astype(f)
    o = np.tile(rot_order(), 2)
    ang = (pos[None, :] * inv[o % half][:, None]).astype(f)
    put("cos", np.cos(ang.astype(np.float64)))
    put("sin", np.sin(ang.astype(np.float64)) * np.where(o < half, -1.0, 1.0)[:, None])
    lg = np.log1p(-np.exp2(-5.0 - np.arange(RH, dtype=f))).astype(f)
    pair = np.arange(RH).reshape(RP, 2).T.reshape(-1)

    def decay(n, mask, rel):
        d = np.exp((np.maximum(rel, 0).astype(f)[:, None, :] * lg[pair][None, :, None]).astype(f))
        return np.where(mask[:, None, :], d, 0.0)

    put("dmask", decay(P, i[None, :] >= i[:, None], i[None, :] - i[:, None]))
    put("sdmask", decay(SMP, ok, s[None, :] - s[:, None]))
    head = 2 * np.arange(RP)[None, :] + i[:, None] // HD
    put("inner", np.exp(((i + 1).astype(f)[None, None, :] * lg[head][:, :, None]).astype(f)))
    put("sinner", np.exp(((np.arange(NT) + 1).astype(f)[None, None, :] * lg[head][:, :, None]).astype(f)))
    put("edec", np.exp(((CH - 1 - i).astype(f)[:, None] * lg[None, :]).astype(f)))
    put("sedec", np.exp(((NT - 1 - s % NT).astype(f)[:, None] * lg[None, :]).astype(f)))
    put("cdec", np.exp((f(CH) * lg[head]).astype(f)))
    put("scdec", np.exp((f(NT) * lg[head]).astype(f)))
    k = np.arange(16)
    put("cnt", np.tile(np.concatenate([w / np.minimum(k + 1.0, w) for w in WINDOWS])[None, :], (P, 1)))
    return t


def resets():
    col = np.arange(TOK)
    start = np.where(col < SEQ, col % CH == 0, (col - SEQ) % NT == 0)
    return np.tile(np.where(start, 0.0, 1.0)[None, :], (HEADS, 1)).astype(np.float32)


_OUTS = {
    "y": (P, KT, TOK), "ssm_p": (DEPTH, P, HEADS * HD), "ssm_s": (DEPTH, NB, P, HEADS * HD),
    "conv_o": (DEPTH, P, CONV_CHUNKS, 1 + NB, 3), "pool_o": (DEPTH, P, 4, 1 + NB, PB),
    "ret_p": (DEPTH, P, RP, HD), "ret_s": (DEPTH, NB, P, RP, HD),
}


def lay_out(v):
    v = {k: np.asarray(q) for k, q in v.items()}
    rot = (np.arange(RH)[:, None] * HD + rot_order()[None, :]).reshape(-1)
    w_in, w_out = v["w_in"], v["w_out"]
    z, c, dt, q, k, vv, gr, u, gp, end = np.cumsum([0, 1024, 1536, HEADS, 512, 512, 512, 512, 512, 512])
    cc = w_in[:, :, c:dt].reshape(DEPTH, D_MODEL, CONV_CHUNKS, P)[:, :, list(CONV_ORDER)]
    w = np.concatenate([w_in[:, :, dt:q], np.zeros((DEPTH, D_MODEL, P - HEADS), w_in.dtype),
                        cc.reshape(DEPTH, D_MODEL, -1), w_in[:, :, q:k][:, :, rot], w_in[:, :, k:vv][:, :, rot],
                        w_in[:, :, vv:gr], w_in[:, :, u:gp], w_in[:, :, gp:end], w_in[:, :, z:c],
                        w_in[:, :, gr:u]], axis=2)
    w = w.reshape(DEPTH, KT, P, U_OUT, P).transpose(0, 3, 2, 1, 4)
    wo = w_out.reshape(DEPTH, 2, KT, P, OUT_CHUNKS, P)
    wo = [wo[:, 1 - (o % 4) // 2, :, :, 2 * (o // 4) + o % 2].transpose(0, 2, 1, 3) for o in range(2 * OUT_CHUNKS)]
    w = np.concatenate([w, np.stack(wo, axis=1)], axis=1)

    def on_parts(a):
        return a.reshape(DEPTH, -1, P).transpose(0, 2, 1)

    cw = v["conv_w"].reshape(DEPTH, CW, CONV_CHUNKS, P).transpose(0, 3, 2, 1).reshape(DEPTH, P, -1)
    vec = np.concatenate([on_parts(v["norm_w"]), cw, on_parts(v["conv_b"]),
                          on_parts(np.repeat(v["d_skip"], HD, axis=1)), on_parts(v["ssd_norm_w"]),
                          on_parts(v["ret_norm_w"]), on_parts(v["pool_scale"])], axis=2)
    x = np.concatenate([v["x_prompt"].reshape(SEQ, D_MODEL), v["x_sample"].reshape(SMP, D_MODEL)])
    tab = tables()
    o, n = TAB["fnw"]
    tab[:, o:o + n] = v["final_norm_w"].reshape(KT, P).T
    ret = v["state_ret"][:, :, :, rot_order(), :].reshape(DEPTH, NB, RP, 2, HD, HD)
    return {
        "x": x.T.reshape(KT, P, TOK).transpose(1, 0, 2), "tab": tab, "reset": resets(), "w": w, "vec": vec,
        "hvec": np.stack([v["dt_bias"], v["a_log"]], axis=2), "pw": v["pool_w"].transpose(0, 2, 1, 3),
        "cst": v["state_conv"].reshape(DEPTH, NB, 3, CONV_CHUNKS, P).transpose(0, 4, 3, 1, 2),
        "pst": v["state_pool"].reshape(DEPTH, NB, PB, 4, P).transpose(0, 4, 3, 1, 2),
        "ssm0": v["state_ssm"].reshape(DEPTH, NB, HEADS * HD, P).transpose(0, 1, 3, 2),
        "ret0": ret.transpose(0, 1, 3, 4, 2, 5).reshape(DEPTH, NB, P, RP, HD),
    }


def taken(r):
    y = r["y"].transpose(1, 0, 2).reshape(D_MODEL, TOK).T
    back = np.argsort(rot_order())

    def ssm(a, n):
        return a.reshape(DEPTH, n, P, HEADS * HD).transpose(0, 1, 3, 2).reshape(DEPTH, n, HEADS, HD, P)

    def ret(a, n):
        a = a.reshape(DEPTH, n, 2, HD, RP, HD).transpose(0, 1, 4, 2, 3, 5).reshape(DEPTH, n, RH, HD, HD)
        return a[:, :, :, back, :]

    def small(a, w):
        return a.transpose(0, 3, 4, 2, 1).reshape(DEPTH, 1 + NB, w, -1)

    conv, pool = small(r["conv_o"], 3), small(r["pool_o"], PB)
    c = np.ascontiguousarray
    return (c(y[:SEQ]).reshape(1, SEQ, D_MODEL), c(y[SEQ:]).reshape(NB, NT, D_MODEL),
            c(ssm(r["ssm_p"], 1)), c(conv[:, :1]), c(ret(r["ret_p"], 1)), c(pool[:, :1]),
            c(ssm(r["ssm_s"], NB)), c(conv[:, 1:]), c(ret(r["ret_s"], NB)), c(pool[:, 1:]))


def program(bacc, arrays):
    nc = bacc.Bacc("TRN2", target_bir_lowering=False, num_devices=1)
    a = {k: nc.dram_tensor(f"in_{k}", q.shape, F32, kind="ExternalInput").ap() for k, q in arrays.items()}
    for k, shape in _OUTS.items():
        a[k] = nc.dram_tensor(f"out_{k}", shape, F32, kind="ExternalOutput").ap()
    a["cum"] = nc.dram_tensor("cum_rows", (HEADS * TOK,), F32, kind="Internal").ap()
    a["x_kept"] = nc.dram_tensor("x_kept", (P, KT, TOK), F32, kind="Internal").ap()
    trunk(nc, a)
    return nc


def kernel(**inputs):
    import concourse.bacc as _bacc
    from concourse.bass_utils import run_bass_kernel_spmd as _run

    arrays = {k: np.ascontiguousarray(q) for k, q in lay_out(inputs).items()}
    nc = program(_bacc, arrays)
    r = _run(nc, [{f"in_{k}": q for k, q in arrays.items()}], core_ids=[0])
    return taken({k: r.results[0][f"out_{k}"] for k in _OUTS})
```

```python
from contextlib import ExitStack

import numpy as np

import concourse.bass as bass
from concourse import mybir

F32 = mybir.dt.float32
F32R = mybir.dt.float32r
ALU = mybir.AluOpType
ACT = mybir.ActivationFunctionType

P = 128
DEPTH = 2
D_MODEL = 1024
SEQ = 512
NB, NT = 8, 8
SMP = NB * NT
TOK = SEQ + SMP
HALF = TOK // 2
KT = D_MODEL // P
HEADS = 16
HD = 64
PAIRS = HEADS // 2
GROUPS = 2
CH = 128
TILES = SEQ // CH + 1
RH = 8
RP = RH // 2
CW = 4
CONV_CHUNKS = 12
WINDOWS = (2, 4, 8, 16)
PB = 15
PAST = 4096
EPS = 1e-6

U_DT = 0
U_Q = 1
U_K = U_Q + RP
U_V = U_K + RP
U_CONV = U_V + RP
U_POOL = U_CONV + CONV_CHUNKS
U_GPOOL = U_POOL + 4
U_GRET = U_GPOOL + 4
U_Z = U_GRET + RP
U_OUT = U_Z + PAIRS
OUT_CHUNKS = D_MODEL // P
UNITS = U_OUT + 2 * OUT_CHUNKS
CONV_ORDER = (8, 9, 10, 11, 0, 1, 2, 3, 4, 5, 6, 7)
RAW = 2

S_STK = U_CONV - 1
S_RET = U_CONV
S_RST = S_RET + 2 * TILES
S_SSD = S_RST + NB // 2
S_SST = S_SSD + 2 * TILES
S_GATE = S_SST + NB // 2
S_RN = S_GATE - 1
S_PL = S_GATE + 1
S_RL = S_GATE + 2
S_NORM = U_OUT
POOL_SLOTS = (U_POOL, U_POOL + 1, S_SSD + 2, S_SSD + 4)
R0 = 7
assert S_RL + 1 < U_OUT and S_SST >= U_Z and S_GATE + PAIRS // 2 <= U_OUT

HALO = 3 + SEQ + NB * (3 + NT)
CVO = HALO - 3
PHALO = PB + SEQ + NB * (PB + NT)

V_NW, V_CW, V_CB = 0, 8, 8 + 48
V_DS = V_CB + 12
V_SN = V_DS + 8
V_RN = V_SN + 8
V_PS = V_RN + 4
V_N = V_PS + 4


def table_places():
    at, n = {}, 0
    for name, w in (("ident", P), ("blk", P), ("causal", P), ("smask", SMP), ("bmask", NB),
                    ("cos", TOK), ("sin", TOK), ("dmask", RH * CH), ("sdmask", RH * SMP),
                    ("inner", RP * CH), ("sinner", RP * NT), ("edec", RH), ("sedec", RH),
                    ("cdec", RP), ("scdec", RP), ("cnt", 4 * 16), ("fnw", KT)):
        at[name] = (n, w)
        n += w
    return at, n


TAB, TAB_N = table_places()


class Lane:

    def __init__(self, eng, chain):
        self.eng, self.chain, self.n, self.last = eng, chain, 0, None

    def go(self, ins, signal=None, n=None):
        if signal is None:
            self.n += 1
            signal, n = self.chain, self.n
        ins.then_inc(signal, 1)
        self.last = (signal, n)

    def settle(self):
        if self.last is not None:
            self.eng.wait_ge(*self.last)
            self.last = None

    def wait(self, signal, n):
        self.eng.wait_ge(signal, n)

    def close(self):
        self.settle()
        if self.n:
            self.eng.wait_ge(self.chain, self.n)
        self.n = 0


def trunk(nc: bass.Bass, a):
    with ExitStack() as ctx:
        top = [(nc.sbuf_base + 63) // 64 * 64]

        def place(name, shape, dt=F32, at=None):
            size = 4
            for d in shape[1:]:
                size *= d
            off = top[0] if at is None else at
            t = nc.alloc_sbuf_tensor_at(name, shape, dt, offset=off)
            if at is None:
                top[0] = off + (size + 31) // 32 * 32
                assert top[0] <= nc.sbuf_usable_end, (name, top[0] - nc.sbuf_usable_end)
            return t

        def sem(name):
            return ctx.enter_context(nc.semaphore(name))

        hin = place("hin", [P, 2, KT, TOK], F32R)
        w_raw = place("w_raw", [P, RAW, KT, P])
        w_hi = place("w_hi", [P, 2, KT, P], F32R)
        w_lo = place("w_lo", [P, 2, KT, P], F32R)
        work = top[0]
        mix = place("mix", [P, 2, 2, 4, TOK], F32R)
        decay = place("decay", [P, 2, HEADS, CH], at=work)
        cdec_t = place("c_decayed", [P, HEADS, CH], at=work + 4 * 4096)
        xdt = place("xdt", [P, HEADS * HD], at=work + 4 * 6144)
        xdw = place("xdt_to_end", [P, HEADS * HD], at=work + 4 * 7168)
        hT = place("ssm_state", [P, HEADS * HD], at=work + 4 * 8192)
        h0 = [place(f"h0_{i}", [P, HEADS * HD], at=work + 4 * (2048 + 1024 * i)) for i in range(4)]
        rw = work + 4 * 4608
        rs0 = [place(f"ret0_{i}", [P, RP, P], at=rw + 4 * 512 * i if i < 3 else work + 4 * (2048 + 512 * (i - 3)))
               for i in range(R0)]
        pmat = place("ret_probs", [P, 2, RP, CH], at=rw + 4 * 1536)
        kw = place("k_to_end", [P, RP * P], at=rw + 4 * 2560)
        kwm = [place("k_to_end_seq_0", [P, RP * P], at=work + 4 * 4096),
               place("k_to_end_seq_1", [P, RP * P], at=rw + 4 * 3072)]
        qd = place("q_decayed", [P, RP, CH], at=rw + 4 * 3584)
        rS = place("ret_state", [P, RP, P], at=rw + 4 * 4096)
        xbc = place("xbc", [P, CONV_CHUNKS, TOK])
        qk_at = top[0]
        qk = place("qk", [P, 2 * RP, TOK])
        x = place("x", [P, KT, TOK], at=qk_at)
        vT = place("vT", [P, RP, TOK])
        halo = place("halo", [P, 2, PHALO])
        cvt = place("conv_out", [P, 2, PHALO])
        tmp = place("tmp", [P, 2, TOK])
        ssq = place("ssq", [P, TOK])
        rstd = place("rstd", [P, TOK])
        tab = place("tab", [P, TAB_N])
        vec = place("vec", [P, V_N])
        hvec = place("head_vec", [HEADS, 2])
        pw = place("pool_w", [P, 4, P])
        cst = place("conv_state", [P, CONV_CHUNKS, NB, 3])
        cso = place("conv_state_out", [P, CONV_CHUNKS, 1 + NB, 3])
        pst = place("pool_state", [P, 4, NB, PB])
        pso = place("pool_state_out", [P, 4, 1 + NB, PB])
        stk = place("stacked", [96, TOK])
        tokv = place("token_vecs", [P, TILES, 96])
        gm = place("scores", [P, GROUPS, CH])
        btok = place("b_tok", [P, GROUPS, P])
        bseq = place("b_tok_seq", [P, 2, GROUPS, P])
        el = place("exp_last", [P, HEADS])
        els = place("exp_last_sample", [P, HEADS, NB])
        dt_raw, dt_e, dt_u, dt_l, dt_r, dt_s, dt_v, dt_w, reset = (xbc[0:HEADS, i, :] for i in range(9))
        cum = stk[0:HEADS, :]
        ret_sq = (tmp[:, 0, :], tmp[:, 1, :], xbc[:, 8, :], xbc[:, 9, :])
        rstds = (rstd[:, :], ssq[:, :])
        z_gate = [halo[:, 0, 0:TOK], halo[:, 1, 0:TOK], cvt[:, 0, 0:TOK], cvt[:, 1, 0:TOK]]
        na = place("neg_a", [HEADS, 1])
        ecs = place("exp_cum_sample", [P, PAIRS, SMP])
        vtok = place("v_tok", [P, RP * P])
        pad = place("pad", [P, 2])
        pool_pad = place("pool_pad", [P, 2])
        eps = place("eps", [P, 1])
        ones_ = place("ones", [P, P])
        ones = ones_[:, :]

        acc = ctx.enter_context(nc.psum_tensor("acc", [P, 2, 2, 512], F32))
        mb = ctx.enter_context(nc.psum_tensor("misc", [P, 4, 512], F32))

        def T(name):
            o, w = TAB[name]
            return tab[:, o:o + w]

        ident, blk = T("ident"), T("blk")

        def acc_of(u):
            return acc[:, u % 2, :, 0:HALF]

        def halves(ap):
            return ap.rearrange("p (a n) -> p a n", a=2)

        def cols(t):
            return slice(t * CH, t * CH + (CH if t < TILES - 1 else SMP))

        def rows(t):
            return CH if t < TILES - 1 else SMP

        tab_in = sem("tables_loaded")
        first_in = [sem(f"first_w_loaded_{i}") for i in range(2)]
        vec_in = sem("layer_vectors_loaded")
        s_x = [sem(f"x_loaded_{i}") for i in range(4)]
        s_raw = [sem(f"w_loaded_{i}") for i in range(RAW)]
        s_par = sem("params_loaded")
        s_st = sem("small_states_loaded")
        w_hid = sem("w_high")
        w_split = sem("w_split")
        proj = sem("projected")
        evac = sem("acc_read")
        x_new = sem("x_updated")
        sqd = sem("squared")
        sq_add = sem("squares_added")
        nsum = sem("norm_sum")
        n_rstd = sem("norm_rstd")
        h_full = sem("h_scaled")
        h_hi = sem("h_high")
        h_lo = sem("h_split")
        dt_s1 = sem("dt_exp")
        dt_s2 = sem("dt_one_plus")
        dt_s3 = sem("dt_log")
        cum_ok = sem("cum_ready")
        wl_ok = sem("exp_to_end")
        stk_ok = sem("stacked_ready")
        stk_T = sem("stacked_turned")
        tokv_ok = sem("token_vecs_ready")
        cum_out = sem("cum_stored")
        cum_in = [sem(f"cum_spread_{i}") for i in range(2)]
        ecs_in = sem("cum_rows_spread")
        ecs_ok = sem("exp_cum_rows")
        halo_in = sem("halo_filled")
        halo_used = sem("halo_used")
        xbc_ok = sem("xbc_ready")
        rot = sem("rotated")
        sT = sem("ssd_turned")
        s_xdt = sem("ssd_xdt")
        s_bt = sem("ssd_b_tok")
        s_exp = sem("ssd_exps")
        s_row = sem("ssd_row_exps")
        s_ec = sem("ssd_c_decayed")
        s_M = sem("ssd_weights")
        s_S = sem("ssd_state_sum")
        s_Y = sem("ssd_y_sum")
        s_y = sem("ssd_y_read")
        s_h = sem("ssd_state")
        h0_in = [sem(f"h0_loaded_{i}") for i in range(4)]
        h0_out = [sem(f"h0_stored_{i}") for i in range(4)]
        b_seq = sem("b_tok_seq_ready")
        hs_S = sem("sample_state_sum")
        hs_n = sem("sample_state")
        hs_I = sem("sample_inter")
        hs_y = sem("sample_y")
        hp_out = sem("ssm_state_stored")
        rT = sem("ret_turned")
        r_P = sem("ret_weights")
        r_v = sem("ret_v_tok")
        r_Y = sem("ret_y_sum")
        r_S = sem("ret_state_sum")
        r_y = sem("ret_y_read")
        r_s = sem("ret_state_new")
        r0_in = [sem(f"ret0_loaded_{i}") for i in range(R0)]
        r0_out = [sem(f"ret0_stored_{i}") for i in range(R0)]
        r_zero = sem("ret_slots_zeroed")
        r_kwm = sem("k_seq_ready")
        rs_S = sem("sample_ret_sum")
        rs_n = sem("sample_ret")
        rs_y = sem("sample_ret_y")
        rp_out = sem("ret_state_stored")
        pooled_ok = sem("pooled")
        pool_mm = sem("pool_mixed")
        g_z_used = sem("z_gated")
        mix_hi = sem("mix_high")
        mix_lo = sem("mix_split")
        b_sq = sem("branch_squared")
        b_add = sem("branch_squares_added")
        b_sum = sem("branch_norm_sum")
        b_rstd = sem("branch_rstd")
        b_ln = sem("branch_norm_sum_read")
        b_used = sem("branch_rstd_used")
        y_full = sem("ssd_out_full")
        y_hi = sem("ssd_out_high")
        y_lo = sem("ssd_out_split")
        states_out = sem("small_states_stored")
        x_out = sem("x_stored")
        x_back = [sem(f"x_reloaded_{i}") for i in range(4)]
        ret_free = sem("ret_work_free")
        ssd_free = sem("ssd_work_free")
        halo_saved = sem("halo_saved")
        pool_out = sem("pool_gated")
        ret_full = sem("ret_gated")
        eps_ok = sem("eps_set")
        f_out = sem("y_stored")
        f_ok = sem("y_ready")
        chain_v, chain_a, chain_p = sem("vector_order"), sem("scalar_order"), sem("pool_order")
        layer_over = sem("layer_over")
        next_pe, next_act, next_dve, next_sp = (sem(f"next_layer_{e}") for e in ("pe", "act", "dve", "sp"))
        to_clear = range(s_x[0].num, layer_over.num + 1)

        def next_layer(eng, begin):
            eng.sem_inc(layer_over, 1)
            eng.wait_ge(begin, 1)
            eng.sem_clear(begin)

        def clear_signals(pool):
            pool.wait_ge(layer_over, 4)
            pool.dma_reset(to_clear)
            pool.sem_clear(to_clear)
            for begin in (next_pe, next_act, next_dve, next_sp):
                pool.sem_inc(begin, 1)

        block = ctx.enter_context(nc.Block())

        @block.sync
        def _(sp):
            def load_first(l):
                sp.dma_start(vec[:, :], a["vec"][l]).then_inc(vec_in, 16)
                for u in range(2):
                    sp.dma_start(w_raw[:, u, :, :], a["w"][l * UNITS + u]).then_inc(first_in[u], 16)

            def spread(t):
                done = cum_in[t % 2]
                if t >= 2:
                    sp.wait_ge(s_Y, t - 1)
                if t < TILES - 1:
                    src = a["cum"][0:HEADS * SEQ].rearrange("(t n) -> t n", t=4)[t:t + 1, :]
                    sp.dma_start(decay[:, t % 2, :, :].rearrange("p h n -> p (h n)"),
                                 src.to_broadcast([P, HEADS * CH])).then_inc(done, 16)
                else:
                    src = a["cum"][HEADS * SEQ:].rearrange("(o h n) -> o h n", o=1, h=HEADS)
                    sp.dma_start(decay[:, t % 2, :, 0:SMP], src.to_broadcast([P, HEADS, SMP])).then_inc(done, 16)

            def load_ret(l, b):
                for e in range(2):
                    r = slice(e * HD, (e + 1) * HD)
                    sp.dma_start(rs0[b % R0][r, :, e * HD:(e + 1) * HD], a["ret0"][l, b, r]).then_inc(r0_in[b % R0], 16)

            def beside(l, s):
                if s == 0:
                    sp.dma_start(a["x_kept"], x[:, :, :]).then_inc(x_out, 16)
                if s == 1:
                    sp.dma_start(cst[:, :, :, :], a["cst"][l]).then_inc(s_st, 16)
                    sp.dma_start(pst[:, :, :, :], a["pst"][l]).then_inc(s_st, 16)
                    sp.wait_ge(r_zero, 1)
                if 1 <= s <= R0:
                    load_ret(l, s - 1)
                if s == 6:
                    sp.wait_ge(cum_ok, 1)
                    sp.dma_start(a["cum"][0:HEADS * SEQ].rearrange("(t h n) -> h t n", t=4, h=HEADS),
                                 cum[:, 0:SEQ].rearrange("h (t n) -> h t n", t=4)).then_inc(cum_out, 16)
                    sp.dma_start(a["cum"][HEADS * SEQ:].rearrange("(h n) -> h n", h=HEADS),
                                 cum[:, SEQ:]).then_inc(cum_out, 16)
                if s == 7:
                    sp.wait_ge(cum_out, 32)
                    spread(0)
                    by_head = a["cum"][HEADS * SEQ:].rearrange("(j e n) -> e j n", e=2, n=SMP)
                    for e in range(2):
                        sp.dma_start(ecs[e * HD:(e + 1) * HD, :, :], by_head[e:e + 1].to_broadcast([HD, PAIRS, SMP]))\
                          .then_inc(ecs_in, 16)
                if s == S_RST - 1:
                    sp.wait_ge(r_s, TILES - 1)
                    for e in range(2):
                        r = slice(e * HD, (e + 1) * HD)
                        sp.dma_start(a["ret_p"][l, r], rS[r, :, e * HD:(e + 1) * HD]).then_inc(rp_out, 16)
                if S_RST <= s < S_SSD:
                    for b in (2 * (s - S_RST), 2 * (s - S_RST) + 1):
                        sp.wait_ge(rs_n, b + 1)
                        for e in range(2):
                            r = slice(e * HD, (e + 1) * HD)
                            sp.dma_start(a["ret_s"][l, b, r], rs0[b % R0][r, :, e * HD:(e + 1) * HD])\
                              .then_inc(r0_out[b % R0], 16)
                if s == S_RST + 1:
                    for b in range(R0, NB):
                        sp.wait_ge(r0_out[b % R0], 32)
                        load_ret(l, b)
                if s == S_SSD - 1:
                    for b in range(R0):
                        sp.wait_ge(r0_out[b], 32 * len(range(b, NB, R0)))
                    sp.sem_inc(ret_free, 1)
                    spread(1)
                if S_SSD <= s < S_SST and (s - S_SSD) % 2 == 1:
                    t = (s - S_SSD) // 2
                    if t + 2 < TILES:
                        spread(t + 2)
                    if t == TILES - 2:
                        sp.wait_ge(s_h, TILES - 1)
                        sp.dma_start(a["ssm_p"][l], hT[:, :]).then_inc(hp_out, 16)
                        sp.wait_ge(s_Y, TILES - 1)
                        for b in range(4):
                            sp.dma_start(h0[b][:, :], a["ssm0"][l, b]).then_inc(h0_in[b], 16)
                if S_SST <= s < S_GATE:
                    for b in (2 * (s - S_SST), 2 * (s - S_SST) + 1):
                        sp.wait_ge(hs_n, 2 * b + 2)
                        sp.dma_start(a["ssm_s"][l, b], h0[b % 4][:, :]).then_inc(h0_out[b % 4], 16)
                        if b + 4 < NB:
                            sp.wait_ge(h0_out[b % 4], 16 * (b // 4 + 1))
                            sp.dma_start(h0[b % 4][:, :], a["ssm0"][l, b + 4]).then_inc(h0_in[b % 4], 16)
                if s == S_GATE - 1:
                    sp.wait_ge(hp_out, 16)
                    for b in range(4):
                        sp.wait_ge(h0_out[b], 32)
                    sp.sem_inc(ssd_free, 1)
                if s == S_RL:
                    sp.wait_ge(mix_lo, 8)
                    sp.wait_ge(x_out, 16)
                    for i in range(4):
                        sp.dma_start(x[:, 2 * i:2 * i + 2, :], a["x_kept"][:, 2 * i:2 * i + 2, :])\
                          .then_inc(x_back[i], 16)

            for i in range(4):
                sp.dma_start(x[:, 2 * i:2 * i + 2, :], a["x"][:, 2 * i:2 * i + 2, :]).then_inc(s_x[i], 16)
            load_first(0)
            sp.dma_start(tab[:, :], a["tab"]).then_inc(tab_in, 16)
            next_layer(sp, next_sp)
            with sp.Fori(0, DEPTH) as l:
                sp.dma_start(hvec[:, :], a["hvec"][l]).then_inc(s_par, 16)
                sp.dma_start(reset, a["reset"]).then_inc(s_par, 16)
                sp.dma_start(pw[:, :, :], a["pw"][l]).then_inc(s_par, 16)
                for u in range(2, UNITS):
                    sp.wait_ge(w_split, u - RAW + 1)
                    sp.dma_start(w_raw[:, u % RAW, :, :], a["w"][l * UNITS + u]).then_inc(s_raw[u % RAW], 16)
                    if u >= 4:
                        beside(l, u - 4)
                sp.wait_ge(w_split, UNITS)
                load_first(l + 1)
                next_layer(sp, next_sp)
            for u in range(2):
                sp.wait_ge(first_in[u], 16 * (DEPTH + 1))
            sp.wait_ge(vec_in, 16 * (DEPTH + 1))

        @block.tensor
        def _(pe):
            def operands(u, k, c):
                if U_OUT <= u < U_OUT + OUT_CHUNKS:
                    return mix[:, k // 4, 0, k % 4, c], mix[:, k // 4, 1, k % 4, c]
                return hin[:, 0, k, c], hin[:, 1, k, c]

            def products(u, half, k):
                out = acc_of(u)[:, half, :]
                hi, lo = operands(u, k, slice(half * HALF, (half + 1) * HALF))
                wh, wl = w_hi[:, u % 2, k, :], w_lo[:, u % 2, k, :]
                pe.matmul(out, wh, hi, start=k == 0, stop=False)
                pe.matmul(out, wh, lo, start=False, stop=False)
                return pe.matmul(out, wl, hi, start=False, stop=k == KT - 1)

            def project_first():
                pe.wait_ge(w_split, 2)
                for k in range(KT):
                    pe.wait_ge(h_lo, k + 1)
                    for u in range(2):
                        for half in range(2):
                            mm = products(u, half, k)
                        if k == KT - 1:
                            mm.then_inc(proj, 1)

            def project(u, between=None):
                pe.wait_ge(w_split, u + 1)
                o = u - U_OUT
                if o < 2:
                    pe.wait_ge(evac, u - 1)
                else:
                    pe.wait_ge(x_new, o - 1)
                for half in range(2):
                    for k in range(KT):
                        if half == 0 and o == 0:
                            pe.wait_ge(mix_lo, k + 1)
                        if half == 0 and o == OUT_CHUNKS:
                            pe.wait_ge(y_lo, k + 1)
                        mm = products(u, half, k)
                    if half == 0 and between is not None:
                        between()
                mm.then_inc(proj, 1)

            def norm_sum():
                pe.wait_ge(sq_add, KT)
                for half in range(2):
                    mm = pe.matmul(mb[:, 2 + half, 0:HALF], ones, halves(ssq[:, :])[:, half, :], start=True, stop=True)
                mm.then_inc(nsum, 1)

            def ssd_turn(t):
                n = rows(t)
                if t == 0:
                    pe.wait_ge(xbc_ok, CONV_CHUNKS)
                    pe.wait_ge(rs_y, 1)
                    pe.wait_ge(rs_n, NB)
                else:
                    pe.wait_ge(s_h, t)
                    pe.wait_ge(s_y, t)
                for j in range(PAIRS):
                    pe.transpose(mb[0:n, j // 4, (j % 4) * P:(j % 4 + 1) * P], xbc[:, j, cols(t)], ident)
                for g in range(GROUPS):
                    pe.matmul(mb[0:n, 2, g * P:g * P + n], xbc[:, 8 + g, cols(t)], xbc[:, 10 + g, cols(t)],
                              start=True, stop=True)
                for g in range(GROUPS):
                    mm = pe.transpose(mb[0:n, 3, g * P:(g + 1) * P], xbc[:, 8 + g, cols(t)], ident)
                mm.then_inc(sT, 1)

            def ssd_y(t):
                n = rows(t)
                pe.wait_ge(s_xdt, t + 1)
                pe.wait_ge(s_bt, t + 1)
                if t < TILES - 1:
                    for g in range(GROUPS):
                        mm = pe.matmul(mb[:, g, :], btok[:, g, :], xdw[:, g * 512:(g + 1) * 512], start=True, stop=True)
                    mm.then_inc(s_S, 1)
                pe.wait_ge(s_M, t + 1)
                inter = 0 < t < TILES - 1
                if inter:
                    pe.wait_ge(s_ec, t)
                for j in range(PAIRS):
                    if t < TILES - 1:
                        dst = mb[:, 2 + j // 4, (j % 4) * P:(j % 4) * P + n]
                    else:
                        dst = mb[:, 2, j * SMP:(j + 1) * SMP]
                    for e in range(2):
                        h = 2 * j + e
                        r = slice(e * HD, (e + 1) * HD)
                        mm = pe.matmul(dst[r, :], xdt[0:n, h * HD:(h + 1) * HD], decay[0:n, t % 2, h, 0:n],
                                       start=True, stop=not inter)
                        if inter:
                            mm = pe.matmul(dst[r, :], hT[:, h * HD:(h + 1) * HD], cdec_t[:, h, :],
                                           start=False, stop=True)
                mm.then_inc(s_Y, 1)

            def ssd_sample(b):
                c = slice(SEQ + b * NT, SEQ + (b + 1) * NT)
                pe.wait_ge(h0_in[b % 4], 16 * (b // 4 + 1))
                if b == 0:
                    pe.wait_ge(s_y, TILES - 1)
                for j in range(PAIRS):
                    mm = pe.matmul(mb[:, 3, j * SMP + b * NT:j * SMP + (b + 1) * NT], h0[b % 4][:, j * P:(j + 1) * P],
                                   xbc[:, 10 + j // 4, c], start=True, stop=True)
                mm.then_inc(hs_I, 1)
                pe.wait_ge(b_seq, b + 1)
                if b == 0:
                    pe.wait_ge(s_y, TILES)
                for g in range(GROUPS):
                    i = 2 * b + g
                    if i >= 3:
                        pe.wait_ge(hs_n, i - 2)
                    pe.matmul(mb[:, i % 3, :], bseq[0:SMP, b % 2, g, :], xdw[0:SMP, g * 512:(g + 1) * 512],
                              start=True, stop=True).then_inc(hs_S, 1)

            def ret_turn(t):
                n = rows(t)
                if t == 0:
                    pe.wait_ge(rot, 2 * RP)
                    pe.wait_ge(evac, U_CONV)
                    pe.wait_ge(tokv_ok, 1)
                else:
                    pe.wait_ge(r_y, t)
                    pe.wait_ge(r_s, t)
                for j in range(RP):
                    for e in range(2):
                        r = slice(e * HD, (e + 1) * HD)
                        pe.matmul(mb[0:n, e, j * P:j * P + n], qk[r, RP + j, cols(t)], qk[r, j, cols(t)],
                                  start=True, stop=True)
                for j in range(RP):
                    pe.transpose(mb[0:n, 2, j * P:(j + 1) * P], qk[:, RP + j, cols(t)], ident)
                for j in range(RP):
                    mm = pe.transpose(mb[0:n, 3, j * P:(j + 1) * P], vT[:, j, cols(t)], ident)
                mm.then_inc(rT, 1)

            def ret_y(t):
                n = rows(t)
                pe.wait_ge(r_P, t + 1)
                pe.wait_ge(r_v, t + 1)
                inter = 0 < t < TILES - 1
                for j in range(RP):
                    dst = mb[:, 0, j * P:j * P + n]
                    if inter:
                        pe.matmul(dst, rS[:, j, :], qd[:, j, :], start=True, stop=False, skip_group_check=True)
                    for e in range(2):
                        r = slice(e * HD, (e + 1) * HD)
                        c = slice(j * P + e * HD, j * P + (e + 1) * HD)
                        mm = pe.matmul(dst[r, :], vtok[0:n, c], pmat[0:n, e, j, 0:n], start=not inter, stop=True,
                                       skip_group_check=inter)
                mm.then_inc(r_Y, 1)
                if t < TILES - 1:
                    for j in range(RP):
                        c = slice(j * P, (j + 1) * P)
                        mm = pe.matmul(mb[:, 1, c], kw[:, c], vtok[:, c], start=True, stop=True)
                    mm.then_inc(r_S, 1)

            def ret_sample(b):
                pe.wait_ge(r0_in[b % R0], 32 * (b // R0 + 1))
                if b == 0:
                    pe.wait_ge(r_zero, 1)
                pe.wait_ge(r_kwm, b + 1)
                for j in range(RP):
                    pe.matmul(mb[:, 3, j * SMP + b * NT:j * SMP + (b + 1) * NT], rs0[b % R0][:, j, :],
                              qd[:, j, b * NT:(b + 1) * NT], start=True, stop=True)
                if b >= 2:
                    pe.wait_ge(rs_n, b - 1)
                for j in range(RP):
                    c = slice(j * P, (j + 1) * P)
                    mm = pe.matmul(mb[:, 1 + b % 2, c], kwm[b % 2][0:SMP, c], vtok[0:SMP, c], start=True, stop=True)
                mm.then_inc(rs_S, 1)

            def ret_norm_sum(i):
                pe.wait_ge(b_sq, i + 1)
                if i == 0:
                    pe.wait_ge(hs_n, 2 * NB)
                    pe.wait_ge(hs_y, 1)
                if i >= 2:
                    pe.wait_ge(b_ln, i - 1)
                for half in range(2):
                    mm = pe.matmul(mb[:, 2 * (i % 2) + half, 0:HALF], blk, halves(ret_sq[i])[:, half, :],
                                   start=True, stop=True)
                mm.then_inc(b_sum, 1)

            def ssd_norm_sum(g):
                pe.wait_ge(b_add, 4 * (g + 1))
                pe.wait_ge(b_ln, RP)
                for half in range(2):
                    mm = pe.matmul(mb[:, 2 * g + half, 0:HALF], ones, halves(z_gate[g])[:, half, :],
                                   start=True, stop=True)
                mm.then_inc(b_sum, 1)

            def pool_mm_(g):
                pe.wait_ge(pooled_ok, g + 1)
                pe.wait_ge(evac, U_GPOOL + g + 1)
                dst = acc_of(U_GPOOL + g)
                for half in range(2):
                    mm = pe.matmul(dst[:, half, :], pw[:, g, :], halves(vT[:, g, :])[:, half, :],
                                   start=True, stop=True)
                mm.then_inc(pool_mm, 1)

            norm_sum()
            pe.wait_ge(nsum, 1)
            next_layer(pe, next_pe)
            with pe.Fori(0, DEPTH):
                project_first()
                for u in range(1, UNITS):
                    if U_GPOOL + 2 <= u < U_GPOOL + 6:
                        pe.wait_ge(pool_out, u - U_GPOOL - 1)
                    if S_RST <= u < S_SSD:
                        project(u, lambda: ret_sample(2 * (u - S_RST)))
                        ret_sample(2 * (u - S_RST) + 1)
                    elif S_SST <= u < S_GATE:
                        project(u, lambda: ssd_sample(2 * (u - S_SST)))
                        ssd_sample(2 * (u - S_SST) + 1)
                    elif u == S_RN + 2:
                        project(u, lambda: (ret_norm_sum(2), ret_norm_sum(3)))
                    elif U_GPOOL < u < U_GPOOL + 5:
                        project(u, lambda: pool_mm_(u - U_GPOOL - 1))
                    elif u > 1:
                        project(u)
                    if u == S_STK:
                        pe.wait_ge(tab_in, 16)
                        pe.wait_ge(stk_ok, 1)
                        for t in range(TILES):
                            mm = pe.transpose(mb[0:rows(t), t // 4, (t % 4) * 96:(t % 4 + 1) * 96],
                                              stk[:, cols(t)], ident[0:96, 0:96])
                        mm.then_inc(stk_T, 1)
                    if S_RET <= u < S_RST:
                        t = (u - S_RET) // 2
                        (ret_turn if (u - S_RET) % 2 == 0 else ret_y)(t)
                    if S_SSD <= u < S_SST:
                        t = (u - S_SSD) // 2
                        (ssd_turn if (u - S_SSD) % 2 == 0 else ssd_y)(t)
                    if u == S_RN + 1:
                        ret_norm_sum(0)
                        ret_norm_sum(1)
                    if S_NORM < u <= S_NORM + GROUPS:
                        ssd_norm_sum(u - S_NORM - 1)
                norm_sum()
                pe.wait_ge(nsum, 1)
                next_layer(pe, next_pe)

        @block.scalar
        def _(eng):
            lane = Lane(eng, chain_a)
            go, settle, wait = lane.go, lane.settle, lane.wait
            act = nc.scalar.activation

            def high(u, l=None):
                if u < 2:
                    eng.wait_ge(first_in[u], l * 16 + 16)
                else:
                    wait(s_raw[u % RAW], 16 * (u // RAW))
                if u >= 2:
                    wait(proj, u - 1)
                go(act(w_hi[:, u % 2, :, :], w_raw[:, u % RAW, :, :], ACT.Copy), w_hid, u + 1)

            def split_y(j):
                wait(y_full, j + 1)
                go(act(hin[:, 0, j, :], xbc[:, j, :], ACT.Copy), y_hi, j + 1)

            def square(j):
                go(act(tmp[:, j % 2, :], x[:, j, :], ACT.Square), sqd, j + 1)

            def rs(src, n):
                go(act(halves(rstd[:, :]), src, ACT.Ln, scale=1.0 / n, bias=eps[:, 0:1]))
                settle()
                return act(rstd[:, :], rstd[:, :], ACT.Exp, scale=-0.5)

            def norm_rstd():
                wait(nsum, 1)
                go(rs(mb[:, 2:4, 0:HALF], D_MODEL), n_rstd, 1)

            def read_out(u):
                wait(proj, u + 1)
                src = acc_of(u)
                if u == U_DT:
                    go(act(halves(dt_raw), src[0:HEADS], ACT.Identity, bias=hvec[:, 0:1]), evac, u + 1)
                elif u < U_V:
                    i = u - U_Q
                    if i == 0:
                        wait(x_out, 16)
                        wait(h_lo, KT)
                    go(act(halves(qk[:, i, :]), src, ACT.Copy, scale=1.0 if i < RP else HD ** -0.5), evac, u + 1)
                elif u < U_CONV:
                    go(act(halves(vT[:, u - U_V, :]), src, ACT.Copy), evac, u + 1)
                elif u < U_GPOOL:
                    i = u - U_CONV
                    w, end = (3, HALO) if i < CONV_CHUNKS else (PB, PHALO)
                    wait(halo_in, i + 1)
                    hb = halo[:, i % 2, 0:end]
                    go(act(hb[:, w:w + HALF], src[:, 0, :], ACT.Copy))
                    go(act(hb[:, w + HALF:w + SEQ], src[:, 1, 0:SEQ - HALF], ACT.Copy))
                    go(act(hb[:, w + SEQ:].rearrange("p (b n) -> p b n", b=NB)[:, :, w:],
                           src[:, 1, SEQ - HALF:].rearrange("p (b n) -> p b n", b=NB), ACT.Copy), evac, u + 1)
                elif u < U_GRET:
                    i = u - U_GPOOL
                    if i >= 2:
                        wait(pool_out, i - 1)
                    go(act(halves(tmp[:, i % 2, :]), src, ACT.Silu), evac, u + 1)
                elif u < U_Z:
                    i = u - U_GRET
                    go(act(halves(qk[:, RP + i, :]), src, ACT.Silu), evac, u + 1)
                else:
                    i = u - U_Z
                    if i == 0:
                        wait(halo_saved, 16)
                    if i >= 4:
                        wait(g_z_used, i - 3)
                    go(act(halves(z_gate[i % 4]), src, ACT.Silu), evac, u + 1)

            def ssd_row_exps(t):
                m = decay[:, t % 2, :, :]
                wait(cum_in[t % 2], 16 * (t // 2 + 1))
                if t < TILES - 1:
                    if t == 1:
                        wait(ret_free, 1)
                    else:
                        wait(s_Y, t)
                    go(act(cdec_t[:, :, :], m, ACT.Exp))
                    if t > 1:
                        wait(s_h, t)
                    go(act(el[:, :], m[:, :, CH - 1], ACT.Exp), s_row, t)
                else:
                    ms = m[:, :, 0:SMP].rearrange("p h (b k) -> p h b k", b=NB)
                    go(act(els[:, :, :], ms[:, :, :, NT - 1], ACT.Exp), s_row, t)
                    wait(ecs_in, 32)
                    go(act(ecs[:, :, :], ecs[:, :, :], ACT.Exp), ecs_ok, 1)

            def ssd_decay(t):
                n = rows(t)
                m = decay[0:n, t % 2, :, 0:n]
                if t == 0:
                    wait(cum_in[0], 16)
                    wait(tokv_ok, 1)
                settle()
                for h in range(HEADS):
                    go(act(m[:, h, :], m[:, h, :], ACT.Relu, scale=-1.0, bias=tokv[0:n, t, h:h + 1]))
                settle()
                go(act(m, m, ACT.Exp, scale=-1.0), s_exp, t + 1)

            def two_rstd(i, n):
                for q in range(2):
                    wait(b_sum, i + q + 1)
                    if i + q >= 2:
                        wait(b_used, i + q - 1)
                    go(act(halves(rstds[q]), mb[:, 2 * q:2 * q + 2, 0:HALF], ACT.Ln, scale=1.0 / n, bias=eps[:, 0:1]),
                       b_ln, i + q + 1)
                settle()
                for q in range(2):
                    go(act(rstds[q], rstds[q], ACT.Exp, scale=-0.5), b_rstd, i + q + 1)

            def ret_slot(t):
                n = rows(t)
                wait(rT, t + 1)
                if t > 0:
                    wait(r_S, t)
                go(act(vtok[0:n, :], mb[0:n, 3, :], ACT.Copy), r_v, t + 1)

            eng.wait_ge(eps_ok, 1)
            for j in range(KT):
                if j % 2 == 0:
                    eng.wait_ge(s_x[j // 2], 16)
                if j >= 2:
                    eng.wait_ge(sq_add, j - 1)
                square(j)
            norm_rstd()
            lane.close()
            next_layer(eng, next_act)
            with eng.Fori(0, DEPTH) as l:
                high(0, l)
                for j in range(KT):
                    wait(h_full, j + 1)
                    go(act(hin[:, 0, j, :], xbc[:, j, :], ACT.Copy), h_hi, j + 1)
                    if j == 0:
                        high(1, l)
                wait(s_par, 48)
                for u in range(UNITS):
                    if u + 2 < UNITS:
                        high(u + 2)
                    if u < U_OUT:
                        read_out(u)
                    if u == U_DT:
                        settle()
                        go(act(dt_e, dt_raw, ACT.Abs))
                        settle()
                        go(act(dt_e, dt_e, ACT.Exp, scale=-1.0), dt_s1, 1)
                        go(act(na[:, :], hvec[:, 1:2], ACT.Exp))
                    if u == 2:
                        wait(dt_s2, 1)
                        settle()
                        go(act(dt_l, dt_u, ACT.Ln), dt_s3, 1)
                    if u == 7:
                        wait(cum_ok, 1)
                        go(act(dt_w, dt_s, ACT.Exp), wl_ok, 1)
                    if U_CONV < u <= U_POOL:
                        i = u - U_CONV - 1
                        k = CONV_ORDER[i]
                        wait(halo_used, i + 1)
                        cb = vec[:, V_CB + k:V_CB + k + 1]
                        go(act(xbc[:, k, 0:SEQ], cvt[:, i % 2, 0:SEQ], ACT.Silu, bias=cb))
                        go(act(xbc[:, k, SEQ:].rearrange("p (b n) -> p b n", b=NB),
                               cvt[:, i % 2, 3 + SEQ:HALO].rearrange(
                                   "p (b n) -> p b n", b=NB)[:, :, 0:NT], ACT.Silu, bias=cb),
                           xbc_ok, i + 1)
                    if S_RET <= u < S_RST and (u - S_RET) % 2 == 0:
                        ret_slot((u - S_RET) // 2)
                    if u == S_SSD - 1:
                        ssd_decay(0)
                    if S_SSD <= u < S_SST:
                        t = (u - S_SSD) // 2
                        if (u - S_SSD) % 2 == 0:
                            wait(sT, t + 1)
                            if t > 0:
                                wait(s_S, t)
                            n = rows(t)
                            go(act(btok[0:n, :, :], mb[0:n, 3, 0:256].rearrange("p (g n) -> p g n", g=2), ACT.Copy),
                               s_bt, t + 1)
                        elif t + 1 < TILES:
                            ssd_row_exps(t + 1)
                            ssd_decay(t + 1)
                    if u == S_RN:
                        wait(rs_y, 1)
                        wait(pool_out, 4)
                        for i in range(RP):
                            go(act(ret_sq[i], qk[:, i, :], ACT.Square), b_sq, i + 1)
                    if u in (S_RN + 1, S_RN + 2):
                        two_rstd(2 * (u - S_RN - 1), HD)
                    if u == S_PL:
                        wait(ssd_free, 1)
                        for i in range(4):
                            wait(pool_out, i + 1)
                            go(act(mix[:, 0, 0, i, :], vT[:, i, :], ACT.Copy), mix_hi, i + 1)
                    if u == S_RL:
                        for i in range(RP):
                            wait(ret_full, i + 1)
                            go(act(mix[:, 1, 0, i, :], qk[:, i, :], ACT.Copy), mix_hi, 4 + i + 1)
                    if S_NORM <= u < S_NORM + GROUPS:
                        g = u - S_NORM
                        for j in range(4 * g, 4 * g + 4):
                            wait(g_z_used, j + 1)
                            if j < 2:
                                wait(b_sum, RP)
                            else:
                                wait(b_add, j - 1)
                            go(act(tmp[:, j % 2, :], xbc[:, j, :], ACT.Square), b_sq, RP + j + 1)
                    if u == S_NORM + GROUPS:
                        two_rstd(RP, PAIRS // GROUPS * P)
                    if S_NORM + GROUPS < u < S_NORM + GROUPS + 5:
                        for j in (2 * (u - S_NORM - GROUPS - 1), 2 * (u - S_NORM - GROUPS - 1) + 1):
                            split_y(j)
                    m = u - U_OUT - OUT_CHUNKS
                    if m >= 0:
                        wait(x_new, OUT_CHUNKS + m + 1)
                        if m >= 2:
                            wait(sq_add, m - 1)
                        square(m)
                norm_rstd()
                lane.close()
                next_layer(eng, next_act)

        @block.vector
        def _(eng):
            lane = Lane(eng, chain_v)
            go, settle, wait = lane.go, lane.settle, lane.wait
            V = nc.vector

            def split(u):
                wait(w_hid, u + 1)
                go(V.tensor_tensor(w_lo[:, u % 2, :, :], w_raw[:, u % RAW, :, :], w_hi[:, u % 2, :, :].bitcast(F32),
                                   ALU.subtract), w_split, u + 1)

            def add_square(j):
                wait(sqd, j + 1)
                settle()
                if j == 0:
                    go(V.tensor_copy(ssq[:, :], tmp[:, j % 2, :]), sq_add, j + 1)
                else:
                    go(V.tensor_tensor(ssq[:, :], ssq[:, :], tmp[:, j % 2, :], ALU.add), sq_add, j + 1)

            def v_(o, n=1):
                return vec[:, o:o + n]

            def dt_part(k):
                if k == 0:
                    wait(dt_s1, 1)
                    go(V.tensor_scalar(dt_u, dt_e, 1.0, None, ALU.add), dt_s2, 1)
                    settle()
                    go(V.tensor_scalar(dt_r, dt_u, 1.0, None, ALU.subtract))
                    settle()
                    go(V.tensor_scalar(dt_v, dt_r, 0.0, None, ALU.is_equal))
                    go(V.tensor_scalar(dt_s, dt_r, 1e-30, None, ALU.max))
                elif k == 1:
                    go(V.tensor_tensor(dt_v, dt_v, dt_e, ALU.mult))
                    go(V.reciprocal(dt_r, dt_s))
                elif k == 2:
                    go(V.tensor_tensor(dt_r, dt_r, dt_e, ALU.mult))
                    wait(dt_s3, 1)
                    settle()
                    go(V.tensor_tensor(dt_r, dt_r, dt_l, ALU.mult))
                elif k == 3:
                    go(V.tensor_tensor(dt_r, dt_r, dt_v, ALU.add))
                    settle()
                    go(V.scalar_tensor_tensor(out=dt_r, in0=dt_raw, scalar=0.0, in1=dt_r, op0=ALU.max, op1=ALU.add))
                elif k == 4:
                    go(V.tensor_scalar(dt_v, dt_r, na[:, 0:1], -1.0, ALU.mult, ALU.mult))
                    go(V.tensor_copy(stk[32:32 + HEADS, :], dt_r))
                    settle()
                    go(V.tensor_tensor_scan(cum, reset, dt_v, 0.0, ALU.mult, ALU.add))
                elif k == 5:
                    for q, (o, n, w) in enumerate(((0, TILES - 1, CH), (SEQ, NB, NT))):
                        cu = cum[:, o:o + n * w].rearrange("p (a b) -> p a b", a=n)
                        lastc = cu[:, :, w - 1:w].to_broadcast([HEADS, n, w])
                        i = V.tensor_tensor(dt_s[:, o:o + n * w].rearrange("p (a b) -> p a b", a=n), lastc, cu,
                                            ALU.subtract)
                        if q == 0:
                            go(i)
                        else:
                            go(i, cum_ok, 1)
                elif k == 7:
                    wait(wl_ok, 1)
                    go(V.tensor_tensor(stk[64:64 + HEADS, :], dt_w, dt_r, ALU.mult), stk_ok, 1)

            def conv(i):
                k = CONV_ORDER[i]
                wait(evac, U_CONV + i + 1)
                wait(halo_in, i + 1)
                if i >= 2:
                    wait(xbc_ok, i - 1)
                h, o = halo[:, i % 2, :], cvt[:, i % 2, 0:CVO]
                w = [v_(V_CW + 4 * k + c) for c in range(CW)]
                settle()
                go(V.tensor_scalar(o, h[:, 3:3 + CVO], w[3], None, ALU.mult))
                for c in (2, 1, 0):
                    settle()
                    ins = V.scalar_tensor_tensor(out=o, in0=h[:, c:c + CVO], scalar=w[c], in1=o, op0=ALU.mult,
                                                 op1=ALU.add)
                    if c:
                        go(ins)
                    else:
                        go(ins, halo_used, i + 1)

            def rotate(i):
                wait(evac, U_Q + i + 1)
                q = qk[:, i, :]
                settle()
                go(V.stream_shuffle(cvt[:, 0, 0:TOK], q, [(p + 16) % 32 for p in range(32)]))
                settle()
                go(V.tensor_tensor(cvt[:, 1, 0:TOK], cvt[:, 0, 0:TOK], T("sin"), ALU.mult))
                go(V.tensor_tensor(q, q, T("cos"), ALU.mult))
                settle()
                go(V.tensor_tensor(q, q, cvt[:, 1, 0:TOK], ALU.add), rot, i + 1)

            def heads(ap, n=HEADS):
                return ap.rearrange("p (h d) -> p h d", h=n)

            def before(u):
                if U_GPOOL < u < U_GPOOL + 5:
                    pool_gate(u - U_GPOOL - 1)
                if S_RST <= u < S_SSD:
                    ret_seq(2 * (u - S_RST))
                if S_SST <= u < S_GATE:
                    ssd_seq(2 * (u - S_SST))

            def ssd_1(t):
                n = rows(t)
                wait(sT, t + 1)
                src = mb[0:n, 0:2, :].rearrange("p a (h d) -> p (a h) d", d=HD)
                dt_b = tokv[0:n, t, 32:48].unsqueeze(2).to_broadcast([n, HEADS, HD])
                dw_b = tokv[0:n, t, 64:80].unsqueeze(2).to_broadcast([n, HEADS, HD])
                settle()
                go(V.tensor_tensor(heads(xdt[0:n, :]), src, dt_b, ALU.mult))
                go(V.tensor_tensor(heads(xdw[0:n, :]), src, dw_b, ALU.mult))
                mask = (T("causal") if t < TILES - 1 else T("smask")[0:SMP, :])
                go(V.tensor_tensor(gm[0:n, :, 0:n], mb[0:n, 2, 0:256].rearrange("p (g n) -> p g n", g=2)[:, :, 0:n],
                                   mask.unsqueeze(1).to_broadcast([n, GROUPS, n]), ALU.mult), s_xdt, t + 1)
                wait(s_exp, t + 1)
                settle()
                for g in range(GROUPS):
                    m = decay[0:n, t % 2, 8 * g:8 * g + 8, 0:n]
                    ins = V.tensor_tensor(m, m, gm[0:n, g, 0:n].unsqueeze(1).to_broadcast([n, 8, n]), ALU.mult)
                    if g == 0:
                        go(ins)
                    else:
                        go(ins, s_M, t + 1)

            def c_decay(t):
                wait(s_row, t)
                settle()
                for g in range(GROUPS):
                    ins = V.tensor_tensor(cdec_t[:, 8 * g:8 * g + 8, :], cdec_t[:, 8 * g:8 * g + 8, :],
                                          xbc[:, 10 + g, cols(t)].unsqueeze(1).to_broadcast([P, 8, CH]), ALU.mult)
                    if g == 0:
                        go(ins)
                    else:
                        go(ins, s_ec, t)

            def ssd_2(t):
                n = rows(t)
                if t < TILES - 1:
                    wait(s_S, t + 1)
                    st = mb[:, 0:2, :].rearrange("p a n -> p (a n)")
                    if t == 0:
                        wait(rp_out, 32)
                        settle()
                        go(V.tensor_copy(hT[:, :], st), s_h, 1)
                    else:
                        wait(s_Y, t + 1)
                        settle()
                        go(V.tensor_tensor(heads(hT[:, :]), heads(hT[:, :]),
                                           el[:, :].unsqueeze(2).to_broadcast([P, HEADS, HD]), ALU.mult))
                        settle()
                        go(V.tensor_tensor(hT[:, :], hT[:, :], st, ALU.add), s_h, t + 1)
                    settle()
                wait(s_Y, t + 1)
                for j in range(PAIRS):
                    if t < TILES - 1:
                        src = mb[:, 2 + j // 4, (j % 4) * P:(j % 4) * P + n]
                    else:
                        src = mb[:, 2, j * SMP:(j + 1) * SMP]
                    y = xbc[:, j, cols(t)]
                    ins = V.scalar_tensor_tensor(out=y, in0=y, scalar=v_(V_DS + j), in1=src, op0=ALU.mult,
                                                 op1=ALU.add)
                    if j < PAIRS - 1:
                        go(ins)
                    else:
                        go(ins, s_y, t + 1)

            def ssd_b_seq(b):
                if b >= 2:
                    wait(hs_S, 2 * (b - 1))
                if b == 0:
                    wait(s_bt, TILES)
                settle()
                go(V.tensor_scalar(bseq[0:SMP, b % 2, :, :], btok[0:SMP, :, :], T("bmask")[0:SMP, b:b + 1], None,
                                   ALU.mult), b_seq, b + 1)

            def ssd_state(b):
                h = h0[b % 4]
                wait(hs_I, b + 1)
                if b == 0:
                    wait(s_exp, TILES)
                settle()
                go(V.tensor_tensor(heads(h[:, :]), heads(h[:, :]),
                                   els[:, :, b:b + 1].to_broadcast([P, HEADS, HD]), ALU.mult))
                settle()
                for g in range(GROUPS):
                    i = 2 * b + g
                    wait(hs_S, i + 1)
                    c = slice(g * 512, (g + 1) * 512)
                    go(V.tensor_tensor(h[:, c], h[:, c], mb[:, i % 3, :], ALU.add), hs_n, i + 1)

            def ret_1(t):
                n = rows(t)
                wait(rT, t + 1)
                if t == 0:
                    wait(r_zero, 1)
                dm = T("dmask") if t < TILES - 1 else T("sdmask")[0:SMP, :]
                ed = T("edec") if t < TILES - 1 else T("sedec")[0:SMP, :]
                settle()
                go(V.tensor_tensor(pmat[0:n, :, :, 0:n], mb[0:n, 0:2, :].rearrange("p e (j n) -> p e j n", n=P)[:, :, :, 0:n],
                                   dm.rearrange("p (e j n) -> p e j n", e=2, j=RP), ALU.mult))
                go(V.tensor_tensor(heads(kw[0:n, :], RH), heads(mb[0:n, 2, :], RH),
                                   ed.unsqueeze(2).to_broadcast([n, RH, HD]), ALU.mult))
                settle()
                if t < TILES - 1:
                    go(V.tensor_tensor(qd[:, :, :], qk[:, 0:RP, cols(t)], T("inner").rearrange("p (j n) -> p j n", j=RP),
                                       ALU.mult), r_P, t + 1)
                else:
                    for j in range(RP):
                        ins = V.tensor_tensor(qd[:, j, 0:SMP].rearrange("p (b k) -> p b k", b=NB),
                                              qk[:, j, SEQ:].rearrange("p (b k) -> p b k", b=NB),
                                              T("sinner")[:, j * NT:(j + 1) * NT].unsqueeze(1).to_broadcast([P, NB, NT]),
                                              ALU.mult)
                        if j < RP - 1:
                            go(ins)
                        else:
                            go(ins, r_P, t + 1)

            def diag(ap, e):
                r = slice(e * HD, (e + 1) * HD)
                return ap[r, :, e * HD:(e + 1) * HD]

            def ret_2(t):
                n = rows(t)
                wait(r_Y, t + 1)
                settle()
                go(V.tensor_copy(qk[:, 0:RP, cols(t)], mb[:, 0, :].rearrange("p (j n) -> p j n", n=P)[:, :, 0:n]),
                   r_y, t + 1)
                if t < TILES - 1:
                    wait(r_S, t + 1)
                    sm = mb[:, 1, :].rearrange("p (j n) -> p j n", j=RP)
                    settle()
                    if t == 0:
                        go(V.tensor_copy(diag(rS, 0), diag(sm, 0)))
                        go(V.tensor_copy(diag(rS, 1), diag(sm, 1)), r_s, 1)
                    else:
                        for e in range(2):
                            r = slice(e * HD, (e + 1) * HD)
                            go(V.tensor_tensor(diag(rS, e), diag(rS, e),
                                               T("cdec")[r, :].unsqueeze(2).to_broadcast([HD, RP, HD]), ALU.mult))
                        settle()
                        go(V.tensor_tensor(diag(rS, 0), diag(rS, 0), diag(sm, 0), ALU.add))
                        go(V.tensor_tensor(diag(rS, 1), diag(rS, 1), diag(sm, 1), ALU.add), r_s, t + 1)

            def ret_k_seq(b):
                if b >= 2:
                    wait(rs_S, b - 1)
                settle()
                go(V.tensor_scalar(kwm[b % 2][0:SMP, :], kw[0:SMP, :], T("bmask")[0:SMP, b:b + 1], None, ALU.mult),
                   r_kwm, b + 1)

            def ret_state(b):
                wait(rs_S, b + 1)
                s, sm = rs0[b % R0], mb[:, 1 + b % 2, :].rearrange("p (j n) -> p j n", j=RP)
                settle()
                for e in range(2):
                    r = slice(e * HD, (e + 1) * HD)
                    go(V.tensor_tensor(diag(s, e), diag(s, e), T("scdec")[r, :].unsqueeze(2).to_broadcast([HD, RP, HD]),
                                       ALU.mult))
                settle()
                go(V.tensor_tensor(diag(s, 0), diag(s, 0), diag(sm, 0), ALU.add))
                go(V.tensor_tensor(diag(s, 1), diag(s, 1), diag(sm, 1), ALU.add), rs_n, b + 1)

            def ret_seq(b):
                ret_state(b)
                if b + 2 < NB:
                    ret_k_seq(b + 2)

            def ssd_seq(b):
                ssd_state(b)
                if b + 2 < NB:
                    ssd_b_seq(b + 2)

            def pool(i):
                wait(evac, U_POOL + i + 1)
                wait(halo_in, CONV_CHUNKS + i + 1)
                cur, w = halo[:, i % 2, :], 1
                bufs = (cvt[:, 0, :], cvt[:, 1, :])
                while w < WINDOWS[i]:
                    dst = bufs[0]
                    settle()
                    go(V.tensor_tensor(dst[:, 2 * w - 1:PHALO], cur[:, 2 * w - 1:PHALO], cur[:, w - 1:PHALO - w],
                                       ALU.add))
                    cur, w, bufs = dst, 2 * w, bufs[::-1]
                settle()
                go(V.tensor_tensor(cur[:, PB:PB + 16], cur[:, PB:PB + 16], T("cnt")[:, i * 16:(i + 1) * 16], ALU.mult))
                settle()
                raw = halo[:, i % 2, :]
                go(V.scalar_tensor_tensor(out=vT[:, i, 0:SEQ], in0=cur[:, PB:PB + SEQ], scalar=1.0 / WINDOWS[i],
                                          in1=raw[:, PB:PB + SEQ], op0=ALU.mult, op1=ALU.subtract))

                def seqs(ap):
                    return ap[:, PB + SEQ:PHALO].rearrange("p (b k) -> p b k", b=NB)[:, :, PB:]

                settle()
                go(V.scalar_tensor_tensor(out=vT[:, i, SEQ:].rearrange("p (b k) -> p b k", b=NB), in0=seqs(cur),
                                          scalar=1.0 / WINDOWS[i], in1=seqs(raw), op0=ALU.mult, op1=ALU.subtract),
                   pooled_ok, i + 1)
                settle()
                go(V.tensor_copy(pad[:, 0:1], pad[:, 1:2]), halo_used, CONV_CHUNKS + i + 1)

            def pool_gate(i):
                wait(pool_mm, i + 1)
                settle()
                go(V.scalar_tensor_tensor(out=halves(vT[:, i, :]), in0=acc_of(U_GPOOL + i), scalar=v_(V_PS + i),
                                          in1=halves(tmp[:, i % 2, :]), op0=ALU.mult, op1=ALU.mult),
                   pool_out, i + 1)

            def ret_out(i):
                q = qk[:, i, :]
                wait(b_rstd, i + 1)
                settle()
                go(V.scalar_tensor_tensor(out=q, in0=q, scalar=v_(V_RN + i), in1=rstds[i % 2], op0=ALU.mult,
                                          op1=ALU.mult), b_used, i + 1)
                settle()
                go(V.tensor_tensor(q, q, qk[:, RP + i, :], ALU.mult), ret_full, i + 1)

            def z_use(i):
                wait(evac, U_Z + i + 1)
                settle()
                go(V.tensor_tensor(xbc[:, i, :], xbc[:, i, :], z_gate[i % 4], ALU.mult), g_z_used, i + 1)

            go(V.memset(pad[:, :], 0.0))
            go(V.memset(stk[:, :], 0.0))
            go(V.memset(ones, 1.0))
            V.memset(eps[:, :], EPS).then_inc(eps_ok, 1)
            settle()
            for j in range(KT):
                add_square(j)
            wait(n_rstd, 1)
            lane.close()
            next_layer(eng, next_dve)
            with eng.Fori(0, DEPTH) as l:
                eng.wait_ge(vec_in, l * 16 + 16)
                for j in range(KT + 1):
                    if j in (1, 2):
                        split(j - 1)
                    if j < KT:
                        go(V.scalar_tensor_tensor(out=xbc[:, j, :], in0=x[:, j, :], scalar=v_(V_NW + j),
                                                  in1=rstd[:, :], op0=ALU.mult, op1=ALU.mult), h_full, j + 1)
                    if j > 0:
                        wait(h_hi, j)
                        go(V.tensor_tensor(hin[:, 1, j - 1, :], xbc[:, j - 1, :],
                                           hin[:, 0, j - 1, :].bitcast(F32), ALU.subtract), h_lo, j)
                for u in range(UNITS):
                    before(u)
                    if u + 2 < UNITS:
                        split(u + 2)
                    if u == U_Q:
                        wait(tab_in, 16)
                    if U_Q <= u < U_V:
                        rotate(u - U_Q)
                    if 1 <= u <= 8:
                        settle()
                        dt_part(u - 1)
                    if u == S_STK:
                        wait(stk_T, 1)
                        settle()
                        go(V.tensor_copy(tokv[:, 0:4, :], mb[:, 0, 0:384].rearrange("p (t n) -> p t n", t=4)))
                        go(V.tensor_copy(tokv[0:SMP, 4, :], mb[0:SMP, 1, 0:96]), tokv_ok, 1)
                    if S_RET <= u < S_RST:
                        t = (u - S_RET) // 2
                        (ret_1 if (u - S_RET) % 2 == 0 else ret_2)(t)
                    if u == S_RST - 1:
                        ret_k_seq(0)
                        ret_k_seq(1)
                    if S_RST <= u < S_SSD:
                        ret_seq(2 * (u - S_RST) + 1)
                    if u == S_SSD - 1:
                        settle()
                        go(V.tensor_tensor(qk[:, 0:RP, SEQ:], qk[:, 0:RP, SEQ:],
                                           mb[:, 3, 0:RP * SMP].rearrange("p (j n) -> p j n", j=RP), ALU.add),
                           rs_y, 1)
                    if S_SSD <= u < S_SST:
                        t = (u - S_SSD) // 2
                        (ssd_1 if (u - S_SSD) % 2 == 0 else ssd_2)(t)
                        if (u - S_SSD) % 2 == 1 and t + 1 < TILES - 1:
                            c_decay(t + 1)
                    if U_CONV <= u < U_POOL:
                        conv(u - U_CONV)
                    if u in POOL_SLOTS:
                        pool(POOL_SLOTS.index(u))
                    if u == S_SST - 1:
                        ssd_b_seq(0)
                        ssd_b_seq(1)
                    if S_SST <= u < S_GATE:
                        ssd_seq(2 * (u - S_SST) + 1)
                    if u == S_GATE - 1:
                        wait(ecs_ok, 1)
                        settle()
                        go(V.tensor_tensor(ecs[:, :, :], ecs[:, :, :], mb[:, 3, :].rearrange("p (j n) -> p j n", j=PAIRS),
                                           ALU.mult))
                        settle()
                        go(V.tensor_tensor(xbc[:, 0:8, SEQ:], xbc[:, 0:8, SEQ:], ecs[:, :, :], ALU.add), hs_y, 1)
                    if S_GATE <= u < S_GATE + PAIRS // 2:
                        for i in (2 * (u - S_GATE), 2 * (u - S_GATE) + 1):
                            z_use(i)
                    if u in (S_RN + 1, S_RN + 2):
                        for i in (2 * (u - S_RN - 1), 2 * (u - S_RN - 1) + 1):
                            ret_out(i)
                    if u in (S_PL, S_RL):
                        for i in range(4):
                            n = i + 1 if u == S_PL else 4 + i + 1
                            wait(mix_hi, n)
                            which, src = (0, vT) if u == S_PL else (1, qk)
                            go(V.tensor_tensor(mix[:, which, 1, i, :], src[:, i, :], mix[:, which, 0, i, :].bitcast(F32),
                                               ALU.subtract), mix_lo, n)
                    if S_NORM <= u < S_NORM + GROUPS:
                        g = u - S_NORM
                        for j in range(4 * g, 4 * g + 4):
                            wait(b_sq, RP + j + 1)
                            settle()
                            if j % 4 == 0:
                                go(V.tensor_copy(z_gate[g], tmp[:, j % 2, :]), b_add, j + 1)
                            else:
                                go(V.tensor_tensor(z_gate[g], z_gate[g], tmp[:, j % 2, :], ALU.add), b_add, j + 1)
                    if S_NORM + GROUPS <= u < S_NORM + GROUPS + 4:
                        for j in (2 * (u - S_NORM - GROUPS), 2 * (u - S_NORM - GROUPS) + 1):
                            y = xbc[:, j, :]
                            wait(b_rstd, RP + j // 4 + 1)
                            go(V.scalar_tensor_tensor(out=y, in0=y, scalar=v_(V_SN + j), in1=rstds[j // 4],
                                                      op0=ALU.mult, op1=ALU.mult), y_full, j + 1)
                    if S_NORM + GROUPS < u < S_NORM + GROUPS + 5:
                        for j in (2 * (u - S_NORM - GROUPS - 1), 2 * (u - S_NORM - GROUPS - 1) + 1):
                            wait(y_hi, j + 1)
                            go(V.tensor_tensor(hin[:, 1, j, :], xbc[:, j, :], hin[:, 0, j, :].bitcast(F32),
                                               ALU.subtract), y_lo, j + 1)
                    o = u - U_OUT
                    if o >= 0:
                        m = o % OUT_CHUNKS
                        wait(proj, u + 1)
                        if o < OUT_CHUNKS and o % 2 == 0:
                            wait(x_back[o // 2], 16)
                        settle()
                        go(V.tensor_tensor(halves(x[:, m, :]), halves(x[:, m, :]), acc_of(u), ALU.add),
                           x_new, o + 1)
                        if o >= OUT_CHUNKS:
                            add_square(m)
                wait(n_rstd, 1)
                lane.close()
                next_layer(eng, next_dve)
            for j in range(KT):
                V.scalar_tensor_tensor(out=x[:, j, :], in0=x[:, j, :], scalar=T("fnw")[:, j:j + 1], in1=rstd[:, :],
                                       op0=ALU.mult, op1=ALU.mult).then_inc(f_ok, 1)

        @block.gpsimd
        def _(eng):
            lane = Lane(eng, chain_p)
            go, settle, wait = lane.go, lane.settle, lane.wait
            G = nc.gpsimd

            def fill(i):
                conv_ = i < CONV_CHUNKS
                w, end = (3, HALO) if conv_ else (PB, PHALO)
                st = cst[:, CONV_ORDER[i], :, :] if conv_ else pst[:, i - CONV_CHUNKS, :, :]
                hb = halo[:, i % 2, 0:end]
                settle()
                go(G.memset(hb[:, 0:w], 0.0))
                settle()
                go(G.tensor_copy(hb[:, w + SEQ:].rearrange("p (b n) -> p b n", b=NB)[:, :, 0:w], st),
                   halo_in, i + 1)

            def save(i):
                conv_ = i < CONV_CHUNKS
                u = U_CONV + i if conv_ else U_POOL + i - CONV_CHUNKS
                w, end = (3, HALO) if conv_ else (PB, PHALO)
                to = cso[:, CONV_ORDER[i], :, :] if conv_ else pso[:, i - CONV_CHUNKS, :, :]
                hb = halo[:, i % 2, 0:end]
                wait(evac, u + 1)
                settle()
                go(G.tensor_copy(to[:, 0, :], hb[:, SEQ:w + SEQ]))
                go(G.tensor_copy(to[:, 1:, :], hb[:, w + SEQ:].rearrange("p (b n) -> p b n", b=NB)[:, :, NT:]),
                   halo_saved, i + 1)
                wait(halo_used, i + 1)

            clear_signals(eng)
            with eng.Fori(0, DEPTH) as l:
                for i in range(R0):
                    go(G.memset(rs0[i][:, :, :], 0.0))
                go(G.memset(rS[:, :, :], 0.0), r_zero, 1)
                wait(s_st, 32)
                fill(0)
                fill(1)
                for i in range(16):
                    save(i)
                    if i + 2 < 16:
                        fill(i + 2)
                settle()
                eng.dma_start(a["conv_o"][l], cso[:, :, :, :]).then_inc(states_out, 16)
                eng.dma_start(a["pool_o"][l], pso[:, :, :, :]).then_inc(states_out, 16)
                wait(states_out, 32)
                wait(halo_used, 16)
                lane.close()
                clear_signals(eng)
            for j in range(KT):
                eng.wait_ge(f_ok, j + 1)
                eng.dma_start(a["y"][:, j, :], x[:, j, :]).then_inc(f_out, 16)
            eng.wait_ge(f_out, 16 * KT)


def rot_order():
    return np.array([16 * (r // 32) + r % 32 if r % 32 < 16 else 32 + 16 * (r // 32) + r % 32 - 16
                     for r in range(HD)])


def tables():
    f = np.float32
    t = np.zeros((P, TAB_N), f)

    def put(name, v):
        o, w = TAB[name]
        v = np.asarray(v, f).reshape(v.shape[0], w)
        t[:v.shape[0], o:o + w] = v

    i = np.arange(P)
    put("ident", np.eye(P))
    put("blk", (i[:, None] // HD == i[None, :] // HD) * 1.0)
    put("causal", (i[None, :] >= i[:, None]) * 1.0)
    s = np.arange(SMP)
    same = s[:, None] // NT == s[None, :] // NT
    ok = same & (s[None, :] >= s[:, None])
    put("smask", ok * 1.0)
    put("bmask", (s[:, None] // NT == np.arange(NB)[None, :]) * 1.0)
    pos = np.concatenate([np.arange(SEQ), PAST + s % NT]).astype(f)
    half = HD // 2
    inv = (10000.0 ** (-np.arange(half) / half)).astype(f)
    o = np.tile(rot_order(), 2)
    ang = (pos[None, :] * inv[o % half][:, None]).astype(f)
    put("cos", np.cos(ang.astype(np.float64)))
    put("sin", np.sin(ang.astype(np.float64)) * np.where(o < half, -1.0, 1.0)[:, None])
    lg = np.log1p(-np.exp2(-5.0 - np.arange(RH, dtype=f))).astype(f)
    pair = np.arange(RH).reshape(RP, 2).T.reshape(-1)

    def decay(n, mask, rel):
        d = np.exp((np.maximum(rel, 0).astype(f)[:, None, :] * lg[pair][None, :, None]).astype(f))
        return np.where(mask[:, None, :], d, 0.0)

    put("dmask", decay(P, i[None, :] >= i[:, None], i[None, :] - i[:, None]))
    put("sdmask", decay(SMP, ok, s[None, :] - s[:, None]))
    head = 2 * np.arange(RP)[None, :] + i[:, None] // HD
    put("inner", np.exp(((i + 1).astype(f)[None, None, :] * lg[head][:, :, None]).astype(f)))
    put("sinner", np.exp(((np.arange(NT) + 1).astype(f)[None, None, :] * lg[head][:, :, None]).astype(f)))
    put("edec", np.exp(((CH - 1 - i).astype(f)[:, None] * lg[None, :]).astype(f)))
    put("sedec", np.exp(((NT - 1 - s % NT).astype(f)[:, None] * lg[None, :]).astype(f)))
    put("cdec", np.exp((f(CH) * lg[head]).astype(f)))
    put("scdec", np.exp((f(NT) * lg[head]).astype(f)))
    k = np.arange(16)
    put("cnt", np.tile(np.concatenate([w / np.minimum(k + 1.0, w) for w in WINDOWS])[None, :], (P, 1)))
    return t


def resets():
    col = np.arange(TOK)
    start = np.where(col < SEQ, col % CH == 0, (col - SEQ) % NT == 0)
    return np.tile(np.where(start, 0.0, 1.0)[None, :], (HEADS, 1)).astype(np.float32)


_OUTS = {
    "y": (P, KT, TOK), "ssm_p": (DEPTH, P, HEADS * HD), "ssm_s": (DEPTH, NB, P, HEADS * HD),
    "conv_o": (DEPTH, P, CONV_CHUNKS, 1 + NB, 3), "pool_o": (DEPTH, P, 4, 1 + NB, PB),
    "ret_p": (DEPTH, P, RP, HD), "ret_s": (DEPTH, NB, P, RP, HD),
}


def lay_out(v):
    v = {k: np.asarray(q) for k, q in v.items()}
    rot = (np.arange(RH)[:, None] * HD + rot_order()[None, :]).reshape(-1)
    w_in, w_out = v["w_in"], v["w_out"]
    z, c, dt, q, k, vv, gr, u, gp, end = np.cumsum([0, 1024, 1536, HEADS, 512, 512, 512, 512, 512, 512])
    cc = w_in[:, :, c:dt].reshape(DEPTH, D_MODEL, CONV_CHUNKS, P)[:, :, list(CONV_ORDER)]
    w = np.concatenate([w_in[:, :, dt:q], np.zeros((DEPTH, D_MODEL, P - HEADS), w_in.dtype),
                        w_in[:, :, q:k][:, :, rot], w_in[:, :, k:vv][:, :, rot], w_in[:, :, vv:gr],
                        cc.reshape(DEPTH, D_MODEL, -1), w_in[:, :, u:gp], w_in[:, :, gp:end], w_in[:, :, gr:u],
                        w_in[:, :, z:c]], axis=2)
    w = w.reshape(DEPTH, KT, P, U_OUT, P).transpose(0, 3, 2, 1, 4)
    wo = w_out.reshape(DEPTH, 2, KT, P, OUT_CHUNKS, P)
    wo = np.stack([wo[:, 0], np.roll(wo[:, 1], RP, axis=1)], axis=1)
    wo = [wo[:, 1 - o // OUT_CHUNKS, :, :, o % OUT_CHUNKS].transpose(0, 2, 1, 3) for o in range(2 * OUT_CHUNKS)]
    w = np.concatenate([w, np.stack(wo, axis=1)], axis=1).reshape(DEPTH * UNITS, P, KT, P)
    w = np.concatenate([w, np.zeros((2, P, KT, P), w.dtype)])

    def on_parts(a):
        return a.reshape(DEPTH, -1, P).transpose(0, 2, 1)

    cw = v["conv_w"].reshape(DEPTH, CW, CONV_CHUNKS, P).transpose(0, 3, 2, 1).reshape(DEPTH, P, -1)
    vec = np.concatenate([on_parts(v["norm_w"]), cw, on_parts(v["conv_b"]),
                          on_parts(np.repeat(v["d_skip"], HD, axis=1)), on_parts(v["ssd_norm_w"]),
                          on_parts(v["ret_norm_w"]), on_parts(v["pool_scale"])], axis=2)
    vec = np.concatenate([vec, np.zeros((1, P, V_N), vec.dtype)])
    x = np.concatenate([v["x_prompt"].reshape(SEQ, D_MODEL), v["x_sample"].reshape(SMP, D_MODEL)])
    tab = tables()
    o, n = TAB["fnw"]
    tab[:, o:o + n] = v["final_norm_w"].reshape(KT, P).T
    ret = v["state_ret"][:, :, :, rot_order(), :].reshape(DEPTH, NB, RP, 2, HD, HD)
    return {
        "x": x.T.reshape(KT, P, TOK).transpose(1, 0, 2), "tab": tab, "reset": resets(), "w": w, "vec": vec,
        "hvec": np.stack([v["dt_bias"], v["a_log"]], axis=2), "pw": v["pool_w"].transpose(0, 2, 1, 3),
        "cst": v["state_conv"].reshape(DEPTH, NB, 3, CONV_CHUNKS, P).transpose(0, 4, 3, 1, 2),
        "pst": v["state_pool"].reshape(DEPTH, NB, PB, 4, P).transpose(0, 4, 3, 1, 2),
        "ssm0": v["state_ssm"].reshape(DEPTH, NB, HEADS * HD, P).transpose(0, 1, 3, 2),
        "ret0": ret.transpose(0, 1, 3, 4, 2, 5).reshape(DEPTH, NB, P, RP, HD),
    }


def taken(r):
    y = r["y"].transpose(1, 0, 2).reshape(D_MODEL, TOK).T
    back = np.argsort(rot_order())

    def ssm(a, n):
        return a.reshape(DEPTH, n, P, HEADS * HD).transpose(0, 1, 3, 2).reshape(DEPTH, n, HEADS, HD, P)

    def ret(a, n):
        a = a.reshape(DEPTH, n, 2, HD, RP, HD).transpose(0, 1, 4, 2, 3, 5).reshape(DEPTH, n, RH, HD, HD)
        return a[:, :, :, back, :]

    def small(a, w):
        return a.transpose(0, 3, 4, 2, 1).reshape(DEPTH, 1 + NB, w, -1)

    conv, pool = small(r["conv_o"], 3), small(r["pool_o"], PB)
    c = np.ascontiguousarray
    return (c(y[:SEQ]).reshape(1, SEQ, D_MODEL), c(y[SEQ:]).reshape(NB, NT, D_MODEL),
            c(ssm(r["ssm_p"], 1)), c(conv[:, :1]), c(ret(r["ret_p"], 1)), c(pool[:, :1]),
            c(ssm(r["ssm_s"], NB)), c(conv[:, 1:]), c(ret(r["ret_s"], NB)), c(pool[:, 1:]))


def program(bacc, arrays):
    nc = bacc.Bacc("TRN2", target_bir_lowering=False, num_devices=1)
    a = {k: nc.dram_tensor(f"in_{k}", q.shape, F32, kind="ExternalInput").ap() for k, q in arrays.items()}
    for k, shape in _OUTS.items():
        a[k] = nc.dram_tensor(f"out_{k}", shape, F32, kind="ExternalOutput").ap()
    a["cum"] = nc.dram_tensor("cum_rows", (HEADS * TOK,), F32, kind="Internal").ap()
    a["x_kept"] = nc.dram_tensor("x_kept", (P, KT, TOK), F32, kind="Internal").ap()
    trunk(nc, a)
    return nc


def kernel(**inputs):
    import concourse.bacc as _bacc
    from concourse.bass_utils import run_bass_kernel_spmd as _run

    arrays = {k: np.ascontiguousarray(q) for k, q in lay_out(inputs).items()}
    nc = program(_bacc, arrays)
    r = _run(nc, [{f"in_{k}": q for k, q in arrays.items()}], core_ids=[0])
    return taken({k: r.results[0][f"out_{k}"] for k in _OUTS})
```

```python
from contextlib import ExitStack

import numpy as np

import concourse.bass as bass
from concourse import mybir

F32 = mybir.dt.float32
F32R = mybir.dt.float32r
ALU = mybir.AluOpType
ACT = mybir.ActivationFunctionType

P = 128
DEPTH = 2
D_MODEL = 1024
SEQ = 512
NB, NT = 8, 8
SMP = NB * NT
TOK = SEQ + SMP
HALF = TOK // 2
KT = D_MODEL // P
HEADS = 16
HD = 64
PAIRS = HEADS // 2
GROUPS = 2
CH = 128
TILES = SEQ // CH + 1
RH = 8
RP = RH // 2
CW = 4
CONV_CHUNKS = 12
WINDOWS = (2, 4, 8, 16)
PB = 15
PAST = 4096
EPS = 1e-6

U_DT = 0
U_Q = 1
U_K = U_Q + RP
U_V = U_K + RP
U_CONV = U_V + RP
U_POOL = U_CONV + CONV_CHUNKS
U_GRET = U_POOL + 4
U_GPOOL = U_GRET + RP
U_Z = U_GPOOL + 4
U_OUT = U_Z + PAIRS
LAG = 2
OUT_CHUNKS = D_MODEL // P
UNITS = U_OUT + 2 * OUT_CHUNKS
CONV_ORDER = (8, 9, 10, 11, 0, 1, 2, 3, 4, 5, 6, 7)
RAW = 2

TWOS = NB // 2

S_STK = U_CONV - 1
S_RET = U_CONV
S_RST = S_RET + 2 * TILES
S_SSD = S_RST + NB // 2
S_SST = S_SSD + 2 * TILES
S_GATE = S_SST + NB // 2
S_RN = S_GATE - 1
S_PL = S_RN + 1
S_RL = S_GATE + 2
S_NORM = U_OUT
POOL_SLOTS = (U_POOL, U_POOL + 1, S_SSD + 2, S_SSD + 4)
assert S_RL + 1 < U_OUT and S_SST >= U_Z and S_GATE + PAIRS // 2 <= U_OUT

HALO = 3 + SEQ + NB * (3 + NT)
CVO = HALO - 3
PHALO = PB + SEQ + NB * (PB + NT)

V_NW, V_CW, V_CB = 0, 8, 8 + 48
V_DS = V_CB + 12
V_SN = V_DS + 8
V_RN = V_SN + 8
V_PS = V_RN + 4
V_N = V_PS + 4


def table_places():
    at, n = {}, 0
    for name, w in (("ident", P), ("blk", P), ("causal", P), ("smask", SMP), ("bmask", NB),
                    ("cos", TOK), ("sin", TOK), ("dmask", RH * CH), ("sdmask", RH * SMP),
                    ("inner", RP * CH), ("sinner", RP * NT), ("edec", RH), ("sedec", RH),
                    ("cdec", RP), ("scdec", RP), ("cnt", 4 * 16), ("fnw", KT)):
        at[name] = (n, w)
        n += w
    return at, n


TAB, TAB_N = table_places()


class Lane:

    def __init__(self, eng, chain):
        self.eng, self.chain, self.n, self.last = eng, chain, 0, None

    def go(self, ins, signal=None, n=None):
        if signal is None:
            self.n += 1
            signal, n = self.chain, self.n
        ins.then_inc(signal, 1)
        self.last = (signal, n)

    def settle(self):
        if self.last is not None:
            self.eng.wait_ge(*self.last)
            self.last = None

    def wait(self, signal, n):
        self.eng.wait_ge(signal, n)

    def close(self):
        self.settle()
        if self.n:
            self.eng.wait_ge(self.chain, self.n)
        self.n = 0


def trunk(nc: bass.Bass, a):
    with ExitStack() as ctx:
        top = [(nc.sbuf_base + 63) // 64 * 64]

        def place(name, shape, dt=F32, at=None):
            size = 4
            for d in shape[1:]:
                size *= d
            off = top[0] if at is None else at
            t = nc.alloc_sbuf_tensor_at(name, shape, dt, offset=off)
            if at is None:
                top[0] = off + (size + 31) // 32 * 32
                assert top[0] <= nc.sbuf_usable_end, (name, top[0] - nc.sbuf_usable_end)
            return t

        def sem(name):
            return ctx.enter_context(nc.semaphore(name))

        hin = place("hin", [P, 2, KT, TOK], F32R)
        w_raw = place("w_raw", [P, RAW, KT, P])
        w_hi = place("w_hi", [P, 2, KT, P], F32R)
        w_lo = place("w_lo", [P, 2, KT, P], F32R)
        work = top[0]
        mix = place("mix", [P, 2, 2, 4, TOK], F32R)
        decay = place("decay", [P, 2, HEADS, CH], at=work)
        cdec_t = place("c_decayed", [P, HEADS, CH], at=work + 4 * 4096)
        xdt = place("xdt", [P, HEADS * HD], at=work + 4 * 6144)
        xdw = place("xdt_to_end", [P, HEADS * HD], at=work + 4 * 7168)
        hT = place("ssm_state", [P, HEADS * HD], at=work + 4 * 8192)
        h0 = [place(f"h0_{i}", [P, HEADS * HD], at=work + 4 * o)
              for i, o in enumerate((2048, 3072, 4096, 5120, 0, 1024, 6144, 8192))]
        rw = work + 4 * 4608
        rs0 = [place(f"ret0_{i}", [P, RP, P], at=rw + 4 * 512 * i if i < 3 else work + 4 * (2048 + 512 * (i - 3)))
               for i in range(NB)]
        pmat = place("ret_probs", [P, 2, RP, CH], at=rw + 4 * 1536)
        kw = place("k_to_end", [P, RP * P], at=rw + 4 * 2560)
        qd = place("q_decayed", [P, RP, CH], at=rw + 4 * 3584)
        rS = place("ret_state", [P, RP, P], at=rw + 4 * 4096)
        xbc = place("xbc", [P, CONV_CHUNKS, TOK])
        qk_at = top[0]
        qk = place("qk", [P, 2 * RP, TOK])
        x = place("x", [P, KT, TOK], at=qk_at)
        vT = place("vT", [P, RP, TOK])
        halo = place("halo", [P, 2, PHALO])
        cvt = place("conv_out", [P, 2, PHALO])
        tmp = place("tmp", [P, 2, TOK])
        ssq = place("ssq", [P, TOK])
        rstd = place("rstd", [P, TOK])
        tab = place("tab", [P, TAB_N])
        vec = place("vec", [P, V_N])
        hvec = place("head_vec", [HEADS, 2])
        pw = place("pool_w", [P, 4, P])
        cst = place("conv_state", [P, CONV_CHUNKS, NB, 3])
        cso = place("conv_state_out", [P, CONV_CHUNKS, 1 + NB, 3])
        pst = place("pool_state", [P, 4, NB, PB])
        pso = place("pool_state_out", [P, 4, 1 + NB, PB])
        stk = place("stacked", [96, TOK])
        tokv = place("token_vecs", [P, TILES, 96])
        gm = place("scores", [P, GROUPS, CH])
        btok = place("b_tok", [P, GROUPS, P])
        masked = top[0]
        bseq_ = place("b_tok_seq", [P, 2, GROUPS * P])
        el = place("exp_last", [P, HEADS])
        els = place("exp_last_sample", [P, HEADS, NB])
        dt_raw, dt_e, dt_u, dt_l, dt_r, dt_s, dt_v, dt_w, reset = (xbc[0:HEADS, i, :] for i in range(9))
        cum = stk[0:HEADS, :]
        ret_sq = (tmp[:, 0, :], tmp[:, 1, :], xbc[:, 8, :], xbc[:, 9, :])
        rstds = (rstd[:, :], ssq[:, :])
        z_gate = [halo[:, 0, 0:TOK], halo[:, 1, 0:TOK], cvt[:, 0, 0:TOK], cvt[:, 1, 0:TOK]]
        na = place("neg_a", [HEADS, 1])
        ecs = place("exp_cum_sample", [P, PAIRS, SMP])
        vtok = place("v_tok", [P, RP * P])
        pad = place("pad", [P, 2])
        eps = place("eps", [P, 1])
        kwm = [place("k_to_end_seq_0", [P, RP * P], at=masked)[0:SMP, :],
               place("k_to_end_seq_1", [P, RP * P], at=rw + 4 * 3072)[0:SMP, :],
               stk[0:SMP, 0:RP * P], ssq[0:SMP, 0:RP * P]]
        bseq = [bseq_[0:SMP, 0, :], bseq_[0:SMP, 1, :], gm[0:SMP, :, :].rearrange("p g n -> p (g n)"),
                stk[0:SMP, 0:GROUPS * P]]
        ones_ = place("ones", [P, P])
        ones = ones_[:, :]

        acc = ctx.enter_context(nc.psum_tensor("acc", [P, 2, 2, 512], F32))
        mb = ctx.enter_context(nc.psum_tensor("misc", [P, 4, 512], F32))

        def T(name):
            o, w = TAB[name]
            return tab[:, o:o + w]

        ident, blk = T("ident"), T("blk")

        def acc_of(u):
            return acc[:, u % 2, :, 0:HALF]

        def halves(ap):
            return ap.rearrange("p (a n) -> p a n", a=2)

        def cols(t):
            return slice(t * CH, t * CH + (CH if t < TILES - 1 else SMP))

        def rows(t):
            return CH if t < TILES - 1 else SMP

        tab_in = sem("tables_loaded")
        first_in = [sem(f"first_w_loaded_{i}") for i in range(2)]
        vec_in = sem("layer_vectors_loaded")
        s_x = [sem(f"x_loaded_{i}") for i in range(4)]
        s_raw = [sem(f"w_loaded_{i}") for i in range(RAW)]
        s_par = sem("params_loaded")
        s_st = sem("small_states_loaded")
        w_hid = sem("w_high")
        w_split = sem("w_split")
        proj = sem("projected")
        evac = sem("acc_read")
        x_new = sem("x_updated")
        sqd = sem("squared")
        sq_add = sem("squares_added")
        nsum = sem("norm_sum")
        n_rstd = sem("norm_rstd")
        h_full = sem("h_scaled")
        h_hi = sem("h_high")
        h_lo = sem("h_split")
        dt_s1 = sem("dt_exp")
        dt_s2 = sem("dt_one_plus")
        dt_s3 = sem("dt_log")
        cum_ok = sem("cum_ready")
        wl_ok = sem("exp_to_end")
        stk_ok = sem("stacked_ready")
        stk_T = sem("stacked_turned")
        tokv_ok = sem("token_vecs_ready")
        cum_out = sem("cum_stored")
        cum_in = [sem(f"cum_spread_{i}") for i in range(2)]
        ecs_in = sem("cum_rows_spread")
        ecs_ok = sem("exp_cum_rows")
        halo_in = sem("halo_filled")
        halo_used = sem("halo_used")
        xbc_ok = sem("xbc_ready")
        rot = sem("rotated")
        sT = sem("ssd_turned")
        s_xdt = sem("ssd_xdt")
        s_bt = sem("ssd_b_tok")
        s_exp = sem("ssd_exps")
        s_row = sem("ssd_row_exps")
        s_ec = sem("ssd_c_decayed")
        s_M = sem("ssd_weights")
        s_S = sem("ssd_state_sum")
        s_Y = sem("ssd_y_sum")
        s_y = sem("ssd_y_read")
        s_h = sem("ssd_state")
        h0_in = [sem(f"h0_loaded_{i}") for i in range(NB)]
        h0_out = [sem(f"h0_stored_{i}") for i in range(NB)]
        b_seq = sem("b_tok_seq_ready")
        hs_S = sem("sample_state_sum")
        hs_n = sem("sample_state")
        hs_I = sem("sample_inter")
        hs_y = sem("sample_y")
        hp_out = sem("ssm_state_stored")
        rT = sem("ret_turned")
        r_P = sem("ret_weights")
        r_v = sem("ret_v_tok")
        r_Y = sem("ret_y_sum")
        r_S = sem("ret_state_sum")
        r_y = sem("ret_y_read")
        r_s = sem("ret_state_new")
        r0_in = [sem(f"ret0_loaded_{i}") for i in range(NB)]
        r0_out = [sem(f"ret0_stored_{i}") for i in range(NB)]
        r_zero = sem("ret_slots_zeroed")
        r_kwm = sem("k_seq_ready")
        rs_S = sem("sample_ret_sum")
        rs_n = sem("sample_ret")
        rs_y = sem("sample_ret_y")
        rp_out = sem("ret_state_stored")
        pooled_ok = sem("pooled")
        pool_mm = sem("pool_mixed")
        g_z_used = sem("z_gated")
        mix_hi = sem("mix_ret_high")
        mix_lo = sem("mix_split")
        b_sq = sem("branch_squared")
        b_add = sem("branch_squares_added")
        b_sum = sem("branch_norm_sum")
        b_rstd = sem("branch_rstd")
        b_ln = sem("branch_norm_sum_read")
        b_used = sem("branch_rstd_used")
        y_full = sem("ssd_out_full")
        y_hi = sem("ssd_out_high")
        y_lo = sem("ssd_out_split")
        states_out = sem("small_states_stored")
        x_out = sem("x_stored")
        x_back = [sem(f"x_reloaded_{i}") for i in range(4)]
        ret_free = sem("ret_work_free")
        ssd_free = sem("ssd_work_free")
        halo_saved = sem("halo_saved")
        pool_out = sem("pool_gated")
        ret_full = sem("ret_gated")
        eps_ok = sem("eps_set")
        f_out = sem("y_stored")
        f_ok = sem("y_ready")
        chain_v, chain_a, chain_p = sem("vector_order"), sem("scalar_order"), sem("pool_order")
        layer_over = sem("layer_over")
        next_pe, next_act, next_dve, next_sp = (sem(f"next_layer_{e}") for e in ("pe", "act", "dve", "sp"))
        to_clear = range(s_x[0].num, layer_over.num + 1)

        def next_layer(eng, begin):
            eng.sem_inc(layer_over, 1)
            eng.wait_ge(begin, 1)
            eng.sem_clear(begin)

        def clear_signals(pool):
            pool.wait_ge(layer_over, 4)
            pool.dma_reset(to_clear)
            pool.sem_clear(to_clear)
            for begin in (next_pe, next_act, next_dve, next_sp):
                pool.sem_inc(begin, 1)

        block = ctx.enter_context(nc.Block())

        @block.sync
        def _(sp):
            def load_first(l):
                sp.dma_start(vec[:, :], a["vec"][l]).then_inc(vec_in, 16)
                for u in range(2):
                    sp.dma_start(w_raw[:, u, :, :], a["w"][l * UNITS + u]).then_inc(first_in[u], 16)

            def spread(t):
                done = cum_in[t % 2]
                if t >= 2:
                    sp.wait_ge(s_Y, t - 1)
                if t < TILES - 1:
                    src = a["cum"][0:HEADS * SEQ].rearrange("(t n) -> t n", t=4)[t:t + 1, :]
                    sp.dma_start(decay[:, t % 2, :, :].rearrange("p h n -> p (h n)"),
                                 src.to_broadcast([P, HEADS * CH])).then_inc(done, 16)
                else:
                    src = a["cum"][HEADS * SEQ:].rearrange("(o h n) -> o h n", o=1, h=HEADS)
                    sp.dma_start(decay[:, t % 2, :, 0:SMP], src.to_broadcast([P, HEADS, SMP])).then_inc(done, 16)

            def load_ret(l, b):
                for e in range(2):
                    r = slice(e * HD, (e + 1) * HD)
                    sp.dma_start(rs0[b][r, :, e * HD:(e + 1) * HD], a["ret0"][l, b, r]).then_inc(r0_in[b], 16)

            def load_two(l, q):
                for e in range(2):
                    i = 2 * q + e
                    sp.dma_start(h0[i][:, :], a["ssm0"][l, q + e * TWOS]).then_inc(h0_in[i], 16)

            def beside(l, s):
                if s == 1:
                    sp.dma_start(cst[:, :, :, :], a["cst"][l]).then_inc(s_st, 16)
                    sp.dma_start(pst[:, :, :, :], a["pst"][l]).then_inc(s_st, 16)
                    sp.wait_ge(r_zero, 1)
                if 1 <= s <= NB:
                    load_ret(l, s - 1)
                if s == 6:
                    sp.wait_ge(cum_ok, 1)
                    sp.dma_start(a["cum"][0:HEADS * SEQ].rearrange("(t h n) -> h t n", t=4, h=HEADS),
                                 cum[:, 0:SEQ].rearrange("h (t n) -> h t n", t=4)).then_inc(cum_out, 16)
                    sp.dma_start(a["cum"][HEADS * SEQ:].rearrange("(h n) -> h n", h=HEADS),
                                 cum[:, SEQ:]).then_inc(cum_out, 16)
                if s == 7:
                    sp.wait_ge(cum_out, 32)
                    spread(0)
                    by_head = a["cum"][HEADS * SEQ:].rearrange("(j e n) -> e j n", e=2, n=SMP)
                    for e in range(2):
                        sp.dma_start(ecs[e * HD:(e + 1) * HD, :, :], by_head[e:e + 1].to_broadcast([HD, PAIRS, SMP]))\
                          .then_inc(ecs_in, 16)
                if s == S_RST - 1:
                    sp.wait_ge(r_s, TILES - 1)
                    for e in range(2):
                        r = slice(e * HD, (e + 1) * HD)
                        sp.dma_start(a["ret_p"][l, r], rS[r, :, e * HD:(e + 1) * HD]).then_inc(rp_out, 16)
                if S_RST <= s < S_SSD:
                    q = s - S_RST
                    for n, b in enumerate((q, q + TWOS)):
                        sp.wait_ge(rs_n, 2 * q + n + 1)
                        for e in range(2):
                            r = slice(e * HD, (e + 1) * HD)
                            sp.dma_start(a["ret_s"][l, b, r], rs0[b][r, :, e * HD:(e + 1) * HD]).then_inc(r0_out[b], 16)
                if s == S_SSD - 1:
                    for b in range(NB):
                        sp.wait_ge(r0_out[b], 32)
                    sp.sem_inc(ret_free, 1)
                    spread(1)
                if S_SSD <= s < S_SST and (s - S_SSD) % 2 == 1:
                    t = (s - S_SSD) // 2
                    if t + 2 < TILES:
                        spread(t + 2)
                    if t == TILES - 2:
                        sp.wait_ge(s_h, TILES - 1)
                        sp.dma_start(a["ssm_p"][l], hT[:, :]).then_inc(hp_out, 16)
                        sp.wait_ge(s_Y, TILES - 1)
                        for q in range(2):
                            load_two(l, q)
                    if t == TILES - 1:
                        sp.wait_ge(s_Y, TILES)
                        sp.wait_ge(hp_out, 16)
                        for q in range(2, TWOS):
                            load_two(l, q)
                if S_SST < s <= S_GATE:
                    q = s - S_SST - 1
                    for e in range(2):
                        i = 2 * q + e
                        sp.wait_ge(hs_n, 4 * q + 2 + e + 1)
                        sp.dma_start(a["ssm_s"][l, q + e * TWOS], h0[i][:, :]).then_inc(h0_out[i], 16)
                if s == S_GATE:
                    for i in range(NB):
                        sp.wait_ge(h0_out[i], 16)
                    sp.sem_inc(ssd_free, 1)
                if s == S_RL:
                    sp.wait_ge(mix_lo, 8)
                    sp.wait_ge(x_out, 16)
                    for i in range(4):
                        sp.dma_start(x[:, 2 * i:2 * i + 2, :], a["x_kept"][:, 2 * i:2 * i + 2, :])\
                          .then_inc(x_back[i], 16)

            for i in range(4):
                sp.dma_start(x[:, 2 * i:2 * i + 2, :], a["x"][:, 2 * i:2 * i + 2, :]).then_inc(s_x[i], 16)
            load_first(0)
            sp.dma_start(tab[:, :], a["tab"]).then_inc(tab_in, 16)
            next_layer(sp, next_sp)
            with sp.Fori(0, DEPTH) as l:
                sp.dma_start(a["x_kept"], x[:, :, :]).then_inc(x_out, 16)
                sp.dma_start(hvec[:, :], a["hvec"][l]).then_inc(s_par, 16)
                sp.dma_start(reset, a["reset"]).then_inc(s_par, 16)
                sp.dma_start(pw[:, :, :], a["pw"][l]).then_inc(s_par, 16)
                for u in range(2, UNITS):
                    if u >= 2 + RAW:
                        sp.wait_ge(w_split, u - RAW - 1)
                    sp.dma_start(w_raw[:, u % RAW, :, :], a["w"][l * UNITS + u]).then_inc(s_raw[u % RAW], 16)
                    if u >= 4:
                        beside(l, u - 4)
                sp.wait_ge(w_split, UNITS - 2)
                load_first(l + 1)
                next_layer(sp, next_sp)
            for i in range(4):
                sp.wait_ge(f_ok, 2 * i + 2)
                sp.dma_start(a["y"][:, 2 * i:2 * i + 2, :], x[:, 2 * i:2 * i + 2, :]).then_inc(f_out, 16)
            sp.wait_ge(f_out, 16 * 4)
            for u in range(2):
                sp.wait_ge(first_in[u], 16 * (DEPTH + 1))
            sp.wait_ge(vec_in, 16 * (DEPTH + 1))

        @block.tensor
        def _(pe):
            def operands(u, k, c):
                if U_OUT <= u < U_OUT + OUT_CHUNKS:
                    return mix[:, k // 4, 0, k % 4, c], mix[:, k // 4, 1, k % 4, c]
                return hin[:, 0, k, c], hin[:, 1, k, c]

            def products(u, half, k):
                out = acc_of(u)[:, half, :]
                hi, lo = operands(u, k, slice(half * HALF, (half + 1) * HALF))
                wh, wl = w_hi[:, u % 2, k, :], w_lo[:, u % 2, k, :]
                pe.matmul(out, wh, hi, start=k == 0, stop=False)
                pe.matmul(out, wh, lo, start=False, stop=False)
                return pe.matmul(out, wl, hi, start=False, stop=k == KT - 1)

            def project_first():
                for step in range(KT + LAG):
                    for u, k in ((0, step), (1, step - LAG)):
                        if not 0 <= k < KT:
                            continue
                        if u == 0:
                            pe.wait_ge(h_lo, k + 1)
                        for half in range(2):
                            mm = products(u, half, k)
                        if k == KT - 1:
                            mm.then_inc(proj, 1)

            def project(u, between=None):
                pe.wait_ge(w_split, u - 1)
                o = u - U_OUT
                if o < 2:
                    pe.wait_ge(evac, u - 1)
                else:
                    pe.wait_ge(x_new, o - 1)
                for half in range(2):
                    for k in range(KT):
                        if half == 0 and o == 0:
                            pe.wait_ge(mix_lo, k + 1)
                        if half == 0 and o == OUT_CHUNKS:
                            pe.wait_ge(y_lo, k + 1)
                        mm = products(u, half, k)
                    if half == 0 and between is not None:
                        between()
                mm.then_inc(proj, 1)

            def norm_sum():
                last = tmp[:, (KT - 1) % 2, :]
                pe.wait_ge(sq_add, KT - 1)
                for half in range(2):
                    pe.matmul(mb[:, 2 + half, 0:HALF], ones, halves(ssq[:, :])[:, half, :], start=True, stop=False)
                pe.wait_ge(sqd, KT)
                for half in range(2):
                    mm = pe.matmul(mb[:, 2 + half, 0:HALF], ones, halves(last)[:, half, :], start=False, stop=True)
                mm.then_inc(nsum, 1)

            def ssd_turn(t):
                n = rows(t)
                if t == 0:
                    pe.wait_ge(xbc_ok, CONV_CHUNKS)
                    pe.wait_ge(rs_y, 1)
                    pe.wait_ge(rs_n, NB)
                else:
                    pe.wait_ge(s_h, t)
                    pe.wait_ge(s_y, t)
                for j in range(PAIRS):
                    pe.transpose(mb[0:n, j // 4, (j % 4) * P:(j % 4 + 1) * P], xbc[:, j, cols(t)], ident)
                for g in range(GROUPS):
                    pe.matmul(mb[0:n, 2, g * P:g * P + n], xbc[:, 8 + g, cols(t)], xbc[:, 10 + g, cols(t)],
                              start=True, stop=True)
                for g in range(GROUPS):
                    mm = pe.transpose(mb[0:n, 3, g * P:(g + 1) * P], xbc[:, 8 + g, cols(t)], ident)
                mm.then_inc(sT, 1)

            def ssd_y(t):
                n = rows(t)
                pe.wait_ge(s_xdt, t + 1)
                pe.wait_ge(s_bt, t + 1)
                if t < TILES - 1:
                    for g in range(GROUPS):
                        mm = pe.matmul(mb[:, g, :], btok[:, g, :], xdw[:, g * 512:(g + 1) * 512], start=True, stop=True)
                    mm.then_inc(s_S, 1)
                pe.wait_ge(s_M, t + 1)
                inter = 0 < t < TILES - 1
                if inter:
                    pe.wait_ge(s_ec, t)
                for j in range(PAIRS):
                    if t < TILES - 1:
                        dst = mb[:, 2 + j // 4, (j % 4) * P:(j % 4) * P + n]
                    else:
                        dst = mb[:, 2, j * SMP:(j + 1) * SMP]
                    for e in range(2):
                        h = 2 * j + e
                        r = slice(e * HD, (e + 1) * HD)
                        mm = pe.matmul(dst[r, :], xdt[0:n, h * HD:(h + 1) * HD], decay[0:n, t % 2, h, 0:n],
                                       start=True, stop=not inter)
                        if inter:
                            mm = pe.matmul(dst[r, :], hT[:, h * HD:(h + 1) * HD], cdec_t[:, h, :],
                                           start=False, stop=True)
                mm.then_inc(s_Y, 1)

            def ssd_inter(q, e):
                if q == 0 and e == 0:
                    pe.wait_ge(s_y, TILES)
                n, b = 2 * q + e, q + e * TWOS
                pe.wait_ge(h0_in[n], 16)
                for j in range(PAIRS):
                    mm = pe.matmul(mb[:, 3, j * SMP + b * NT:j * SMP + (b + 1) * NT], h0[n][:, j * P:(j + 1) * P],
                                   xbc[:, 10 + j // 4, SEQ + b * NT:SEQ + (b + 1) * NT], start=True, stop=True)
                mm.then_inc(hs_I, 1)

            def ssd_sums(q, g):
                pe.wait_ge(b_seq, 2 * q + 2)
                for e in range(2):
                    i = 4 * q + 2 * g + e
                    if i >= 3:
                        pe.wait_ge(hs_n, i - 2)
                    pe.matmul(mb[:, i % 3, :], bseq[2 * (q % 2) + e][:, g * P:(g + 1) * P], xdw[0:SMP, g * 512:(g + 1) * 512],
                              start=True, stop=True).then_inc(hs_S, 1)

            def ret_turn(t):
                n = rows(t)
                if t == 0:
                    pe.wait_ge(rot, 2 * RP)
                    pe.wait_ge(evac, U_CONV)
                    pe.wait_ge(tokv_ok, 1)
                else:
                    pe.wait_ge(r_y, t)
                    pe.wait_ge(r_s, t)
                for j in range(RP):
                    for e in range(2):
                        r = slice(e * HD, (e + 1) * HD)
                        pe.matmul(mb[0:n, e, j * P:j * P + n], qk[r, RP + j, cols(t)], qk[r, j, cols(t)],
                                  start=True, stop=True)
                for j in range(RP):
                    pe.transpose(mb[0:n, 2, j * P:(j + 1) * P], qk[:, RP + j, cols(t)], ident)
                for j in range(RP):
                    mm = pe.transpose(mb[0:n, 3, j * P:(j + 1) * P], vT[:, j, cols(t)], ident)
                mm.then_inc(rT, 1)

            def ret_y(t):
                n = rows(t)
                pe.wait_ge(r_P, t + 1)
                pe.wait_ge(r_v, t + 1)
                inter = 0 < t < TILES - 1
                for j in range(RP):
                    dst = mb[:, 0, j * P:j * P + n]
                    if inter:
                        pe.matmul(dst, rS[:, j, :], qd[:, j, :], start=True, stop=False, skip_group_check=True)
                    for e in range(2):
                        r = slice(e * HD, (e + 1) * HD)
                        c = slice(j * P + e * HD, j * P + (e + 1) * HD)
                        mm = pe.matmul(dst[r, :], vtok[0:n, c], pmat[0:n, e, j, 0:n], start=not inter, stop=True,
                                       skip_group_check=inter)
                mm.then_inc(r_Y, 1)
                if t < TILES - 1:
                    for j in range(RP):
                        c = slice(j * P, (j + 1) * P)
                        mm = pe.matmul(mb[:, 1, c], kw[:, c], vtok[:, c], start=True, stop=True)
                    mm.then_inc(r_S, 1)

            def ret_sample(q):
                for e in range(2):
                    b = q + e * TWOS
                    pe.wait_ge(r0_in[b], 32)
                    for j in range(RP):
                        pe.matmul(mb[:, 3, j * SMP + b * NT:j * SMP + (b + 1) * NT], rs0[b][:, j, :],
                                  qd[:, j, b * NT:(b + 1) * NT], start=True, stop=True)
                pe.wait_ge(r_kwm, 2 * q + 2)
                if q > 0:
                    pe.wait_ge(rs_n, 2 * q)
                for e in range(2):
                    for j in range(RP):
                        c = slice(j * P, (j + 1) * P)
                        mm = pe.matmul(mb[:, 1 + e, c], kwm[2 * (q % 2) + e][:, c], vtok[0:SMP, c], start=True, stop=True)
                mm.then_inc(rs_S, 1)

            def ret_norm_sum(i):
                pe.wait_ge(b_sq, i + 1)
                if i == 0:
                    pe.wait_ge(hs_n, 2 * NB)
                    pe.wait_ge(hs_y, 1)
                if i >= 2:
                    pe.wait_ge(b_ln, i - 1)
                for half in range(2):
                    mm = pe.matmul(mb[:, 2 * (i % 2) + half, 0:HALF], blk, halves(ret_sq[i])[:, half, :],
                                   start=True, stop=True)
                mm.then_inc(b_sum, 1)

            def ssd_norm_sum(g):
                pe.wait_ge(b_add, 4 * (g + 1))
                pe.wait_ge(b_ln, RP)
                for half in range(2):
                    mm = pe.matmul(mb[:, 2 * g + half, 0:HALF], ones, halves(z_gate[g])[:, half, :],
                                   start=True, stop=True)
                mm.then_inc(b_sum, 1)

            def pool_mm_(g):
                pe.wait_ge(pooled_ok, g + 1)
                pe.wait_ge(evac, U_GPOOL + g + 1)
                dst = acc_of(U_GPOOL + g)
                for half in range(2):
                    mm = pe.matmul(dst[:, half, :], pw[:, g, :], halves(vT[:, g, :])[:, half, :],
                                   start=True, stop=True)
                mm.then_inc(pool_mm, 1)

            pe.wait_ge(sq_add, KT)
            for half in range(2):
                mm = pe.matmul(mb[:, 2 + half, 0:HALF], ones, halves(ssq[:, :])[:, half, :], start=True, stop=True)
            mm.then_inc(nsum, 1)
            pe.wait_ge(nsum, 1)
            next_layer(pe, next_pe)
            with pe.Fori(0, DEPTH):
                project_first()
                for u in range(1, UNITS):
                    if U_GPOOL + 2 <= u < U_GPOOL + 6:
                        pe.wait_ge(pool_out, u - U_GPOOL - 1)
                    if S_RST <= u < S_SSD:
                        project(u, lambda: ret_sample(u - S_RST))
                    elif S_SST <= u < S_GATE:
                        q = u - S_SST

                        def beside():
                            if u == U_GPOOL + 4:
                                pool_mm_(3)
                            ssd_inter(q, 0)
                            if q > 0:
                                ssd_sums(q - 1, 1)

                        project(u, beside)
                        ssd_inter(q, 1)
                        ssd_sums(q, 0)
                    elif u == S_GATE:
                        project(u, lambda: ssd_sums(TWOS - 1, 1))
                    elif u == S_NORM + 2:
                        project(u, lambda: ssd_norm_sum(0))
                        ssd_norm_sum(1)
                    elif u == S_RN + 2:
                        project(u, lambda: (ret_norm_sum(2), ret_norm_sum(3)))
                    elif U_GPOOL < u < U_GPOOL + 4 and (u - S_SSD) % 2 == 0:
                        project(u, lambda: pool_mm_(u - U_GPOOL - 1))
                    elif u > 1:
                        project(u)
                    if U_GPOOL < u < U_GPOOL + 4 and (u - S_SSD) % 2 == 1:
                        pool_mm_(u - U_GPOOL - 1)
                    if u == S_STK:
                        pe.wait_ge(tab_in, 16)
                        pe.wait_ge(stk_ok, 1)
                        for t in range(TILES):
                            mm = pe.transpose(mb[0:rows(t), t // 4, (t % 4) * 96:(t % 4 + 1) * 96],
                                              stk[:, cols(t)], ident[0:96, 0:96])
                        mm.then_inc(stk_T, 1)
                    if S_RET <= u < S_RST:
                        t = (u - S_RET) // 2
                        (ret_turn if (u - S_RET) % 2 == 0 else ret_y)(t)
                    if S_SSD <= u < S_SST:
                        t = (u - S_SSD) // 2
                        (ssd_turn if (u - S_SSD) % 2 == 0 else ssd_y)(t)
                    if u == S_RN + 1:
                        ret_norm_sum(0)
                        ret_norm_sum(1)
                norm_sum()
                pe.wait_ge(nsum, 1)
                next_layer(pe, next_pe)

        @block.scalar
        def _(eng):
            lane = Lane(eng, chain_a)
            go, settle, wait = lane.go, lane.settle, lane.wait
            act = nc.scalar.activation

            def high(u, n):
                go(act(w_hi[:, u % 2, :, :], w_raw[:, u % RAW, :, :], ACT.Copy), w_hid, n)

            def split_y(j):
                wait(y_full, j + 1)
                go(act(hin[:, 0, j, :], xbc[:, j, :], ACT.Copy), y_hi, j + 1)

            def square(j):
                go(act(tmp[:, j % 2, :], x[:, j, :], ACT.Square), sqd, j + 1)

            def rs(src, n):
                go(act(halves(rstd[:, :]), src, ACT.Ln, scale=1.0 / n, bias=eps[:, 0:1]))
                settle()
                return act(rstd[:, :], rstd[:, :], ACT.Exp, scale=-0.5)

            def norm_rstd():
                wait(nsum, 1)
                go(rs(mb[:, 2:4, 0:HALF], D_MODEL), n_rstd, 1)

            def read_out(u):
                src = acc_of(u)
                if u == U_DT:
                    go(act(halves(dt_raw), src[0:HEADS], ACT.Identity, bias=hvec[:, 0:1]), evac, u + 1)
                elif u < U_V:
                    i = u - U_Q
                    if i == 0:
                        wait(x_out, 16)
                        wait(h_lo, KT)
                    go(act(halves(qk[:, i, :]), src, ACT.Copy, scale=1.0 if i < RP else HD ** -0.5), evac, u + 1)
                elif u < U_CONV:
                    go(act(halves(vT[:, u - U_V, :]), src, ACT.Copy), evac, u + 1)
                elif u < U_GRET:
                    i = u - U_CONV
                    w, end = (3, HALO) if i < CONV_CHUNKS else (PB, PHALO)
                    wait(halo_in, i + 1)
                    hb = halo[:, i % 2, 0:end]
                    go(act(hb[:, w:w + HALF], src[:, 0, :], ACT.Copy))
                    go(act(hb[:, w + HALF:w + SEQ], src[:, 1, 0:SEQ - HALF], ACT.Copy))
                    go(act(hb[:, w + SEQ:].rearrange("p (b n) -> p b n", b=NB)[:, :, w:],
                           src[:, 1, SEQ - HALF:].rearrange("p (b n) -> p b n", b=NB), ACT.Copy), evac, u + 1)
                elif u < U_GPOOL:
                    go(act(halves(qk[:, RP + u - U_GRET, :]), src, ACT.Silu), evac, u + 1)
                elif u < U_Z:
                    i = u - U_GPOOL
                    if i >= 2:
                        wait(pool_out, i - 1)
                    go(act(halves(tmp[:, i % 2, :]), src, ACT.Silu), evac, u + 1)
                else:
                    i = u - U_Z
                    if i == 0:
                        wait(halo_saved, 16)
                    if i >= 4:
                        wait(g_z_used, i - 3)
                    go(act(halves(z_gate[i % 4]), src, ACT.Silu), evac, u + 1)

            def ssd_row_exps(t):
                m = decay[:, t % 2, :, :]
                wait(cum_in[t % 2], 16 * (t // 2 + 1))
                if t < TILES - 1:
                    if t == 1:
                        wait(ret_free, 1)
                    else:
                        wait(s_Y, t)
                    go(act(cdec_t[:, :, :], m, ACT.Exp))
                    if t > 1:
                        wait(s_h, t)
                    go(act(el[:, :], m[:, :, CH - 1], ACT.Exp), s_row, t)
                else:
                    ms = m[:, :, 0:SMP].rearrange("p h (b k) -> p h b k", b=NB)
                    go(act(els[:, :, :], ms[:, :, :, NT - 1], ACT.Exp), s_row, t)
                    wait(ecs_in, 32)
                    go(act(ecs[:, :, :], ecs[:, :, :], ACT.Exp), ecs_ok, 1)

            def ssd_clamp(t, part=0, parts=1):
                n = rows(t)
                if t == 0:
                    wait(cum_in[0], 16)
                    wait(tokv_ok, 1)
                settle()
                for h in range(HEADS * part // parts, HEADS * (part + 1) // parts):
                    m = decay[0:n, t % 2, h, 0:n]
                    go(act(m, m, ACT.Relu, scale=-1.0, bias=tokv[0:n, t, h:h + 1]))

            def ssd_decay(t):
                n = rows(t)
                m = decay[0:n, t % 2, :, 0:n]
                settle()
                go(act(m, m, ACT.Exp, scale=-1.0), s_exp, t + 1)

            def two_rstd(i, n):
                for q in range(2):
                    wait(b_sum, i + q + 1)
                    if i + q >= 2:
                        wait(b_used, i + q - 1)
                    go(act(halves(rstds[q]), mb[:, 2 * q:2 * q + 2, 0:HALF], ACT.Ln, scale=1.0 / n, bias=eps[:, 0:1]),
                       b_ln, i + q + 1)
                settle()
                for q in range(2):
                    go(act(rstds[q], rstds[q], ACT.Exp, scale=-0.5), b_rstd, i + q + 1)

            def ret_slot(t):
                n = rows(t)
                wait(rT, t + 1)
                if t > 0:
                    wait(r_S, t)
                go(act(vtok[0:n, :], mb[0:n, 3, :], ACT.Copy), r_v, t + 1)

            eng.wait_ge(eps_ok, 1)
            for j in range(KT):
                if j % 2 == 0:
                    eng.wait_ge(s_x[j // 2], 16)
                if j >= 2:
                    eng.wait_ge(sq_add, j - 1)
                square(j)
            norm_rstd()
            lane.close()
            next_layer(eng, next_act)
            with eng.Fori(0, DEPTH) as l:
                for j in range(KT):
                    wait(h_full, j + 1)
                    go(act(hin[:, 0, j, :], xbc[:, j, :], ACT.Copy), h_hi, j + 1)
                wait(s_par, 48)
                for u in range(UNITS):
                    wait(proj, u + 1)
                    if u + 2 < UNITS:
                        wait(s_raw[u % RAW], 16 * (u // RAW + 1))
                    else:
                        eng.wait_ge(first_in[u % 2], l * 16 + 32)
                    high(u + 2, u + 1)
                    even = S_SSD <= u < S_SST and (u - S_SSD) % 2 == 0
                    if even:
                        t, n = (u - S_SSD) // 2, rows((u - S_SSD) // 2)
                        if t > 0:
                            ssd_clamp(t, 1, 2)
                            wait(s_S, t)
                        wait(sT, t + 1)
                        go(act(btok[0:n, :, :], mb[0:n, 3, 0:256].rearrange("p (g n) -> p g n", g=2), ACT.Copy),
                           s_bt, t + 1)
                        if t > 0:
                            ssd_decay(t)
                    if u < U_OUT:
                        read_out(u)
                    if u == U_DT:
                        settle()
                        go(act(dt_e, dt_raw, ACT.Abs))
                        settle()
                        go(act(dt_e, dt_e, ACT.Exp, scale=-1.0), dt_s1, 1)
                        go(act(na[:, :], hvec[:, 1:2], ACT.Exp))
                    if u == 2:
                        wait(dt_s2, 1)
                        settle()
                        go(act(dt_l, dt_u, ACT.Ln), dt_s3, 1)
                    if u == 7:
                        wait(cum_ok, 1)
                        go(act(dt_w, dt_s, ACT.Exp), wl_ok, 1)
                    if U_CONV < u <= U_POOL:
                        i = u - U_CONV - 1
                        k = CONV_ORDER[i]
                        wait(halo_used, i + 1)
                        cb = vec[:, V_CB + k:V_CB + k + 1]
                        go(act(xbc[:, k, 0:SEQ], cvt[:, i % 2, 0:SEQ], ACT.Silu, bias=cb))
                        go(act(xbc[:, k, SEQ:].rearrange("p (b n) -> p b n", b=NB),
                               cvt[:, i % 2, 3 + SEQ:HALO].rearrange(
                                   "p (b n) -> p b n", b=NB)[:, :, 0:NT], ACT.Silu, bias=cb),
                           xbc_ok, i + 1)
                    if S_RET <= u < S_RST and (u - S_RET) % 2 == 0:
                        ret_slot((u - S_RET) // 2)
                    if S_RET <= u < S_RET + 4:
                        ssd_clamp(0, u - S_RET, 4)
                    if u == S_RET + 4:
                        ssd_decay(0)
                    if S_SSD <= u < S_SST - 1 and not even:
                        t = (u - S_SSD) // 2 + 1
                        ssd_row_exps(t)
                        ssd_clamp(t, 0, 2)
                    if u == S_RN:
                        wait(rs_y, 1)
                        wait(pool_out, 4)
                        for i in range(RP):
                            go(act(ret_sq[i], qk[:, i, :], ACT.Square), b_sq, i + 1)
                    if u == S_RN + 1:
                        two_rstd(0, HD)
                        two_rstd(2, HD)
                    if u == S_RL:
                        for i in range(RP):
                            wait(ret_full, i + 1)
                            go(act(mix[:, 1, 0, i, :], qk[:, i, :], ACT.Copy), mix_hi, i + 1)
                    if S_NORM <= u < S_NORM + GROUPS:
                        g = u - S_NORM
                        for j in range(4 * g, 4 * g + 4):
                            wait(g_z_used, j + 1)
                            if j < 2:
                                wait(b_sum, RP)
                            else:
                                wait(b_add, j - 1)
                            go(act(tmp[:, j % 2, :], xbc[:, j, :], ACT.Square), b_sq, RP + j + 1)
                    if u == S_NORM + GROUPS:
                        two_rstd(RP, PAIRS // GROUPS * P)
                    if S_NORM + GROUPS < u < S_NORM + GROUPS + 5:
                        for j in (2 * (u - S_NORM - GROUPS - 1), 2 * (u - S_NORM - GROUPS - 1) + 1):
                            split_y(j)
                    m = u - U_OUT - OUT_CHUNKS
                    if m >= 0:
                        wait(x_new, OUT_CHUNKS + m + 1)
                        if m >= 2:
                            wait(sq_add, m - 1)
                        square(m)
                norm_rstd()
                lane.close()
                next_layer(eng, next_act)

        @block.vector
        def _(eng):
            lane = Lane(eng, chain_v)
            go, settle, wait = lane.go, lane.settle, lane.wait
            V = nc.vector

            def split(u, n):
                wait(w_hid, n)
                go(V.tensor_tensor(w_lo[:, u % 2, :, :], w_raw[:, u % RAW, :, :], w_hi[:, u % 2, :, :].bitcast(F32),
                                   ALU.subtract), w_split, n)

            def add_square(j):
                wait(sqd, j + 1)
                settle()
                if j == 0:
                    go(V.tensor_copy(ssq[:, :], tmp[:, j % 2, :]), sq_add, j + 1)
                else:
                    go(V.tensor_tensor(ssq[:, :], ssq[:, :], tmp[:, j % 2, :], ALU.add), sq_add, j + 1)

            def v_(o, n=1):
                return vec[:, o:o + n]

            def dt_part(k):
                if k == 0:
                    wait(dt_s1, 1)
                    go(V.tensor_scalar(dt_u, dt_e, 1.0, None, ALU.add), dt_s2, 1)
                    settle()
                    go(V.tensor_scalar(dt_r, dt_u, 1.0, None, ALU.subtract))
                    settle()
                    go(V.tensor_scalar(dt_v, dt_r, 0.0, None, ALU.is_equal))
                    go(V.tensor_scalar(dt_s, dt_r, 1e-30, None, ALU.max))
                elif k == 1:
                    go(V.tensor_tensor(dt_v, dt_v, dt_e, ALU.mult))
                    go(V.reciprocal(dt_r, dt_s))
                elif k == 2:
                    go(V.tensor_tensor(dt_r, dt_r, dt_e, ALU.mult))
                    wait(dt_s3, 1)
                    settle()
                    go(V.tensor_tensor(dt_r, dt_r, dt_l, ALU.mult))
                elif k == 3:
                    go(V.tensor_tensor(dt_r, dt_r, dt_v, ALU.add))
                    settle()
                    go(V.scalar_tensor_tensor(out=dt_r, in0=dt_raw, scalar=0.0, in1=dt_r, op0=ALU.max, op1=ALU.add))
                elif k == 4:
                    go(V.tensor_scalar(dt_v, dt_r, na[:, 0:1], -1.0, ALU.mult, ALU.mult))
                    go(V.tensor_copy(stk[32:32 + HEADS, :], dt_r))
                    settle()
                    go(V.tensor_tensor_scan(cum, reset, dt_v, 0.0, ALU.mult, ALU.add))
                elif k == 5:
                    for q, (o, n, w) in enumerate(((0, TILES - 1, CH), (SEQ, NB, NT))):
                        cu = cum[:, o:o + n * w].rearrange("p (a b) -> p a b", a=n)
                        lastc = cu[:, :, w - 1:w].to_broadcast([HEADS, n, w])
                        i = V.tensor_tensor(dt_s[:, o:o + n * w].rearrange("p (a b) -> p a b", a=n), lastc, cu,
                                            ALU.subtract)
                        if q == 0:
                            go(i)
                        else:
                            go(i, cum_ok, 1)
                elif k == 7:
                    wait(wl_ok, 1)
                    go(V.tensor_tensor(stk[64:64 + HEADS, :], dt_w, dt_r, ALU.mult), stk_ok, 1)

            def conv(i):
                k = CONV_ORDER[i]
                wait(evac, U_CONV + i + 1)
                wait(halo_in, i + 1)
                if i >= 2:
                    wait(xbc_ok, i - 1)
                h, o = halo[:, i % 2, :], cvt[:, i % 2, 0:CVO]
                w = [v_(V_CW + 4 * k + c) for c in range(CW)]
                settle()
                go(V.tensor_scalar(o, h[:, 3:3 + CVO], w[3], None, ALU.mult))
                for c in (2, 1, 0):
                    settle()
                    ins = V.scalar_tensor_tensor(out=o, in0=h[:, c:c + CVO], scalar=w[c], in1=o, op0=ALU.mult,
                                                 op1=ALU.add)
                    if c:
                        go(ins)
                    else:
                        go(ins, halo_used, i + 1)

            def rotate(i):
                wait(evac, U_Q + i + 1)
                q = qk[:, i, :]
                settle()
                go(V.stream_shuffle(cvt[:, 0, 0:TOK], q, [(p + 16) % 32 for p in range(32)]))
                settle()
                go(V.tensor_tensor(cvt[:, 1, 0:TOK], cvt[:, 0, 0:TOK], T("sin"), ALU.mult))
                go(V.tensor_tensor(q, q, T("cos"), ALU.mult))
                settle()
                go(V.tensor_tensor(q, q, cvt[:, 1, 0:TOK], ALU.add), rot, i + 1)

            def heads(ap, n=HEADS):
                return ap.rearrange("p (h d) -> p h d", h=n)

            def before(u):
                if U_GPOOL < u < U_GPOOL + 5:
                    pool_gate(u - U_GPOOL - 1)
                if S_RST <= u < S_SSD:
                    ret_state(u - S_RST)
                if S_SST <= u < S_GATE:
                    ssd_decayed(u - S_SST, 0)
                if S_SST < u <= S_GATE:
                    ssd_add(u - S_SST - 1, 1)

            def ssd_1(t):
                n = rows(t)
                wait(sT, t + 1)
                src = mb[0:n, 0:2, :].rearrange("p a (h d) -> p (a h) d", d=HD)
                dt_b = tokv[0:n, t, 32:48].unsqueeze(2).to_broadcast([n, HEADS, HD])
                dw_b = tokv[0:n, t, 64:80].unsqueeze(2).to_broadcast([n, HEADS, HD])
                settle()
                go(V.tensor_tensor(heads(xdt[0:n, :]), src, dt_b, ALU.mult))
                go(V.tensor_tensor(heads(xdw[0:n, :]), src, dw_b, ALU.mult))
                mask = (T("causal") if t < TILES - 1 else T("smask")[0:SMP, :])
                go(V.tensor_tensor(gm[0:n, :, 0:n], mb[0:n, 2, 0:256].rearrange("p (g n) -> p g n", g=2)[:, :, 0:n],
                                   mask.unsqueeze(1).to_broadcast([n, GROUPS, n]), ALU.mult), s_xdt, t + 1)

            def ssd_weights(t):
                n = rows(t)
                wait(s_exp, t + 1)
                settle()
                for g in range(GROUPS):
                    m = decay[0:n, t % 2, 8 * g:8 * g + 8, 0:n]
                    ins = V.tensor_tensor(m, m, gm[0:n, g, 0:n].unsqueeze(1).to_broadcast([n, 8, n]), ALU.mult)
                    if g == 0:
                        go(ins)
                    else:
                        go(ins, s_M, t + 1)

            def c_decay(t):
                wait(s_row, t)
                settle()
                for g in range(GROUPS):
                    ins = V.tensor_tensor(cdec_t[:, 8 * g:8 * g + 8, :], cdec_t[:, 8 * g:8 * g + 8, :],
                                          xbc[:, 10 + g, cols(t)].unsqueeze(1).to_broadcast([P, 8, CH]), ALU.mult)
                    if g == 0:
                        go(ins)
                    else:
                        go(ins, s_ec, t)

            def ssd_2(t):
                n = rows(t)
                if t < TILES - 1:
                    wait(s_S, t + 1)
                    st = mb[:, 0:2, :].rearrange("p a n -> p (a n)")
                    if t == 0:
                        wait(rp_out, 32)
                        settle()
                        go(V.tensor_copy(hT[:, :], st), s_h, 1)
                    else:
                        wait(s_Y, t + 1)
                        settle()
                        go(V.tensor_tensor(heads(hT[:, :]), heads(hT[:, :]),
                                           el[:, :].unsqueeze(2).to_broadcast([P, HEADS, HD]), ALU.mult))
                        settle()
                        go(V.tensor_tensor(hT[:, :], hT[:, :], st, ALU.add), s_h, t + 1)
                    settle()
                wait(s_Y, t + 1)
                for j in range(PAIRS):
                    if t < TILES - 1:
                        src = mb[:, 2 + j // 4, (j % 4) * P:(j % 4) * P + n]
                    else:
                        src = mb[:, 2, j * SMP:(j + 1) * SMP]
                    y = xbc[:, j, cols(t)]
                    ins = V.scalar_tensor_tensor(out=y, in0=y, scalar=v_(V_DS + j), in1=src, op0=ALU.mult,
                                                 op1=ALU.add)
                    if j < PAIRS - 1:
                        go(ins)
                    else:
                        go(ins, s_y, t + 1)

            def ssd_b_two(q):
                if q >= 2:
                    wait(hs_S, 4 * (q - 1))
                if q == 0:
                    wait(s_bt, TILES)
                settle()
                for e in range(2):
                    b = q + e * TWOS
                    go(V.tensor_scalar(bseq[2 * (q % 2) + e], btok[0:SMP, :, :].rearrange("p g n -> p (g n)"),
                                       T("bmask")[0:SMP, b:b + 1], None, ALU.mult), b_seq, 2 * q + e + 1)

            def ssd_decayed(q, e):
                wait(hs_I, 2 * q + e + 1)
                if q == 0 and e == 0:
                    wait(s_exp, TILES)
                settle()
                h, b = h0[2 * q + e], q + e * TWOS
                go(V.tensor_tensor(heads(h[:, :]), heads(h[:, :]), els[:, :, b:b + 1].to_broadcast([P, HEADS, HD]),
                                   ALU.mult))

            def ssd_add(q, g):
                settle()
                for e in range(2):
                    i, h = 4 * q + 2 * g + e, h0[2 * q + e]
                    wait(hs_S, i + 1)
                    c = slice(g * 512, (g + 1) * 512)
                    go(V.tensor_tensor(h[:, c], h[:, c], mb[:, i % 3, :], ALU.add), hs_n, i + 1)

            def ret_1(t):
                n = rows(t)
                wait(rT, t + 1)
                if t == 0:
                    wait(r_zero, 1)
                dm = T("dmask") if t < TILES - 1 else T("sdmask")[0:SMP, :]
                ed = T("edec") if t < TILES - 1 else T("sedec")[0:SMP, :]
                settle()
                go(V.tensor_tensor(pmat[0:n, :, :, 0:n], mb[0:n, 0:2, :].rearrange("p e (j n) -> p e j n", n=P)[:, :, :, 0:n],
                                   dm.rearrange("p (e j n) -> p e j n", e=2, j=RP), ALU.mult))
                go(V.tensor_tensor(heads(kw[0:n, :], RH), heads(mb[0:n, 2, :], RH),
                                   ed.unsqueeze(2).to_broadcast([n, RH, HD]), ALU.mult))
                settle()
                if t < TILES - 1:
                    go(V.tensor_tensor(qd[:, :, :], qk[:, 0:RP, cols(t)], T("inner").rearrange("p (j n) -> p j n", j=RP),
                                       ALU.mult), r_P, t + 1)
                else:
                    for j in range(RP):
                        ins = V.tensor_tensor(qd[:, j, 0:SMP].rearrange("p (b k) -> p b k", b=NB),
                                              qk[:, j, SEQ:].rearrange("p (b k) -> p b k", b=NB),
                                              T("sinner")[:, j * NT:(j + 1) * NT].unsqueeze(1).to_broadcast([P, NB, NT]),
                                              ALU.mult)
                        if j < RP - 1:
                            go(ins)
                        else:
                            go(ins, r_P, t + 1)

            def diag(ap, e):
                r = slice(e * HD, (e + 1) * HD)
                return ap[r, :, e * HD:(e + 1) * HD]

            def ret_2(t):
                n = rows(t)
                wait(r_Y, t + 1)
                settle()
                go(V.tensor_copy(qk[:, 0:RP, cols(t)], mb[:, 0, :].rearrange("p (j n) -> p j n", n=P)[:, :, 0:n]),
                   r_y, t + 1)
                if t < TILES - 1:
                    wait(r_S, t + 1)
                    sm = mb[:, 1, :].rearrange("p (j n) -> p j n", j=RP)
                    settle()
                    if t == 0:
                        go(V.tensor_copy(diag(rS, 0), diag(sm, 0)))
                        go(V.tensor_copy(diag(rS, 1), diag(sm, 1)), r_s, 1)
                    else:
                        for e in range(2):
                            r = slice(e * HD, (e + 1) * HD)
                            go(V.tensor_tensor(diag(rS, e), diag(rS, e),
                                               T("cdec")[r, :].unsqueeze(2).to_broadcast([HD, RP, HD]), ALU.mult))
                        settle()
                        go(V.tensor_tensor(diag(rS, 0), diag(rS, 0), diag(sm, 0), ALU.add))
                        go(V.tensor_tensor(diag(rS, 1), diag(rS, 1), diag(sm, 1), ALU.add), r_s, t + 1)

            def ret_k_two(q):
                if q >= 2:
                    wait(rs_S, q - 1)
                settle()
                for e in range(2):
                    b = q + e * TWOS
                    go(V.tensor_scalar(kwm[2 * (q % 2) + e], kw[0:SMP, :], T("bmask")[0:SMP, b:b + 1], None, ALU.mult),
                       r_kwm, 2 * q + e + 1)

            def ret_state(q):
                wait(rs_S, q + 1)
                settle()
                two = [(rs0[q + e * TWOS], mb[:, 1 + e, :].rearrange("p (j n) -> p j n", j=RP)) for e in range(2)]
                for state, _ in two:
                    for e in range(2):
                        r = slice(e * HD, (e + 1) * HD)
                        go(V.tensor_tensor(diag(state, e), diag(state, e),
                                           T("scdec")[r, :].unsqueeze(2).to_broadcast([HD, RP, HD]), ALU.mult))
                settle()
                for n, (state, new) in enumerate(two):
                    go(V.tensor_tensor(diag(state, 0), diag(state, 0), diag(new, 0), ALU.add))
                    go(V.tensor_tensor(diag(state, 1), diag(state, 1), diag(new, 1), ALU.add), rs_n, 2 * q + n + 1)

            def pool(i):
                wait(evac, U_POOL + i + 1)
                wait(halo_in, CONV_CHUNKS + i + 1)
                cur, w = halo[:, i % 2, :], 1
                bufs = (cvt[:, 0, :], cvt[:, 1, :])
                while w < WINDOWS[i]:
                    dst = bufs[0]
                    settle()
                    go(V.tensor_tensor(dst[:, 2 * w - 1:PHALO], cur[:, 2 * w - 1:PHALO], cur[:, w - 1:PHALO - w],
                                       ALU.add))
                    cur, w, bufs = dst, 2 * w, bufs[::-1]
                settle()
                go(V.tensor_tensor(cur[:, PB:PB + 16], cur[:, PB:PB + 16], T("cnt")[:, i * 16:(i + 1) * 16], ALU.mult))
                settle()
                raw = halo[:, i % 2, :]
                go(V.scalar_tensor_tensor(out=vT[:, i, 0:SEQ], in0=cur[:, PB:PB + SEQ], scalar=1.0 / WINDOWS[i],
                                          in1=raw[:, PB:PB + SEQ], op0=ALU.mult, op1=ALU.subtract))

                def seqs(ap):
                    return ap[:, PB + SEQ:PHALO].rearrange("p (b k) -> p b k", b=NB)[:, :, PB:]

                settle()
                go(V.scalar_tensor_tensor(out=vT[:, i, SEQ:].rearrange("p (b k) -> p b k", b=NB), in0=seqs(cur),
                                          scalar=1.0 / WINDOWS[i], in1=seqs(raw), op0=ALU.mult, op1=ALU.subtract),
                   pooled_ok, i + 1)
                settle()
                go(V.tensor_copy(pad[:, 0:1], pad[:, 1:2]), halo_used, CONV_CHUNKS + i + 1)

            def pool_gate(i):
                wait(pool_mm, i + 1)
                settle()
                go(V.scalar_tensor_tensor(out=halves(vT[:, i, :]), in0=acc_of(U_GPOOL + i), scalar=v_(V_PS + i),
                                          in1=halves(tmp[:, i % 2, :]), op0=ALU.mult, op1=ALU.mult),
                   pool_out, i + 1)

            def ret_out(i):
                q = qk[:, i, :]
                wait(b_rstd, i + 1)
                settle()
                go(V.scalar_tensor_tensor(out=q, in0=q, scalar=v_(V_RN + i), in1=rstds[i % 2], op0=ALU.mult,
                                          op1=ALU.mult), b_used, i + 1)
                settle()
                go(V.tensor_tensor(q, q, qk[:, RP + i, :], ALU.mult), ret_full, i + 1)

            def mix_low(which, i):
                go(V.tensor_tensor(mix[:, which, 1, i, :], (vT, qk)[which][:, i, :],
                                   mix[:, which, 0, i, :].bitcast(F32), ALU.subtract), mix_lo, 4 * which + i + 1)

            def z_use(i):
                wait(evac, U_Z + i + 1)
                settle()
                go(V.tensor_tensor(xbc[:, i, :], xbc[:, i, :], z_gate[i % 4], ALU.mult), g_z_used, i + 1)

            go(V.memset(pad[:, :], 0.0))
            go(V.memset(stk[:, :], 0.0))
            go(V.memset(ones, 1.0))
            V.memset(eps[:, :], EPS).then_inc(eps_ok, 1)
            settle()
            for j in range(KT):
                add_square(j)
            for u in (1, 0):
                eng.wait_ge(first_in[u], 16)
                go(V.tensor_copy(w_hi[:, u % 2, :, :], w_raw[:, u % RAW, :, :]), w_hid, 2 - u)
                split(u, 2 - u)
            wait(n_rstd, 1)
            lane.close()
            next_layer(eng, next_dve)
            with eng.Fori(0, DEPTH) as l:
                eng.wait_ge(vec_in, l * 16 + 16)
                for j in range(KT + 1):
                    if j < KT:
                        go(V.scalar_tensor_tensor(out=xbc[:, j, :], in0=x[:, j, :], scalar=v_(V_NW + j),
                                                  in1=rstd[:, :], op0=ALU.mult, op1=ALU.mult), h_full, j + 1)
                    if j > 0:
                        wait(h_hi, j)
                        go(V.tensor_tensor(hin[:, 1, j - 1, :], xbc[:, j - 1, :],
                                           hin[:, 0, j - 1, :].bitcast(F32), ALU.subtract), h_lo, j)
                for u in range(UNITS):
                    before(u)
                    even = S_SSD <= u < S_SST and (u - S_SSD) % 2 == 0
                    if even:
                        ssd_1((u - S_SSD) // 2)
                    if u < UNITS - 1:
                        split(u + 2, u + 1)
                    o = u - U_OUT
                    if o >= 0:
                        m = o % OUT_CHUNKS
                        wait(proj, u + 1)
                        if o < OUT_CHUNKS and o % 2 == 0:
                            wait(x_back[o // 2], 16)
                        settle()
                        go(V.tensor_tensor(halves(x[:, m, :]), halves(x[:, m, :]), acc_of(u), ALU.add),
                           x_new, o + 1)
                        if o >= OUT_CHUNKS and m < KT - 1:
                            add_square(m)
                    if u == U_Q:
                        wait(tab_in, 16)
                    if U_Q <= u < U_V:
                        rotate(u - U_Q)
                    if 1 <= u <= 8:
                        settle()
                        dt_part(u - 1)
                    if u == S_STK:
                        wait(stk_T, 1)
                        settle()
                        go(V.tensor_copy(tokv[:, 0:4, :], mb[:, 0, 0:384].rearrange("p (t n) -> p t n", t=4)))
                        go(V.tensor_copy(tokv[0:SMP, 4, :], mb[0:SMP, 1, 0:96]), tokv_ok, 1)
                    if S_RET <= u < S_RST:
                        t = (u - S_RET) // 2
                        (ret_1 if (u - S_RET) % 2 == 0 else ret_2)(t)
                    if u == S_RST - 1:
                        ret_k_two(0)
                        ret_k_two(1)
                    if S_RST <= u < S_SSD:
                        if u - S_RST + 2 < TWOS:
                            ret_k_two(u - S_RST + 2)
                    if u == S_SSD - 1:
                        settle()
                        go(V.tensor_tensor(qk[:, 0:RP, SEQ:], qk[:, 0:RP, SEQ:],
                                           mb[:, 3, 0:RP * SMP].rearrange("p (j n) -> p j n", j=RP), ALU.add),
                           rs_y, 1)
                    if S_SSD <= u < S_SST:
                        t = (u - S_SSD) // 2
                        (ssd_weights if even else ssd_2)(t)
                        if (u - S_SSD) % 2 == 1 and t + 1 < TILES - 1:
                            c_decay(t + 1)
                    if U_CONV <= u < U_POOL:
                        conv(u - U_CONV)
                    if u in POOL_SLOTS:
                        pool(POOL_SLOTS.index(u))
                    if u == S_SST - 1:
                        ssd_b_two(0)
                        ssd_b_two(1)
                    if S_SST <= u < S_GATE:
                        ssd_decayed(u - S_SST, 1)
                        ssd_add(u - S_SST, 0)
                        if 2 <= u - S_SST + 1 < TWOS:
                            ssd_b_two(u - S_SST + 1)
                    if u == S_GATE - 1:
                        wait(ecs_ok, 1)
                        settle()
                        go(V.tensor_tensor(ecs[:, :, :], ecs[:, :, :], mb[:, 3, :].rearrange("p (j n) -> p j n", j=PAIRS),
                                           ALU.mult))
                        settle()
                        go(V.tensor_tensor(xbc[:, 0:8, SEQ:], xbc[:, 0:8, SEQ:], ecs[:, :, :], ALU.add), hs_y, 1)
                    if u == S_RL:
                        for i in range(RP):
                            wait(mix_hi, i + 1)
                            mix_low(1, i)
                    for i in {S_GATE: (0, 1), S_GATE + 1: (2, 3), S_RL + 1: (4, 5, 6, 7)}.get(u, ()):
                        z_use(i)
                    if u in (S_RN + 1, S_RN + 2):
                        for i in (2 * (u - S_RN - 1), 2 * (u - S_RN - 1) + 1):
                            ret_out(i)
                    if u == S_PL:
                        wait(ssd_free, 1)
                        settle()
                        for i in range(4):
                            go(V.tensor_copy(mix[:, 0, 0, i, :], vT[:, i, :]))
                        settle()
                        for i in range(4):
                            mix_low(0, i)
                    if S_NORM <= u < S_NORM + GROUPS:
                        g = u - S_NORM
                        for j in range(4 * g, 4 * g + 4):
                            wait(b_sq, RP + j + 1)
                            settle()
                            if j % 4 == 0:
                                go(V.tensor_copy(z_gate[g], tmp[:, j % 2, :]), b_add, j + 1)
                            else:
                                go(V.tensor_tensor(z_gate[g], z_gate[g], tmp[:, j % 2, :], ALU.add), b_add, j + 1)
                    if S_NORM + GROUPS <= u < S_NORM + GROUPS + 4:
                        for j in (2 * (u - S_NORM - GROUPS), 2 * (u - S_NORM - GROUPS) + 1):
                            y = xbc[:, j, :]
                            wait(b_rstd, RP + j // 4 + 1)
                            go(V.scalar_tensor_tensor(out=y, in0=y, scalar=v_(V_SN + j), in1=rstds[j // 4],
                                                      op0=ALU.mult, op1=ALU.mult), y_full, j + 1)
                    if S_NORM + GROUPS < u < S_NORM + GROUPS + 5:
                        for j in (2 * (u - S_NORM - GROUPS - 1), 2 * (u - S_NORM - GROUPS - 1) + 1):
                            wait(y_hi, j + 1)
                            go(V.tensor_tensor(hin[:, 1, j, :], xbc[:, j, :], hin[:, 0, j, :].bitcast(F32),
                                               ALU.subtract), y_lo, j + 1)
                    if u == UNITS - 1:
                        split(u + 2, u + 1)
                wait(n_rstd, 1)
                lane.close()
                next_layer(eng, next_dve)
            for j in range(KT):
                V.scalar_tensor_tensor(out=x[:, j, :], in0=x[:, j, :], scalar=T("fnw")[:, j:j + 1], in1=rstd[:, :],
                                       op0=ALU.mult, op1=ALU.mult).then_inc(f_ok, 1)

        @block.gpsimd
        def _(eng):
            lane = Lane(eng, chain_p)
            go, settle, wait = lane.go, lane.settle, lane.wait
            G = nc.gpsimd

            def fill(i):
                conv_ = i < CONV_CHUNKS
                w, end = (3, HALO) if conv_ else (PB, PHALO)
                st = cst[:, CONV_ORDER[i], :, :] if conv_ else pst[:, i - CONV_CHUNKS, :, :]
                hb = halo[:, i % 2, 0:end]
                settle()
                go(G.memset(hb[:, 0:w], 0.0))
                settle()
                go(G.tensor_copy(hb[:, w + SEQ:].rearrange("p (b n) -> p b n", b=NB)[:, :, 0:w], st),
                   halo_in, i + 1)

            def save(i):
                conv_ = i < CONV_CHUNKS
                u = U_CONV + i if conv_ else U_POOL + i - CONV_CHUNKS
                w, end = (3, HALO) if conv_ else (PB, PHALO)
                to = cso[:, CONV_ORDER[i], :, :] if conv_ else pso[:, i - CONV_CHUNKS, :, :]
                hb = halo[:, i % 2, 0:end]
                wait(evac, u + 1)
                settle()
                go(G.tensor_copy(to[:, 0, :], hb[:, SEQ:w + SEQ]))
                go(G.tensor_copy(to[:, 1:, :], hb[:, w + SEQ:].rearrange("p (b n) -> p b n", b=NB)[:, :, NT:]),
                   halo_saved, i + 1)
                wait(halo_used, i + 1)

            clear_signals(eng)
            with eng.Fori(0, DEPTH) as l:
                for i in range(NB):
                    go(G.memset(rs0[i][:, :, :], 0.0))
                go(G.memset(rS[:, :, :], 0.0), r_zero, 1)
                wait(s_st, 32)
                fill(0)
                fill(1)
                for i in range(16):
                    save(i)
                    if i + 2 < 16:
                        fill(i + 2)
                settle()
                eng.dma_start(a["conv_o"][l], cso[:, :, :, :]).then_inc(states_out, 16)
                eng.dma_start(a["pool_o"][l], pso[:, :, :, :]).then_inc(states_out, 16)
                wait(states_out, 32)
                wait(halo_used, 16)
                lane.close()
                clear_signals(eng)


def rot_order():
    return np.array([16 * (r // 32) + r % 32 if r % 32 < 16 else 32 + 16 * (r // 32) + r % 32 - 16
                     for r in range(HD)])


def tables():
    f = np.float32
    t = np.zeros((P, TAB_N), f)

    def put(name, v):
        o, w = TAB[name]
        v = np.asarray(v, f).reshape(v.shape[0], w)
        t[:v.shape[0], o:o + w] = v

    i = np.arange(P)
    put("ident", np.eye(P))
    put("blk", (i[:, None] // HD == i[None, :] // HD) * 1.0)
    put("causal", (i[None, :] >= i[:, None]) * 1.0)
    s = np.arange(SMP)
    same = s[:, None] // NT == s[None, :] // NT
    ok = same & (s[None, :] >= s[:, None])
    put("smask", ok * 1.0)
    put("bmask", (s[:, None] // NT == np.arange(NB)[None, :]) * 1.0)
    pos = np.concatenate([np.arange(SEQ), PAST + s % NT]).astype(f)
    half = HD // 2
    inv = (10000.0 ** (-np.arange(half) / half)).astype(f)
    o = np.tile(rot_order(), 2)
    ang = (pos[None, :] * inv[o % half][:, None]).astype(f)
    put("cos", np.cos(ang.astype(np.float64)))
    put("sin", np.sin(ang.astype(np.float64)) * np.where(o < half, -1.0, 1.0)[:, None])
    lg = np.log1p(-np.exp2(-5.0 - np.arange(RH, dtype=f))).astype(f)
    pair = np.arange(RH).reshape(RP, 2).T.reshape(-1)

    def decay(n, mask, rel):
        d = np.exp((np.maximum(rel, 0).astype(f)[:, None, :] * lg[pair][None, :, None]).astype(f))
        return np.where(mask[:, None, :], d, 0.0)

    put("dmask", decay(P, i[None, :] >= i[:, None], i[None, :] - i[:, None]))
    put("sdmask", decay(SMP, ok, s[None, :] - s[:, None]))
    head = 2 * np.arange(RP)[None, :] + i[:, None] // HD
    put("inner", np.exp(((i + 1).astype(f)[None, None, :] * lg[head][:, :, None]).astype(f)))
    put("sinner", np.exp(((np.arange(NT) + 1).astype(f)[None, None, :] * lg[head][:, :, None]).astype(f)))
    put("edec", np.exp(((CH - 1 - i).astype(f)[:, None] * lg[None, :]).astype(f)))
    put("sedec", np.exp(((NT - 1 - s % NT).astype(f)[:, None] * lg[None, :]).astype(f)))
    put("cdec", np.exp((f(CH) * lg[head]).astype(f)))
    put("scdec", np.exp((f(NT) * lg[head]).astype(f)))
    k = np.arange(16)
    put("cnt", np.tile(np.concatenate([w / np.minimum(k + 1.0, w) for w in WINDOWS])[None, :], (P, 1)))
    return t


def resets():
    col = np.arange(TOK)
    start = np.where(col < SEQ, col % CH == 0, (col - SEQ) % NT == 0)
    return np.tile(np.where(start, 0.0, 1.0)[None, :], (HEADS, 1)).astype(np.float32)


_OUTS = {
    "y": (P, KT, TOK), "ssm_p": (DEPTH, P, HEADS * HD), "ssm_s": (DEPTH, NB, P, HEADS * HD),
    "conv_o": (DEPTH, P, CONV_CHUNKS, 1 + NB, 3), "pool_o": (DEPTH, P, 4, 1 + NB, PB),
    "ret_p": (DEPTH, P, RP, HD), "ret_s": (DEPTH, NB, P, RP, HD),
}


def lay_out(v):
    v = {k: np.asarray(q) for k, q in v.items()}
    rot = (np.arange(RH)[:, None] * HD + rot_order()[None, :]).reshape(-1)
    w_in, w_out = v["w_in"], v["w_out"]
    z, c, dt, q, k, vv, gr, u, gp, end = np.cumsum([0, 1024, 1536, HEADS, 512, 512, 512, 512, 512, 512])
    cc = w_in[:, :, c:dt].reshape(DEPTH, D_MODEL, CONV_CHUNKS, P)[:, :, list(CONV_ORDER)]
    w = np.concatenate([w_in[:, :, dt:q], np.zeros((DEPTH, D_MODEL, P - HEADS), w_in.dtype),
                        w_in[:, :, q:k][:, :, rot], w_in[:, :, k:vv][:, :, rot], w_in[:, :, vv:gr],
                        cc.reshape(DEPTH, D_MODEL, -1), w_in[:, :, u:gp], w_in[:, :, gr:u], w_in[:, :, gp:end],
                        w_in[:, :, z:c]], axis=2)
    w = w.reshape(DEPTH, KT, P, U_OUT, P).transpose(0, 3, 2, 1, 4)
    wo = w_out.reshape(DEPTH, 2, KT, P, OUT_CHUNKS, P)
    wo = np.stack([wo[:, 0], np.roll(wo[:, 1], RP, axis=1)], axis=1)
    wo = [wo[:, 1 - o // OUT_CHUNKS, :, :, o % OUT_CHUNKS].transpose(0, 2, 1, 3) for o in range(2 * OUT_CHUNKS)]
    w = np.concatenate([w, np.stack(wo, axis=1)], axis=1).reshape(DEPTH * UNITS, P, KT, P)
    w = np.concatenate([w, np.zeros((2, P, KT, P), w.dtype)])

    def on_parts(a):
        return a.reshape(DEPTH, -1, P).transpose(0, 2, 1)

    cw = v["conv_w"].reshape(DEPTH, CW, CONV_CHUNKS, P).transpose(0, 3, 2, 1).reshape(DEPTH, P, -1)
    vec = np.concatenate([on_parts(v["norm_w"]), cw, on_parts(v["conv_b"]),
                          on_parts(np.repeat(v["d_skip"], HD, axis=1)), on_parts(v["ssd_norm_w"]),
                          on_parts(v["ret_norm_w"]), on_parts(v["pool_scale"])], axis=2)
    vec = np.concatenate([vec, np.zeros((1, P, V_N), vec.dtype)])
    x = np.concatenate([v["x_prompt"].reshape(SEQ, D_MODEL), v["x_sample"].reshape(SMP, D_MODEL)])
    tab = tables()
    o, n = TAB["fnw"]
    tab[:, o:o + n] = v["final_norm_w"].reshape(KT, P).T
    ret = v["state_ret"][:, :, :, rot_order(), :].reshape(DEPTH, NB, RP, 2, HD, HD)
    return {
        "x": x.T.reshape(KT, P, TOK).transpose(1, 0, 2), "tab": tab, "reset": resets(), "w": w, "vec": vec,
        "hvec": np.stack([v["dt_bias"], v["a_log"]], axis=2), "pw": v["pool_w"].transpose(0, 2, 1, 3),
        "cst": v["state_conv"].reshape(DEPTH, NB, 3, CONV_CHUNKS, P).transpose(0, 4, 3, 1, 2),
        "pst": v["state_pool"].reshape(DEPTH, NB, PB, 4, P).transpose(0, 4, 3, 1, 2),
        "ssm0": v["state_ssm"].reshape(DEPTH, NB, HEADS * HD, P).transpose(0, 1, 3, 2),
        "ret0": ret.transpose(0, 1, 3, 4, 2, 5).reshape(DEPTH, NB, P, RP, HD),
    }


def taken(r):
    y = r["y"].transpose(1, 0, 2).reshape(D_MODEL, TOK).T
    back = np.argsort(rot_order())

    def ssm(a, n):
        return a.reshape(DEPTH, n, P, HEADS * HD).transpose(0, 1, 3, 2).reshape(DEPTH, n, HEADS, HD, P)

    def ret(a, n):
        a = a.reshape(DEPTH, n, 2, HD, RP, HD).transpose(0, 1, 4, 2, 3, 5).reshape(DEPTH, n, RH, HD, HD)
        return a[:, :, :, back, :]

    def small(a, w):
        return a.transpose(0, 3, 4, 2, 1).reshape(DEPTH, 1 + NB, w, -1)

    conv, pool = small(r["conv_o"], 3), small(r["pool_o"], PB)
    c = np.ascontiguousarray
    return (c(y[:SEQ]).reshape(1, SEQ, D_MODEL), c(y[SEQ:]).reshape(NB, NT, D_MODEL),
            c(ssm(r["ssm_p"], 1)), c(conv[:, :1]), c(ret(r["ret_p"], 1)), c(pool[:, :1]),
            c(ssm(r["ssm_s"], NB)), c(conv[:, 1:]), c(ret(r["ret_s"], NB)), c(pool[:, 1:]))


def program(bacc, arrays):
    nc = bacc.Bacc("TRN2", target_bir_lowering=False, num_devices=1)
    a = {k: nc.dram_tensor(f"in_{k}", q.shape, F32, kind="ExternalInput").ap() for k, q in arrays.items()}
    for k, shape in _OUTS.items():
        a[k] = nc.dram_tensor(f"out_{k}", shape, F32, kind="ExternalOutput").ap()
    a["cum"] = nc.dram_tensor("cum_rows", (HEADS * TOK,), F32, kind="Internal").ap()
    a["x_kept"] = nc.dram_tensor("x_kept", (P, KT, TOK), F32, kind="Internal").ap()
    trunk(nc, a)
    return nc


def kernel(**inputs):
    import concourse.bacc as _bacc
    from concourse.bass_utils import run_bass_kernel_spmd as _run

    arrays = {k: np.ascontiguousarray(q) for k, q in lay_out(inputs).items()}
    nc = program(_bacc, arrays)
    r = _run(nc, [{f"in_{k}": q for k, q in arrays.items()}], core_ids=[0])
    return taken({k: r.results[0][f"out_{k}"] for k in _OUTS})
```
